# Optimizing a Trainium2 kernel written in Bass

```python
import math
import jax
import jax.numpy as jnp
from jax import lax
import numpy as np

D_MODEL = 1024
BATCH = 1
SEQ = 256
DEPTH = 2
DEC_BATCH = 8
DEC_SEQ = 4
PAST_LEN = 2048
PAGE_SIZE = 128

RET_HEADS = 8
RET_DK = 64
RET_DV = 128
GLA_HEADS = 4
GLA_DK = 128
GLA_DV = 256
GLA_GATE_RANK = 16
GLA_GATE_NORM = 16.0
RWKV_HEADS = 16
RWKV_HD = 64
RWKV_W = RWKV_HEADS * RWKV_HD
RWKV_DECAY_RANK = 64
RWKV_A_RANK = 64
RWKV_GATE_RANK = 128
RWKV_GN_EPS = 64e-5
D_FF = 2816
N_EXPERTS = 8
TOP_K = 2
N_BRANCH = 3
CHUNK = 64
ROPE_BASE = 10000.0
EPS = 1e-6
RET_PROJ = 2 * RET_HEADS * RET_DK + 2 * RET_HEADS * RET_DV
GLA_PROJ = 2 * GLA_HEADS * GLA_DK + 2 * GLA_HEADS * GLA_DV + GLA_GATE_RANK
RWKV_PROJ = 3 * RWKV_W + RWKV_DECAY_RANK + RWKV_A_RANK + RWKV_GATE_RANK
MERGE_COLS = N_BRANCH * D_MODEL
IN_COLS = RET_PROJ + GLA_PROJ + RWKV_PROJ + MERGE_COLS

kernel_name = 'hybrid_retention_rwkv7_gla_decoder_step'

def split_cols(x, widths):
    idx = [int(v) for v in np.cumsum(widths)[:-1]]
    return jnp.split(x, idx, axis=-1)

def rmsnorm(x, g):
    xf = x.astype(jnp.float32)
    y = xf * lax.rsqrt(jnp.mean(xf * xf, axis=-1, keepdims=True) + EPS)
    return (y * g.astype(jnp.float32)).astype(x.dtype)

def head_rmsnorm(o):
    return o * lax.rsqrt(jnp.mean(o * o, axis=-1, keepdims=True) + EPS)

def head_groupnorm(y, w, b):
    mu = jnp.mean(y, axis=-1, keepdims=True)
    yc = y - mu
    var = jnp.mean(yc * yc, axis=-1, keepdims=True)
    yn = yc * lax.rsqrt(var + RWKV_GN_EPS)
    return yn * w.reshape(RWKV_HEADS, RWKV_HD) + b.reshape(RWKV_HEADS, RWKV_HD)

def rope(x, pos):
    half = x.shape[-1] // 2
    inv = ROPE_BASE ** (-jnp.arange(half, dtype=jnp.float32) / half)
    ang = pos.astype(jnp.float32)[:, None] * inv[None, :]
    cos = jnp.cos(ang)[None, :, None, :]
    sin = jnp.sin(ang)[None, :, None, :]
    x1, x2 = x[..., :half], x[..., half:]
    return jnp.concatenate([x1 * cos - x2 * sin, x1 * sin + x2 * cos], axis=-1)

def to_chunks(x, L):
    B, T, H, d = x.shape
    return x.reshape(B, T // L, L, H, d).transpose(1, 0, 3, 2, 4)

def from_chunks(x):
    N, B, H, L, d = x.shape
    return x.transpose(1, 0, 3, 2, 4).reshape(B, N * L, H, d)

def retention_scan(q, k, v, S0, log_gamma):
    T = q.shape[1]
    L = math.gcd(T, CHUNK)
    i = jnp.arange(L, dtype=jnp.float32)
    diff = i[:, None] - i[None, :]
    dmat = jnp.where(diff >= 0, jnp.exp(log_gamma[:, None, None] * jnp.maximum(diff, 0.0)), 0.0)
    q_dec = jnp.exp(log_gamma[:, None] * (i + 1.0))[:, :, None]
    k_dec = jnp.exp(log_gamma[:, None] * (L - 1.0 - i))[:, :, None]
    c_dec = jnp.exp(log_gamma * L)[:, None, None]

    def step(S, xs):
        qb, kb, vb = xs
        sc = jnp.einsum('bhid,bhjd->bhij', qb, kb) * dmat
        o = jnp.einsum('bhij,bhjv->bhiv', sc, vb) + jnp.einsum('bhid,bhdv->bhiv', qb * q_dec, S)
        S = S * c_dec + jnp.einsum('bhjd,bhjv->bhdv', kb * k_dec, vb)
        return S, o

    S, o = lax.scan(step, S0, (to_chunks(q, L), to_chunks(k, L), to_chunks(v, L)))
    return from_chunks(o), S

def gla_scan(q, k, v, log_a, S0):
    T = q.shape[1]
    L = math.gcd(T, CHUNK)
    causal = jnp.tril(jnp.ones((L, L), dtype=bool))

    def step(S, xs):
        qb, kb, vb, gb = xs
        b = jnp.cumsum(gb, axis=2)
        rel = jnp.where(causal[:, :, None], b[:, :, :, None, :] - b[:, :, None, :, :], -jnp.inf)
        att = jnp.einsum('bhid,bhjd,bhijd->bhij', qb, kb, jnp.exp(rel))
        o = jnp.einsum('bhij,bhjv->bhiv', att, vb) + jnp.einsum('bhid,bhdv->bhiv', qb * jnp.exp(b), S)
        bl = b[:, :, -1:, :]
        S = S * jnp.exp(bl)[:, :, 0, :, None] + jnp.einsum('bhjd,bhjv->bhdv', kb * jnp.exp(bl - b), vb)
        return S, o

    xs = (to_chunks(q, L), to_chunks(k, L), to_chunks(v, L), to_chunks(log_a, L))
    S, o = lax.scan(step, S0, xs)
    return from_chunks(o), S

def rwkv7_scan(r, w, k, v, kk, a, S0):
    def step(S, xs):
        r_t, w_t, k_t, v_t, kk_t, a_t = xs
        sa = jnp.einsum('bhvk,bhk->bhv', S, -kk_t)
        S = (S * w_t[:, :, None, :] + sa[..., None] * (kk_t * a_t)[:, :, None, :]
             + v_t[..., None] * k_t[:, :, None, :])
        y = jnp.einsum('bhvk,bhk->bhv', S, r_t)
        return S, y

    xs = tuple(jnp.swapaxes(t, 0, 1) for t in (r, w, k, v, kk, a))
    S, y = lax.scan(step, S0, xs)
    return jnp.swapaxes(y, 0, 1), S

def retention_branch(p_ret, pos0, S0):
    B, T, _ = p_ret.shape
    q, k, v, g = split_cols(p_ret, (RET_HEADS * RET_DK, RET_HEADS * RET_DK, RET_HEADS * RET_DV, RET_HEADS * RET_DV))
    pos = pos0 + jnp.arange(T, dtype=jnp.int32)
    q = rope(q.reshape(B, T, RET_HEADS, RET_DK), pos)
    k = rope(k.reshape(B, T, RET_HEADS, RET_DK), pos) * (RET_DK ** -0.5)
    v = v.reshape(B, T, RET_HEADS, RET_DV)
    log_gamma = jnp.log1p(-jnp.exp2(-5.0 - jnp.arange(RET_HEADS, dtype=jnp.float32)))
    o, S = retention_scan(q, k, v, S0, log_gamma)
    o = head_rmsnorm(o).reshape(B, T, RET_HEADS * RET_DV)
    return jax.nn.silu(g) * o, S

def gla_branch(p_gla, S0, gk_up, gk_bias, norm_w):
    B, T, _ = p_gla.shape
    q, k, v, g, gk = split_cols(p_gla, (GLA_HEADS * GLA_DK, GLA_HEADS * GLA_DK, GLA_HEADS * GLA_DV, GLA_HEADS * GLA_DV, GLA_GATE_RANK))
    log_a = jax.nn.log_sigmoid(gk @ gk_up + gk_bias) / GLA_GATE_NORM
    q = q.reshape(B, T, GLA_HEADS, GLA_DK) * (GLA_DK ** -0.5)
    k = k.reshape(B, T, GLA_HEADS, GLA_DK)
    v = v.reshape(B, T, GLA_HEADS, GLA_DV)
    log_a = log_a.reshape(B, T, GLA_HEADS, GLA_DK)
    o, S = gla_scan(q, k, v, log_a, S0)
    o = (head_rmsnorm(o) * norm_w).reshape(B, T, GLA_HEADS * GLA_DV)
    return jax.nn.silu(g) * o, S

def rwkv7_branch(p_rwkv, S0, prev0, mu, w0, w_up, a0, a_up, g_up, kk_scale, ka, rk, ln_w, ln_b):
    B, T, _ = p_rwkv.shape
    prev = jnp.concatenate([prev0[:, None, :], p_rwkv[:, :-1, :]], axis=1)
    xm = p_rwkv + (prev - p_rwkv) * mu
    r, wd, k, v, ad, gd = split_cols(xm, (RWKV_W, RWKV_DECAY_RANK, RWKV_W, RWKV_W, RWKV_A_RANK, RWKV_GATE_RANK))
    w_log = -jax.nn.softplus(-(w0 + jnp.tanh(wd) @ w_up)) - 0.5
    decay = jnp.exp(-jnp.exp(w_log))
    a = jax.nn.sigmoid(a0 + ad @ a_up)
    g = jax.nn.sigmoid(gd) @ g_up
    hs = lambda t: t.reshape(B, T, RWKV_HEADS, RWKV_HD)
    kk = hs(k * kk_scale)
    kk = kk * lax.rsqrt(jnp.sum(kk * kk, axis=-1, keepdims=True) + 1e-12)
    k = k * (1.0 + (a - 1.0) * ka)
    r_h, k_h, v_h, w_h, a_h = hs(r), hs(k), hs(v), hs(decay), hs(a)
    y, S = rwkv7_scan(r_h, w_h, k_h, v_h, kk, a_h, S0)
    y = head_groupnorm(y, ln_w, ln_b)
    y = y + jnp.sum(r_h * k_h * rk, axis=-1, keepdims=True) * v_h
    return y.reshape(B, T, RWKV_W) * g, S, p_rwkv[:, -1, :]

def token_mixer(h, pos0, s_ret, s_gla, s_rwkv, s_shift, p, l):
    B, T, _ = h.shape
    f32 = jnp.float32
    proj = (h @ p['w_in'][l]).astype(f32)
    p_ret, p_gla, p_rwkv, p_merge = split_cols(proj, (RET_PROJ, GLA_PROJ, RWKV_PROJ, MERGE_COLS))
    y_ret, sr = retention_branch(p_ret, pos0, s_ret.astype(f32))
    y_gla, sg = gla_branch(p_gla, s_gla.astype(f32), p['gla_gk_up'][l], p['gla_gk_bias'][l], p['gla_norm_w'][l])
    y_rw, sw, ss = rwkv7_branch(p_rwkv, s_rwkv.astype(f32), s_shift.astype(f32), p['rwkv_mu'][l],
                                p['rwkv_w0'][l], p['rwkv_w_up'][l], p['rwkv_a0'][l], p['rwkv_a_up'][l],
                                p['rwkv_g_up'][l], p['rwkv_kk_scale'][l], p['rwkv_ka'][l], p['rwkv_rk'][l],
                                p['rwkv_ln_w'][l], p['rwkv_ln_b'][l])
    gates = jax.nn.sigmoid(p_merge).reshape(B, T, N_BRANCH, D_MODEL)
    wb = p['w_branch'][l]
    merged = (gates[:, :, 0] * (y_ret @ wb[0]) + gates[:, :, 1] * (y_gla @ wb[1])
              + gates[:, :, 2] * (y_rw @ wb[2]))
    out = merged.astype(h.dtype) @ p['w_out'][l]
    return out, sr, sg, sw, ss

def swiglu(h, w1, w3, w2):
    return (jax.nn.silu(h @ w1) * (h @ w3)) @ w2

def moe_swiglu(h, router, w1, w3, w2):
    logits = (h @ router).astype(jnp.float32)
    top_v, top_i = lax.top_k(logits, TOP_K)
    probs = jax.nn.softmax(top_v, axis=-1)
    gate = jnp.sum(jax.nn.one_hot(top_i, N_EXPERTS, dtype=jnp.float32) * probs[..., None], axis=-2)
    out = jnp.zeros(h.shape, jnp.float32)
    for e in range(N_EXPERTS):
        out = out + gate[..., e:e + 1] * swiglu(h, w1[e], w3[e], w2[e]).astype(jnp.float32)
    return out.astype(h.dtype)

def trunk(x, pos0, s_ret, s_gla, s_rwkv, s_shift, p):
    new_ret, new_gla, new_rwkv, new_shift = [], [], [], []
    for l in range(DEPTH):
        h = rmsnorm(x, p['norm_mix'][l])
        m, sr, sg, sw, ss = token_mixer(h, pos0, s_ret[l], s_gla[l], s_rwkv[l], s_shift[l], p, l)
        x = x + m.astype(x.dtype)
        h = rmsnorm(x, p['norm_ffn'][l])
        j = l // 2
        if l % 2 == 0:
            f = swiglu(h, p['ffn_w1'][j], p['ffn_w3'][j], p['ffn_w2'][j])
        else:
            f = moe_swiglu(h, p['moe_router'][j], p['moe_w1'][j], p['moe_w3'][j], p['moe_w2'][j])
        x = x + f.astype(x.dtype)
        new_ret.append(sr)
        new_gla.append(sg)
        new_rwkv.append(sw)
        new_shift.append(ss)
    y = rmsnorm(x, p['norm_final'])
    return y, jnp.stack(new_ret), jnp.stack(new_gla), jnp.stack(new_rwkv), jnp.stack(new_shift)

def setup_inputs(seed: int = 0) -> dict:
    key = jax.random.key(seed)
    ks = iter(jax.random.split(key, 40))
    nrm = lambda shape, scale: jax.random.normal(next(ks), shape, jnp.float32) * scale
    uni = lambda shape, lo, hi: jax.random.uniform(next(ks), shape, jnp.float32, lo, hi)
    n_dense = (DEPTH + 1) // 2
    n_moe = DEPTH // 2
    D = D_MODEL
    return {
        'x_prompt': nrm((BATCH, SEQ, D), 1.0),
        'x_sample': nrm((DEC_BATCH, DEC_SEQ, D), 1.0),
        'state_ret': nrm((DEPTH, DEC_BATCH, RET_HEADS, RET_DK, RET_DV), 1.0),
        'state_gla': nrm((DEPTH, DEC_BATCH, GLA_HEADS, GLA_DK, GLA_DV), 1.0),
        'state_rwkv': nrm((DEPTH, DEC_BATCH, RWKV_HEADS, RWKV_HD, RWKV_HD), 0.5),
        'state_shift': nrm((DEPTH, DEC_BATCH, RWKV_PROJ), 1.0),
        'norm_mix': 1.0 + nrm((DEPTH, D), 0.02),
        'norm_ffn': 1.0 + nrm((DEPTH, D), 0.02),
        'w_in': nrm((DEPTH, D, IN_COLS), D ** -0.5),
        'gla_gk_up': nrm((DEPTH, GLA_GATE_RANK, GLA_HEADS * GLA_DK), GLA_GATE_RANK ** -0.5),
        'gla_gk_bias': nrm((DEPTH, GLA_HEADS * GLA_DK), 0.1),
        'gla_norm_w': 1.0 + nrm((DEPTH, GLA_DV), 0.02),
        'rwkv_mu': uni((DEPTH, RWKV_PROJ), 0.0, 1.0),
        'rwkv_w0': uni((DEPTH, RWKV_W), -6.0, -1.0),
        'rwkv_w_up': nrm((DEPTH, RWKV_DECAY_RANK, RWKV_W), 0.1 * RWKV_DECAY_RANK ** -0.5),
        'rwkv_a0': nrm((DEPTH, RWKV_W), 0.1),
        'rwkv_a_up': nrm((DEPTH, RWKV_A_RANK, RWKV_W), 0.5 * RWKV_A_RANK ** -0.5),
        'rwkv_g_up': nrm((DEPTH, RWKV_GATE_RANK, RWKV_W), RWKV_GATE_RANK ** -0.5),
        'rwkv_kk_scale': 0.85 + nrm((DEPTH, RWKV_W), 0.02),
        'rwkv_ka': 1.0 + nrm((DEPTH, RWKV_W), 0.02),
        'rwkv_rk': nrm((DEPTH, RWKV_HEADS, RWKV_HD), 0.1),
        'rwkv_ln_w': 1.0 + nrm((DEPTH, RWKV_W), 0.02),
        'rwkv_ln_b': nrm((DEPTH, RWKV_W), 0.02),
        'w_branch': nrm((DEPTH, N_BRANCH, RET_HEADS * RET_DV, D), (RET_HEADS * RET_DV) ** -0.5),
        'w_out': nrm((DEPTH, D, D), D ** -0.5),
        'ffn_w1': nrm((n_dense, D, D_FF), D ** -0.5),
        'ffn_w3': nrm((n_dense, D, D_FF), D ** -0.5),
        'ffn_w2': nrm((n_dense, D_FF, D), D_FF ** -0.5),
        'moe_router': nrm((n_moe, D, N_EXPERTS), D ** -0.5),
        'moe_w1': nrm((n_moe, N_EXPERTS, D, D_FF), D ** -0.5),
        'moe_w3': nrm((n_moe, N_EXPERTS, D, D_FF), D ** -0.5),
        'moe_w2': nrm((n_moe, N_EXPERTS, D_FF, D), D_FF ** -0.5),
        'norm_final': 1.0 + nrm((D,), 0.02),
    }

def reference(x_prompt, x_sample, state_ret, state_gla, state_rwkv, state_shift, norm_mix, norm_ffn, w_in,
              gla_gk_up, gla_gk_bias, gla_norm_w, rwkv_mu, rwkv_w0, rwkv_w_up, rwkv_a0, rwkv_a_up, rwkv_g_up,
              rwkv_kk_scale, rwkv_ka, rwkv_rk, rwkv_ln_w, rwkv_ln_b, w_branch, w_out, ffn_w1, ffn_w3, ffn_w2,
              moe_router, moe_w1, moe_w3, moe_w2, norm_final):
    p = {
        'norm_mix': norm_mix, 'norm_ffn': norm_ffn, 'w_in': w_in,
        'gla_gk_up': gla_gk_up, 'gla_gk_bias': gla_gk_bias, 'gla_norm_w': gla_norm_w,
        'rwkv_mu': rwkv_mu, 'rwkv_w0': rwkv_w0, 'rwkv_w_up': rwkv_w_up, 'rwkv_a0': rwkv_a0,
        'rwkv_a_up': rwkv_a_up, 'rwkv_g_up': rwkv_g_up, 'rwkv_kk_scale': rwkv_kk_scale, 'rwkv_ka': rwkv_ka,
        'rwkv_rk': rwkv_rk, 'rwkv_ln_w': rwkv_ln_w, 'rwkv_ln_b': rwkv_ln_b,
        'w_branch': w_branch, 'w_out': w_out,
        'ffn_w1': ffn_w1, 'ffn_w3': ffn_w3, 'ffn_w2': ffn_w2,
        'moe_router': moe_router, 'moe_w1': moe_w1, 'moe_w3': moe_w3, 'moe_w2': moe_w2,
        'norm_final': norm_final,
    }
    f32 = jnp.float32
    bp = x_prompt.shape[0]
    z_ret = jnp.zeros((DEPTH, bp, RET_HEADS, RET_DK, RET_DV), f32)
    z_gla = jnp.zeros((DEPTH, bp, GLA_HEADS, GLA_DK, GLA_DV), f32)
    z_rwkv = jnp.zeros((DEPTH, bp, RWKV_HEADS, RWKV_HD, RWKV_HD), f32)
    z_shift = jnp.zeros((DEPTH, bp, RWKV_PROJ), f32)
    y_prompt, ret_p, gla_p, rwkv_p, shift_p = trunk(x_prompt, 0, z_ret, z_gla, z_rwkv, z_shift, p)
    y_sample, ret_s, gla_s, rwkv_s, shift_s = trunk(x_sample, PAST_LEN, state_ret, state_gla, state_rwkv, state_shift, p)
    return (y_prompt, y_sample, ret_p, gla_p, rwkv_p, shift_p, ret_s, gla_s, rwkv_s, shift_s)


_drawn_inputs = setup_inputs


def setup_inputs(seed=0):
    import zlib

    import numpy as np

    out = dict(_drawn_inputs(seed))
    spreads = {}
    factors = {'gla_norm_w': 3.504,
     'rwkv_w_up': 8.0,
     'rwkv_kk_scale': 7.483,
     'rwkv_ln_b': 2.852,
     'norm_final': 7.322,
     'rwkv_ln_w': 3.619}
    for name, (base, spread) in spreads.items():
        noise = np.random.default_rng([zlib.crc32(name.encode()), seed]).standard_normal(out[name].shape)
        drawn = base * np.exp(spread * noise) if base else spread * noise
        out[name] = jnp.asarray(drawn.astype(out[name].dtype))
    for name, factor in factors.items():
        out[name] = (out[name] * factor).astype(out[name].dtype)
    return out
```

```python
from contextlib import ExitStack, contextmanager

import numpy as np

import concourse.bass as bass
from concourse import mybir

F32 = mybir.dt.float32
U32 = mybir.dt.uint32
ALU = mybir.AluOpType
ACT = mybir.ActivationFunctionType

D = 1024
DEPTH = 2
NP = 256
NB, NT = 8, 4
NS = NB * NT
T = NP + NS
TILE = 128
PAST = 2048
KT = D // 128
RET_H, RET_DK, RET_DV = 8, 64, 128
GLA_H, GLA_DK, GLA_DV, GLA_RANK = 4, 128, 256, 16
RW_H, RW_HD = 16, 64
RW_COLS = 3328
NLORA = 2
RW_SLABS = RW_COLS // 128
FF = 2816
FT = FF // 128
NE = 8
CAP = 96
MAXP = NE + 2 * T // CAP
NFF = NE + 1
EPS = 1e-6
GN_EPS = 64e-5
KAPPA = float(np.exp(-0.5))

RING = 8
G_RET, G_RET_OUT, G_GLA, G_GLA_OUT, G_RW, G_RW_OUT, G_OUT, G_FF = 0, 3, 5, 8, 10, 13, 15, 16
MIX_SLABS = G_FF * RING
UP_SLABS = 2 * FT
DOWN_SLABS = 24
FF_SLABS = UP_SLABS + DOWN_SLABS

V_MIX, V_FFN, V_GKB, V_GNW, V_MU, V_W0, V_A0, V_KKS, V_KA, V_RK, V_LNW, V_LNB, NV = (
    0, 8, 16, 20, 22, 48, 56, 64, 72, 80, 88, 96, 104)

LEVELS = (1, 2, 4, 8, 16, 32, 64)


def constants():
    c = {}
    p = np.arange(128)
    eye = np.eye(128)
    c["ident"] = eye
    c["ones"] = np.ones((128, 128))
    c["headones"] = (p[:, None] // 64 == p[None, :] // 64) * 1.0
    c["swap"] = (p[:, None] == (p[None, :] ^ 32)) * 1.0
    c["eye64"] = (p[:, None] % 64 == np.arange(64)[None, :]) * 1.0
    pos = np.concatenate([np.arange(NP), np.tile(PAST + np.arange(NT), NB)]).astype(np.float32)
    inv = (np.float32(10000.0) ** (-np.arange(32, dtype=np.float32) / np.float32(32))).astype(np.float32)
    ang = (pos[:, None] * inv[None, :]).astype(np.float32)
    cos, sin = np.cos(ang.astype(np.float64)).T, np.sin(ang.astype(np.float64)).T
    cosp = cos[p % 32]
    sinp = sin[p % 32] * np.where(p % 64 < 32, -1.0, 1.0)[:, None]
    c["qcos"], c["qsin"] = cosp, sinp
    c["kcos"], c["ksin"] = cosp * RET_DK ** -0.5, sinp * RET_DK ** -0.5
    lg = np.log1p(-np.exp2(-5.0 - np.arange(RET_H)))
    i = np.arange(128)
    dif = i[None, :] - i[:, None]
    dm = np.where(dif >= 0, np.exp(lg[:, None, None] * np.maximum(dif, 0)), 0.0)
    c["dmP"] = dm.transpose(1, 0, 2).reshape(128, -1)
    same = (i[:32, None] // NT == i[None, :32] // NT)
    dms = np.zeros((128, RET_H, 32))
    dms[:32] = (dm[:, :32, :32] * same).transpose(1, 0, 2)
    c["dmS"] = dms.reshape(128, -1)
    n = np.concatenate([np.arange(128), np.tile(np.arange(NT), NB)])
    hp = 2 * np.arange(4)[None, :] + (p // 64)[:, None]
    c["qdec"] = np.exp(lg[hp][:, :, None] * (n + 1.0)).reshape(128, -1)
    c["kdecP"] = np.exp(lg[None, :] * (127.0 - i)[:, None])
    c["kdecS"] = np.exp(lg[None, :] * (NT - 1.0 - i % NT)[:, None])
    c["cdec"] = np.stack([np.exp(lg[hp] * 128), np.exp(lg[hp] * NT)], -1).reshape(128, -1)
    c["strict"] = (i[:, None] < i[None, :]) * 1.0
    c["causal"] = (i[:, None] <= i[None, :]) * 1.0
    c["strictS"] = np.zeros((128, 32)); c["strictS"][:32] = c["strict"][:32, :32] * same
    c["causalS"] = np.zeros((128, 32)); c["causalS"][:32] = c["causal"][:32, :32] * same
    keep = np.ones(T); keep[[0, 128]] = 0; keep[NP::NT] = 0
    c["keep"] = np.tile(keep, (128, 1))
    c["inseq"] = np.zeros((128, NB)); c["inseq"][:32] = (i[:32, None] // NT == np.arange(NB)[None, :])
    c["seqcols"] = np.tile((np.arange(NB)[:, None] == np.arange(32)[None, :] // NT).reshape(-1), (128, 1))
    c["valid"] = np.stack([np.ones(128), np.ones(128), p < NS], 1)
    c["nowhere"] = (c["valid"] - 1) * 1e6
    c["place"] = np.concatenate([128 * np.arange(3)[None, :] + p[:, None], np.full((128, 3), -1.0)], 1)
    c["column"] = np.tile(np.arange(float(CAP)), (128, 1))
    c["passno"] = np.tile(np.arange(float(MAXP)), (128, 1))
    c["dense_passes"] = np.full((128, 1), T / CAP)
    c["iota8"] = np.tile(np.arange(8.0), (128, 1))
    c["flag"] = np.tile(np.array([0.0, 1.0, 1.0, 0.0]), (128, 1))
    c["eps"] = np.tile(np.array([EPS, 1e-12, GN_EPS, 0.0]), (128, 1))
    off, at = 0, {}
    for k, v in c.items():
        at[k] = (off, v.shape[1])
        off += v.shape[1]
    table = np.concatenate([v.astype(np.float32) for v in c.values()], 1)
    m = []
    for s in LEVELS:
        blk = i // (2 * s)
        lo, hi = i % (2 * s) < s, i % (2 * s) >= s
        m.append((blk[:, None] == blk[None, :]) & lo[:, None] & hi[None, :])
    m += [x.T for x in m]
    m.append(eye > 0)
    return table, at, np.concatenate(m, 1).astype(np.uint32)


TABLE, TABLE_AT, MASKS = constants()


class Signals:

    def __init__(self, nc, phase):
        self.nc, self.phase, self.sems = nc, phase, {}

    def __call__(self, name):
        if name not in self.sems:
            self.sems[name] = self.nc.alloc_semaphore(name=f"{self.phase}_{name}")
        return self.sems[name]


@contextmanager
def phase(nc, name):
    with nc.cleanup_on_exit():
        sig = Signals(nc, name)
        with nc.Block() as block:
            yield block, sig


def rep(ap, axis, n):
    shape = list(ap.shape)
    return ap.unsqueeze(axis).to_broadcast(shape[:axis] + [n] + shape[axis:])


def wide(ap, n):
    return ap.to_broadcast(list(ap.shape[:-1]) + [n])


def build(nc, xT_in, w_mix, w_lora, w_rank, w_gkup, vec_in, vecf_in, router_in, w_ff, s_ret, s_gla, s_rw,
          s_shift, table_in, masks_in, yT_out, ret_p, ret_s, gla_p, gla_s, rw_p, rw_s, shift_out):
    def sb(name, shape, dt=F32):
        return nc.alloc_sbuf_tensor(name, shape, dt)

    xT = sb("xT", [128, KT, T])
    hT = sb("hT", [128, KT, T])
    merged = sb("merged", [128, KT, T])
    proj = sb("proj", [128, 24, T])
    y = sb("y", [128, KT, T])
    ring = sb("ring", [128, RING, KT, 128])
    lora_w = sb("lora_w", [128, KT, 272])
    gkup = sb("gkup", [16, 512])
    vec = sb("vec", [128, NV])
    vecf = sb("vecf", [128, KT])
    router = sb("router", [128, KT, NE])
    ctl = sb("ctl", [128, MAXP + 1], U32)
    table = sb("table", [128, TABLE.shape[1]])
    masks = sb("masks", [128, MASKS.shape[1]], U32)
    lora = sb("lora", [128, NLORA, T])
    work = sb("work", [128, 18500])
    bank = [nc.alloc_psum_tensor(f"bank{i}", [128, 512], F32) for i in range(8)]

    def cst(name):
        o, n = TABLE_AT[name]
        return table[:, o:o + n]

    ident, ones, headones, eye64 = cst("ident"), cst("ones"), cst("headones"), cst("eye64")
    eps, tiny, gn_eps = (cst("eps")[:, i:i + 1] for i in range(3))

    def level_mask(s, later_rows=False):
        i = LEVELS.index(s) + (len(LEVELS) if later_rows else 0)
        return masks[:, 128 * i:128 * i + 128]

    diag_mask = masks[:, 128 * 2 * len(LEVELS):128 * (2 * len(LEVELS) + 1)]

    def settle(eng):
        eng.sem_inc(settled, 1)

    def grant(eng, *sems, by=1):
        for sem in sems:
            eng.sem_inc(sem, by)

    class Work:

        def __init__(self):
            self.at = 0

        def __call__(self, *dims):
            n = int(np.prod(dims))
            ap = work[:, self.at:self.at + n]
            self.at += n
            assert self.at <= 18500, self.at
            if len(dims) == 1:
                return ap
            names = [f"d{i}" for i in range(len(dims))]
            return ap.rearrange(f"p ({' '.join(names)}) -> p {' '.join(names)}", **dict(zip(names, dims)))

    settled = nc.alloc_semaphore(name="settled")

    with phase(nc, "start") as (block, sig):
        @block.sync
        def _(sp):
            sp.dma_start(table[:, :], table_in).then_inc(sig("loaded"), 16)
            sp.dma_start(masks[:, :], masks_in).then_inc(sig("loaded"), 16)
            sp.dma_start(xT[:, :, :], xT_in).then_inc(sig("loaded"), 16)
            sp.dma_start(vecf[:, :], vecf_in).then_inc(sig("loaded"), 16)
            sp.dma_start(router[:, :, :], router_in).then_inc(sig("loaded"), 16)
            sp.wait_ge(sig("loaded"), 5 * 16)

    def rms(block, sig, gain, out, psum, w):
        sq = w(KT, T)
        root, rs = w(T), w(T)

        @block.scalar
        def _(act):
            nc.scalar.activation(sq, xT[:, :, :], ACT.Square).then_inc(sig("squares"), 1)
            act.wait_ge(sig("sum"), 1)
            nc.scalar.activation(root, psum[:, 0:T], ACT.Sqrt, scale=1.0 / D, bias=eps).then_inc(sig("root"), 1)

        @block.tensor
        def _(pe):
            pe.wait_ge(sig("squares"), 1)
            for k in range(KT):
                mm = nc.tensor.matmul(psum[:, 0:T], ones, sq[:, k, :], start=(k == 0), stop=(k == KT - 1))
            mm.then_inc(sig("sum"), 1)

        @block.vector
        def _(dve):
            dve.wait_ge(sig("root"), 1)
            nc.vector.reciprocal(rs, root).then_inc(sig("rs"), 1)
            dve.wait_ge(sig("rs"), 1)
            dve.wait_ge(sig("vec"), 16)
            for k in range(KT):
                last = nc.vector.scalar_tensor_tensor(out=out[:, k, :], in0=xT[:, k, :], scalar=gain[:, k:k + 1],
                                                      in1=rs, op0=ALU.mult, op1=ALU.mult)
            last.then_inc(sig("normed"), 1)

    SAMPLE = slice(NP, T)

    def heads_of(ap, hh):
        return ap[64 * hh:64 * hh + 64]

    def retention(nc, block, sig, layer):
        w = Work()
        c1, c2, qr, kr = w(2, T), w(2, T), w(T), w(T)
        qd = w(128 + NS)
        vst = w(2, T)
        vtok, vtokS = w(2, 2, 128), w(2, 128)
        ktok, ktokS = w(2, 2, 64), w(2, 64)
        kseq = w(NB, 128)
        att, attS = w(2, 2, 128), w(2, 32)
        mid, fin = w(RET_DV), w(RET_DV)
        st = w(NB, RET_DV)
        o, osq, lnv, rs = w(2, T), w(2, T), w(2, T), w(2, T)
        dmP = cst("dmP").rearrange("p (h i) -> p h i", h=RET_H)
        dmS = cst("dmS").rearrange("p (h i) -> p h i", h=RET_H)
        qdec = cst("qdec").rearrange("p (h i) -> p h i", h=4)
        cdec = cst("cdec").rearrange("p (h i) -> p h i", h=4)
        B = bank
        PAIRS = RET_H // 2

        @block.sync
        def _(sp):
            grant(sp, sig("stored"), by=32)
            with sp.Fori(0, PAIRS) as i:
                sp.wait_ge(sig("stored"), i * 32 + 32)
                sp.dma_start(st, s_ret[layer, i]).then_inc(sig("state"), 16)
                sp.wait_ge(sig("fin"), i + 1)
                sp.dma_start(ret_p[layer, i], fin).then_inc(sig("stored"), 16)
                sp.wait_ge(sig("stS"), i * 2 + 2)
                sp.dma_start(ret_s[layer, i], st).then_inc(sig("stored"), 16)
            sp.wait_ge(sig("stored"), PAIRS * 32 + 32)

        @block.tensor
        def _(pe):
            with pe.Fori(0, PAIRS) as i:
                pe.wait_ge(sig("y"), i + 1)
                nc.tensor.matmul(B[0][:, 0:T], cst("swap"), proj[:, i, :], start=True, stop=True)
                nc.tensor.matmul(B[1][:, 0:T], cst("swap"), proj[:, i + 4, :], start=True,
                                 stop=True).then_inc(sig("swapped"), 1)
                pe.wait_ge(sig("vst"), i + 1)
                for t in range(2):
                    for h in range(2):
                        nc.tensor.transpose(B[2][:, 256 * t + 128 * h:][:, 0:128], vst[:, h, 128 * t:128 * t + 128], ident)
                for h in range(2):
                    mm = nc.tensor.transpose(B[3][0:NS, 128 * h:128 * h + 128], vst[:, h, SAMPLE], ident)
                mm.then_inc(sig("vT"), 1)
                pe.wait_ge(sig("rot"), i + 1)
                for t in range(2):
                    nc.tensor.transpose(B[4][:, 128 * t:128 * t + 128], kr[:, 128 * t:128 * t + 128], ident)
                nc.tensor.transpose(B[4][0:NS, 256:384], kr[:, SAMPLE], ident).then_inc(sig("kT"), 1)
                for h in range(2):
                    for t in range(2):
                        c = slice(128 * t, 128 * t + 128)
                        nc.tensor.matmul(B[5 + h][:, c], heads_of(kr, h)[:, c],
                                         heads_of(qr, h)[:, c], start=True, stop=True)
                for h in range(2):
                    mm = nc.tensor.matmul(B[5 + h][0:NS, SAMPLE], heads_of(kr, h)[:, SAMPLE],
                                          heads_of(qr, h)[:, SAMPLE], start=True, stop=True)
                mm.then_inc(sig("scores"), 1)
                pe.wait_ge(sig("ktok"), i + 1)
                pe.wait_ge(sig("vtok"), i + 1)
                for h in range(2):
                    mm = nc.tensor.matmul(heads_of(B[7], h)[:, 0:128], ktok[:, 0, h, :], vtok[:, 0, h, :],
                                          start=True, stop=True)
                mm.then_inc(sig("mid_ps"), 1)
                pe.wait_ge(sig("att"), i + 1)
                pe.wait_ge(sig("qd"), i + 1)
                pe.wait_ge(sig("state"), (i + 1) * 16)
                pe.wait_ge(sig("mid"), i + 1)
                for h in range(2):
                    ob = B[h]
                    nc.tensor.matmul(ob[:, 0:128], vtok[:, 0, h, :], att[:, h, 0, :], start=True, stop=True)
                    nc.tensor.matmul(ob[:, SAMPLE], vtokS[0:NS, h, :], attS[0:NS, h, :], start=True, stop=False)
                    for b in range(NB):
                        nc.tensor.matmul(ob[:, NP + NT * b:NP + NT * b + NT], heads_of(st, h)[:, b, :],
                                         heads_of(qd, h)[:, 128 + NT * b:128 + NT * b + NT], start=False,
                                         stop=(b == NB - 1))
                    nc.tensor.matmul(ob[:, 128:256], vtok[:, 1, h, :], att[:, h, 1, :], start=True, stop=False)
                    mm = nc.tensor.matmul(ob[:, 128:256], heads_of(mid, h), heads_of(qd, h)[:, 0:128],
                                          start=False, stop=True)
                mm.then_inc(sig("o_ps"), 1)
                for h in range(2):
                    mm = nc.tensor.matmul(heads_of(B[7], h)[:, 0:128], ktok[:, 1, h, :], vtok[:, 1, h, :],
                                          start=True, stop=True)
                mm.then_inc(sig("fin_ps"), 1)
                pe.wait_ge(sig("kseq"), i + 1)
                for b in range(NB):
                    for h in range(2):
                        mm = nc.tensor.matmul(heads_of(B[5 + b // 4], h)[:, 128 * (b % 4):128 * (b % 4) + 128],
                                              kseq[0:NS, b, 64 * h:64 * h + 64], vtokS[0:NS, h, :],
                                              start=True, stop=True)
                mm.then_inc(sig("stS_ps"), 1)
                pe.wait_ge(sig("osq"), i + 1)
                for h in range(2):
                    mm = nc.tensor.matmul(B[2 + h][:, 0:T], ones, osq[:, h, :], start=True, stop=True)
                mm.then_inc(sig("ss"), 1)

        @block.scalar
        def _(act):
            with act.Fori(0, PAIRS) as i:
                act.wait_ge(sig("y"), i + 1)
                nc.scalar.activation(vst, proj[:, bass.ds(i * 2 + 8, 2), :], ACT.Copy).then_inc(sig("vst"), 1)
                act.wait_ge(sig("vT"), i + 1)
                nc.scalar.activation(vtok, B[2][:, :].rearrange("p (t h d) -> p t h d", t=2, h=2), ACT.Copy)
                nc.scalar.activation(vtokS[0:NS], B[3][0:NS, 0:256].rearrange("p (h d) -> p h d", h=2),
                                     ACT.Copy).then_inc(sig("vtok"), 1)
                act.wait_ge(sig("mid_ps"), i + 1)
                nc.scalar.activation(mid, B[7][:, 0:128], ACT.Copy).then_inc(sig("mid"), 1)
                act.wait_ge(sig("o_ps"), i + 1)
                for h in range(2):
                    nc.scalar.activation(o[:, h, :], B[h][:, 0:T], ACT.Copy)
                    ins = nc.scalar.activation(osq[:, h, :], B[h][:, 0:T], ACT.Square)
                ins.then_inc(sig("osq"), 1)
                act.wait_ge(sig("ss"), i + 1)
                for h in range(2):
                    ins = nc.scalar.activation(lnv[:, h, :], B[2 + h][:, 0:T], ACT.Ln, scale=1.0 / RET_DV, bias=eps)
                ins.then_inc(sig("ln"), 1)
                act.wait_ge(sig("ln"), i + 1)
                nc.scalar.activation(rs, lnv, ACT.Exp, scale=-0.5).then_inc(sig("rs"), 1)

        @block.vector
        def _(dve):
            grant(dve, sig("y"))
            with dve.Fori(0, PAIRS) as i:
                dve.wait_ge(sig("swapped"), i + 1)
                nc.vector.tensor_tensor(c1[:, 0, :], proj[:, i, :], cst("qcos"), ALU.mult)
                nc.vector.tensor_tensor(c1[:, 1, :], proj[:, i + 4, :], cst("kcos"), ALU.mult)
                nc.vector.tensor_tensor(c2[:, 0, :], B[0][:, 0:T], cst("qsin"), ALU.mult)
                nc.vector.tensor_tensor(c2[:, 1, :], B[1][:, 0:T], cst("ksin"), ALU.mult).then_inc(sig("cs"), 1)
                dve.wait_ge(sig("cs"), i + 1)
                nc.vector.tensor_tensor(qr, c1[:, 0, :], c2[:, 0, :], ALU.add)
                nc.vector.tensor_tensor(kr, c1[:, 1, :], c2[:, 1, :], ALU.add).then_inc(sig("rot"), 1)
                dve.wait_ge(sig("rot"), i + 1)
                nc.vector.tensor_tensor(qd, qr[:, 128:T], qdec[:, i, :], ALU.mult).then_inc(sig("qd"), 1)
                dve.wait_ge(sig("kT"), i + 1)
                nc.vector.tensor_tensor(ktok, B[4][:, 0:256].rearrange("p (t h d) -> p t h d", t=2, h=2),
                                        rep(wide(cst("kdecP")[:, bass.ds(i * 2, 2)].unsqueeze(2), 64), 1, 2), ALU.mult)
                nc.vector.tensor_tensor(ktokS[0:NS], B[4][0:NS, 256:384].rearrange("p (h d) -> p h d", h=2),
                                        wide(cst("kdecS")[0:NS, bass.ds(i * 2, 2)].unsqueeze(2), 64),
                                        ALU.mult).then_inc(sig("ktok"), 1)
                dve.wait_ge(sig("scores"), i + 1)
                for h in range(2):
                    nc.vector.tensor_tensor(att[:, h], B[5 + h][:, 0:NP].rearrange("p (t q) -> p t q", t=2),
                                            rep(dmP[:, i * 2 + h, :], 1, 2), ALU.mult)
                    ins = nc.vector.tensor_tensor(attS[0:NS, h, :], B[5 + h][0:NS, SAMPLE], dmS[0:NS, i * 2 + h, :],
                                                  ALU.mult)
                ins.then_inc(sig("att"), 1)
                dve.wait_ge(sig("ktok"), i + 1)
                nc.vector.tensor_tensor(kseq[0:NS], rep(ktokS[0:NS].rearrange("p h d -> p (h d)"), 1, NB),
                                        wide(cst("inseq")[0:NS].unsqueeze(2), 128), ALU.mult).then_inc(sig("kseq"), 1)
                dve.wait_ge(sig("mid"), i + 1)
                dve.wait_ge(sig("fin_ps"), i + 1)
                dve.wait_ge(sig("stored"), i * 32 + 32)
                nc.vector.scalar_tensor_tensor(out=fin, in0=mid, scalar=cdec[:, i, 0:1], in1=B[7][:, 0:128],
                                               op0=ALU.mult, op1=ALU.add).then_inc(sig("fin"), 1)
                dve.wait_ge(sig("stS_ps"), i + 1)
                for n in range(2):
                    nc.vector.scalar_tensor_tensor(out=st[:, 4 * n:4 * n + 4, :], in0=st[:, 4 * n:4 * n + 4, :],
                                                   scalar=cdec[:, i, 1:2],
                                                   in1=B[5 + n][:, :].rearrange("p (b d) -> p b d", b=4),
                                                   op0=ALU.mult, op1=ALU.add).then_inc(sig("stS"), 1)
                dve.wait_ge(sig("rs"), i + 1)
                nc.vector.tensor_tensor(c1, o, rs, ALU.mult).then_inc(sig("on"), 1)
                dve.wait_ge(sig("on"), i + 1)
                nc.vector.tensor_tensor(y[:, bass.ds(i * 2, 2), :], c1, proj[:, bass.ds(i * 2 + 16, 2), :],
                                        ALU.mult).then_inc(sig("y"), 1)

    def gated_linear(nc, block, sig, layer):
        w = Work()
        cum = w(4, T)
        z = w(4, T)
        tmp1, tmp2 = w(4, T), w(4, T)
        la = w(4, T)
        w.at -= 4 * 4 * T
        q, k, v = w(T), w(T), w(2, T)
        dif, fac, ql, kl = w(2, T), w(2, T), w(2, T), w(2, T)
        dend, fend, kend, eb, qb = w(T), w(T), w(T), w(T), w(T)
        eend = w(2 + NB)
        w.at = max(w.at, 5 * 4 * T)
        vtok, vtokS = w(2, 256), w(256)
        ktok, ktokS, kseq = w(2, 128), w(128), w(NB, 128)
        att, attS = w(2, 128), w(32)
        mid, fin, st = w(256), w(256), w(NB, 256)
        o, osq, lnv, rs = w(2, T), w(2, T), w(T), w(T)
        B = bank

        @block.sync
        def _(sp):
            grant(sp, sig("stored"), by=32)
            with sp.Fori(0, GLA_H) as i:
                sp.wait_ge(sig("stored"), i * 32 + 32)
                sp.dma_start(st, s_gla[layer, i]).then_inc(sig("state"), 16)
                sp.wait_ge(sig("fin"), i + 1)
                sp.dma_start(gla_p[layer, i], fin).then_inc(sig("stored"), 16)
                sp.wait_ge(sig("stS"), i * NB + NB)
                sp.dma_start(gla_s[layer, i], st).then_inc(sig("stored"), 16)
            sp.wait_ge(sig("stored"), GLA_H * 32 + 32)

        @block.tensor
        def _(pe):
            for kt in range(KT):
                mm = nc.tensor.matmul(B[4][0:GLA_RANK, 0:T], lora_w[:, kt, 256:272], hT[:, kt, :],
                                      start=(kt == 0), stop=(kt == KT - 1))
            mm.then_inc(sig("gk_ps"), 1)
            pe.wait_ge(sig("gk"), 1)
            for h in range(GLA_H):
                mm = nc.tensor.matmul(B[h][:, 0:T], gkup[:, 128 * h:128 * h + 128], tmp2[0:GLA_RANK, 0, :],
                                      start=True, stop=True)
            mm.then_inc(sig("z_ps"), 1)
            grant(pe, sig("kT"), sig("o_ps"))
            pe.wait_ge(sig("z"), 1)
            with pe.Fori(0, GLA_H) as i:
                pe.wait_ge(sig("staged"), i + 1)
                for t in range(2):
                    for h in range(2):
                        nc.tensor.transpose(B[2][:, 256 * t + 128 * h:][:, 0:128], v[:, h, 128 * t:128 * t + 128], ident)
                for h in range(2):
                    mm = nc.tensor.transpose(B[3][0:NS, 128 * h:128 * h + 128], v[:, h, SAMPLE], ident)
                mm.then_inc(sig("vT"), 1)
                for n, s in enumerate((0,) + LEVELS):
                    if n == 0:
                        kk, qq = k, q
                    else:
                        pe.wait_ge(sig("lev"), i * len(LEVELS) + n)
                        kk, qq = kl[:, n % 2, :], ql[:, n % 2, :]
                    if n >= 2:
                        pe.wait_ge(sig("att"), i * 8 + n - 1)
                    for t in range(2):
                        c = slice(128 * t, 128 * t + 128)
                        mm = nc.tensor.matmul(B[n % 2][:, c], kk[:, c], qq[:, c], start=True, stop=True)
                    if s <= 2:
                        mm = nc.tensor.matmul(B[n % 2][0:NS, 256:288], kk[:, SAMPLE], qq[:, SAMPLE],
                                              start=True, stop=True)
                    mm.then_inc(sig("scores"), 1)
                pe.wait_ge(sig("kend"), i + 1)
                for t in range(2):
                    nc.tensor.transpose(B[4][:, 128 * t:128 * t + 128], kend[:, 128 * t:128 * t + 128], ident)
                nc.tensor.transpose(B[4][0:NS, 256:384], kend[:, SAMPLE], ident).then_inc(sig("kT"), 1)
                pe.wait_ge(sig("ktok"), i + 1)
                nc.tensor.matmul(B[5][:, 0:256], ktok[:, 0, :], vtok[:, 0, :], start=True,
                                 stop=True).then_inc(sig("mid_ps"), 1)
                nc.tensor.matmul(B[6][:, 0:256], ktok[:, 1, :], vtok[:, 1, :], start=True,
                                 stop=True).then_inc(sig("fin_ps"), 1)
                pe.wait_ge(sig("qb"), i + 1)
                pe.wait_ge(sig("att"), i * 8 + 8)
                pe.wait_ge(sig("mid"), i + 1)
                pe.wait_ge(sig("state"), (i + 1) * 16)
                for h in range(2):
                    ob, f = B[h], slice(128 * h, 128 * h + 128)
                    nc.tensor.matmul(ob[:, 0:128], vtok[:, 0, f], att[:, 0, :], start=True, stop=True)
                    nc.tensor.matmul(ob[:, SAMPLE], vtokS[0:NS, f], attS[0:NS, :], start=True, stop=False)
                    for b in range(NB):
                        c = slice(NP + NT * b, NP + NT * b + NT)
                        nc.tensor.matmul(ob[:, c], st[:, b, f], qb[:, c], start=False, stop=(b == NB - 1))
                    nc.tensor.matmul(ob[:, 128:256], vtok[:, 1, f], att[:, 1, :], start=True, stop=False)
                    mm = nc.tensor.matmul(ob[:, 128:256], mid[:, f], qb[:, 128:256], start=False, stop=True)
                mm.then_inc(sig("o_ps"), 1)
                pe.wait_ge(sig("kseq"), i + 1)
                pe.wait_ge(sig("fin"), i + 1)
                for b in range(NB):
                    mm = nc.tensor.matmul(B[4 + b // 2][:, 256 * (b % 2):256 * (b % 2) + 256], kseq[0:NS, b, :],
                                          vtokS[0:NS, :], start=True, stop=True)
                mm.then_inc(sig("stS_ps"), 1)
                pe.wait_ge(sig("osq"), i + 1)
                for h in range(2):
                    mm = nc.tensor.matmul(B[2][:, 0:T], ones, osq[:, h, :], start=(h == 0), stop=(h == 1))
                mm.then_inc(sig("ss"), 1)

        @block.scalar
        def _(act):
            act.wait_ge(sig("gk_ps"), 1)
            nc.scalar.activation(tmp2[0:GLA_RANK, 0, :], B[4][0:GLA_RANK, 0:T], ACT.Copy).then_inc(sig("gk"), 1)
            act.wait_ge(sig("z_ps"), 1)
            for h in range(GLA_H):
                ins = nc.scalar.activation(z[:, h, :], B[h][:, 0:T], ACT.Identity, bias=vec[:, V_GKB + h:V_GKB + h + 1])
            ins.then_inc(sig("z"), 1)
            act.wait_ge(sig("z"), 1)
            nc.scalar.activation(tmp1, z, ACT.Abs).then_inc(sig("absz"), 1)
            act.wait_ge(sig("absz"), 1)
            nc.scalar.activation(tmp2, tmp1, ACT.Exp, scale=-1.0).then_inc(sig("ez"), 1)
            act.wait_ge(sig("ez"), 1)
            nc.scalar.activation(tmp1, tmp2, ACT.Ln, bias=1.0).then_inc(sig("lnz"), 1)
            act.wait_ge(sig("cum"), 1)
            with act.Fori(0, GLA_H) as i:
                act.wait_ge(sig("y"), i + 1)
                nc.scalar.activation(q, proj[:, i, :], ACT.Copy, scale=GLA_DK ** -0.5)
                nc.scalar.activation(k, proj[:, i + 4, :], ACT.Copy)
                nc.scalar.activation(v, proj[:, bass.ds(i * 2 + 8, 2), :], ACT.Copy).then_inc(sig("staged"), 1)
                act.wait_ge(sig("dend"), i + 1)
                nc.scalar.activation(eb, cum[:, i, :], ACT.Exp)
                nc.scalar.activation(fend, dend, ACT.Exp)
                nc.scalar.activation(eend[:, 0:2], cum[:, i, 127:256:128], ACT.Exp)
                nc.scalar.activation(eend[:, 2:2 + NB], cum[:, i, NP + NT - 1:T:NT], ACT.Exp).then_inc(sig("eb"), 1)
                act.wait_ge(sig("vT"), i + 1)
                nc.scalar.activation(vtok, B[2][:, :].rearrange("p (t d) -> p t d", t=2), ACT.Copy)
                nc.scalar.activation(vtokS[0:NS], B[3][0:NS, 0:256], ACT.Copy).then_inc(sig("vtok"), 1)
                for n, s in enumerate(LEVELS):
                    cols = T if s <= 2 else NP
                    act.wait_ge(sig("dif"), i * len(LEVELS) + n + 1)
                    d = dif[:, (n + 1) % 2, 0:cols].rearrange("p (n c s) -> p n c s", c=2, s=s)
                    f = fac[:, (n + 1) % 2, 0:cols].rearrange("p (n c s) -> p n c s", c=2, s=s)
                    nc.scalar.activation(f[:, :, 0, :], d[:, :, 0, :], ACT.Exp, scale=-1.0)
                    nc.scalar.activation(f[:, :, 1, :], d[:, :, 1, :], ACT.Exp).then_inc(sig("fac"), 1)
                act.wait_ge(sig("kT"), i + 2)
                nc.scalar.activation(ktok, B[4][:, 0:256].rearrange("p (t d) -> p t d", t=2), ACT.Copy)
                nc.scalar.activation(ktokS[0:NS], B[4][0:NS, 256:384], ACT.Copy).then_inc(sig("ktok"), 1)
                act.wait_ge(sig("mid_ps"), i + 1)
                nc.scalar.activation(mid, B[5][:, 0:256], ACT.Copy).then_inc(sig("mid"), 1)
                act.wait_ge(sig("o_ps"), i + 2)
                for h in range(2):
                    nc.scalar.activation(o[:, h, :], B[h][:, 0:T], ACT.Copy)
                    ins = nc.scalar.activation(osq[:, h, :], B[h][:, 0:T], ACT.Square)
                ins.then_inc(sig("osq"), 1)
                act.wait_ge(sig("ss"), i + 1)
                nc.scalar.activation(lnv, B[2][:, 0:T], ACT.Ln, scale=1.0 / GLA_DV, bias=eps).then_inc(sig("ln"), 1)
                act.wait_ge(sig("ln"), i + 1)
                nc.scalar.activation(rs, lnv, ACT.Exp, scale=-0.5).then_inc(sig("rs"), 1)

        @block.vector
        def _(dve):
            dve.wait_ge(sig("z"), 1)
            nc.vector.tensor_scalar(la, z, 0.0, None, ALU.min).then_inc(sig("minz"), 1)
            dve.wait_ge(sig("minz"), 1)
            dve.wait_ge(sig("lnz"), 1)
            nc.vector.tensor_tensor(la, la, tmp1, ALU.subtract).then_inc(sig("ls"), 1)
            dve.wait_ge(sig("ls"), 1)
            nc.vector.tensor_scalar(la, la, 1.0 / 16.0, None, ALU.mult).then_inc(sig("la"), 1)
            dve.wait_ge(sig("la"), 1)
            for h in range(GLA_H):
                ins = nc.vector.tensor_tensor_scan(cum[:, h, :], cst("keep"), la[:, h, :], 0.0, ALU.mult, ALU.add)
            ins.then_inc(sig("cum"), 1)
            dve.wait_ge(sig("cum"), 1)
            grant(dve, sig("y"))
            with dve.Fori(0, GLA_H) as i:
                dve.wait_ge(sig("kT"), i + 1)
                c = cum[:, i, :]
                for a, n, m in ((0, 128, 2), (NP, NT, NB)):
                    cc = c[:, a:a + n * m].rearrange("p (m n) -> p m n", n=n)
                    ins = nc.vector.tensor_tensor(dend[:, a:a + n * m].rearrange("p (m n) -> p m n", n=n),
                                                  wide(cc[:, :, n - 1:n], n), cc, ALU.subtract)
                ins.then_inc(sig("dend"), 1)

                def distance(n, s):
                    cols = T if s <= 2 else NP
                    cc = c[:, 0:cols].rearrange("p (n c) -> p n c", c=2 * s)
                    nc.vector.tensor_tensor(dif[:, (n + 1) % 2, 0:cols].rearrange("p (n c) -> p n c", c=2 * s), cc,
                                            wide(cc[:, :, s - 1:s], 2 * s), ALU.subtract).then_inc(sig("dif"), 1)

                distance(0, LEVELS[0])
                dve.wait_ge(sig("o_ps"), i + 1)
                nc.vector.memset(att, 0.0)
                nc.vector.memset(attS[0:NS], 0.0).then_inc(sig("zero"), 1)
                dve.wait_ge(sig("staged"), i + 1)
                dve.wait_ge(sig("eb"), i + 1)
                nc.vector.tensor_tensor(kend, k, fend, ALU.mult).then_inc(sig("kend"), 1)
                nc.vector.tensor_tensor(qb, q, eb, ALU.mult).then_inc(sig("qb"), 1)

                def take(n, s):
                    dve.wait_ge(sig("scores"), i * 8 + n + 1)
                    dve.wait_ge(sig("att" if n else "zero"), i * 8 + n if n else i + 1)
                    mask = level_mask(s) if n else diag_mask
                    settle(dve)
                    if s <= 2:
                        nc.vector.copy_predicated(attS[0:NS], mask[0:NS, 0:NS], B[n % 2][0:NS, 256:288])
                    nc.vector.copy_predicated(att, rep(mask, 1, 2),
                                              B[n % 2][:, 0:256].rearrange("p (t q) -> p t q", t=2)).then_inc(sig("att"), 1)

                for n, s in enumerate(LEVELS):
                    if n + 1 < len(LEVELS):
                        if n >= 1:
                            dve.wait_ge(sig("fac"), i * len(LEVELS) + n)
                        distance(n + 1, LEVELS[n + 1])
                    dve.wait_ge(sig("fac"), i * len(LEVELS) + n + 1)
                    cols = T if s <= 2 else NP
                    b = (n + 1) % 2
                    if n >= 1:
                        take(n - 1, LEVELS[n - 2] if n >= 2 else 0)
                    nc.vector.tensor_tensor(ql[:, b, 0:cols], q[:, 0:cols], fac[:, b, 0:cols], ALU.mult)
                    nc.vector.tensor_tensor(kl[:, b, 0:cols], k[:, 0:cols], fac[:, b, 0:cols],
                                            ALU.mult).then_inc(sig("lev"), 1)
                take(6, LEVELS[5])
                take(7, LEVELS[6])
                dve.wait_ge(sig("ktok"), i + 1)
                nc.vector.tensor_tensor(kseq[0:NS], rep(ktokS[0:NS], 1, NB),
                                        wide(cst("inseq")[0:NS].unsqueeze(2), 128), ALU.mult).then_inc(sig("kseq"), 1)
                dve.wait_ge(sig("mid"), i + 1)
                dve.wait_ge(sig("fin_ps"), i + 1)
                dve.wait_ge(sig("stored"), i * 32 + 32)
                nc.vector.scalar_tensor_tensor(out=fin, in0=mid, scalar=eend[:, 1:2], in1=B[6][:, 0:256],
                                               op0=ALU.mult, op1=ALU.add).then_inc(sig("fin"), 1)
                dve.wait_ge(sig("stS_ps"), i + 1)
                for b in range(NB):
                    nc.vector.scalar_tensor_tensor(out=st[:, b, :], in0=st[:, b, :], scalar=eend[:, 2 + b:3 + b],
                                                   in1=B[4 + b // 2][:, 256 * (b % 2):256 * (b % 2) + 256],
                                                   op0=ALU.mult, op1=ALU.add).then_inc(sig("stS"), 1)
                dve.wait_ge(sig("rs"), i + 1)
                for h in range(2):
                    ins = nc.vector.scalar_tensor_tensor(out=o[:, h, :], in0=o[:, h, :],
                                                         scalar=vec[:, V_GNW + h:V_GNW + h + 1], in1=rs,
                                                         op0=ALU.mult, op1=ALU.mult)
                ins.then_inc(sig("on"), 1)
                dve.wait_ge(sig("on"), i + 1)
                nc.vector.tensor_tensor(y[:, bass.ds(i * 2, 2), :], o, proj[:, bass.ds(i * 2 + 16, 2), :],
                                        ALU.mult).then_inc(sig("y"), 1)

    def rwkv_project(nc, block, sig, layer):
        w = Work()
        ROW = 1 + NP + (NT + 1) * NB
        row, dif = w(2, ROW), w(2, ROW)
        shin, shout = w(RW_SLABS, NB), w(RW_SLABS, 1 + NB)

        @block.sync
        def _(sp):
            sp.dma_start(shin, s_shift[layer]).then_inc(sig("shift"), 16)
            with sp.Fori(1, 3) as g:
                load_group(sp, g + G_RW)
            load_group(sp, G_RW + 3)
            sp.wait_ge(sig("row"), RW_SLABS)
            sp.dma_start(shift_out[layer], shout).then_inc(sig("stored"), 16)
            sp.wait_ge(sig("stored"), 16)

        @block.tensor
        def _(pe):
            for s in range(NLORA):
                for k in range(KT):
                    mm = nc.tensor.matmul(bank[4 + s][:, 0:T], lora_w[:, k, 128 * s:128 * s + 128], hT[:, k, :],
                                          start=(k == 0), stop=(k == KT - 1))
                mm.then_inc(sig("lora_ps"), 1)
            with pe.Fori(0, 3) as g:
                for s in range(RING):
                    pe.wait_ge(slab_in[s], (g + G_RW + 1) * 16)
                    pe.wait_ge(sig("bank_free"), g * RING + s + 1)
                    slab_products(pe, s, bank[s % 4][:, 0:T], hT)

        @block.scalar
        def _(act):
            def fill(slab, n, ps, r):
                tail = row[:, r, 1 + NP:ROW].rearrange("p (b t) -> p b t", t=NT + 1)
                nc.scalar.activation(row[:, r, 1:1 + NP], ps[:, 0:NP], ACT.Copy)
                nc.scalar.activation(tail[:, :, 1:], ps[:, SAMPLE].rearrange("p (b t) -> p b t", t=NT), ACT.Copy)
                nc.scalar.activation(tail[:, :, 0:1], shin[:, slab, :].unsqueeze(2), ACT.Copy)
                nc.scalar.activation(shout[:, slab, 0:1], ps[:, NP - 1:NP], ACT.Copy)
                nc.scalar.activation(shout[:, slab, 1:1 + NB], ps[:, NP + NT - 1:T:NT], ACT.Copy)\
                    .then_inc(sig("row"), 1)

            act.wait_ge(sig("shift"), 16)
            act.wait_ge(sig("zero"), 1)
            for s in range(NLORA):
                act.wait_ge(sig("lora_ps"), s + 1)
                fill(24 + s, s, bank[4 + s], s)
            act.sem_inc(sig("bank_free"), 4)
            with act.Fori(0, 3) as g:
                for s in range(RING):
                    act.wait_ge(slab_done, (g + G_RW) * RING + s + 1)
                    act.wait_ge(sig("mixed"), g * RING + s + 1)
                    fill(g * RING + s, g * RING + s + 2, bank[s % 4], s % 2)
                    act.wait_ge(sig("row"), g * RING + s + 3)
                    act.sem_inc(sig("bank_free"), 1)

        @block.vector
        def _(dve):
            def mix(n, r, mu, out):
                dve.wait_ge(sig("row"), n + 1)
                nc.vector.tensor_tensor(dif[:, r, 0:ROW - 1], row[:, r, 0:ROW - 1], row[:, r, 1:ROW],
                                        ALU.subtract).then_inc(sig("dif"), 1)
                dve.wait_ge(sig("dif"), n + 1)
                nc.vector.scalar_tensor_tensor(out=out[:, 0:NP], in0=dif[:, r, 0:NP], scalar=mu,
                                               in1=row[:, r, 1:1 + NP], op0=ALU.mult, op1=ALU.add)
                tail = slice(1 + NP, ROW)
                nc.vector.scalar_tensor_tensor(
                    out=out[:, SAMPLE].rearrange("p (b t) -> p b t", t=NT),
                    in0=dif[:, r, tail].rearrange("p (b t) -> p b t", t=NT + 1)[:, :, 0:NT], scalar=mu,
                    in1=row[:, r, tail].rearrange("p (b t) -> p b t", t=NT + 1)[:, :, 1:],
                    op0=ALU.mult, op1=ALU.add).then_inc(sig("mixed"), 1)

            nc.vector.memset(row[:, :, 0:1], 0.0).then_inc(sig("zero"), 1)
            for s in range(NLORA):
                mix(s, s, vec[:, V_MU + 24 + s:V_MU + 25 + s], lora[:, s, :])
            with dve.Fori(0, 3) as g:
                for s in range(RING):
                    mix(g * RING + s + 2, s % 2, vec[:, bass.ds(g * RING + (V_MU + s), 1)], proj[:, g * RING + s, :])

    def rwkv(nc, block, sig, layer):
        w = Work()
        th, sg = w(T), w(T)
        wr = w(256)
        v = w(T)
        sw, a, g = w(T), w(T), w(T)
        early1, early2 = w(4 * T), w(4 * T)
        kk2, lnk, rsk, u1 = (early1[:, T * n:T * n + T] for n in range(4))
        dif, dex, e_in, e_out = (early2[:, T * n:T * n + T] for n in range(4))
        bseq, kseq = (x[:, 0:NB * 128].rearrange("p (b k) -> p b k", b=NB) for x in (early1, early2))
        kk, cum, e_ex = w(T), w(T), w(T)
        emid, eend, edec = w(2 + NB), w(2 + NB), w(2 + NB)
        dend = w(2 + NB)
        knew, kka = w(T), w(T)
        rt, at, bt, kt = w(T), w(T), w(T), w(T)
        bh, kh = w(T), w(T)
        rk = w(T)
        oneka = w(KT)
        tok, tokS = w(2, 3, 128), w(3, 128)
        AT, X, XT, W1 = w(4, 128), w(4, 128), w(4, 128), w(4, 128)
        ATs, Xs, XTs, W1s = w(2, 32), w(2, 32), w(2, 32), w(2, 32)
        Pk, Pb, Pr = w(4, 128), w(4, 128), w(4, 128)
        Pks, Pbs, Prs = w(2, 32), w(2, 32), w(2, 32)
        R, U = w(2, 64), w(2, 64)
        Rs, Us = w(2, 64), w(2, 64)
        mid, midm = w(64), w(64)
        st, s0T, s0m, stn = w(NB, 64), w(NB, 64), w(NB, 64), w(NB, 64)
        dg = w(1 + NB, 64)
        aseq = w(NB, NS)
        fin = w(64)
        o, mean, oc, osq, lnv, rs = w(T), w(T), w(T), w(T), w(T), w(T)
        B = bank

        GRANTED = {"y": 1, "g": 1, "s0T": 1, "var_ps": 1}

        def done(eng, name, i, n=1, of=1):
            eng.wait_ge(sig(name), i * of + n + GRANTED.get(name, 0))

        @block.sync
        def _(sp):
            grant(sp, sig("stored"), by=32)
            with sp.Fori(0, KT) as i:
                done(sp, "g", i, 0)
                sp.dma_start(wr, w_rank[layer, i]).then_inc(sig("wr"), 16)
                done(sp, "s0T", i, 0)
                sp.dma_start(st, s_rw[layer, i]).then_inc(sig("state"), 16)
                done(sp, "fin", i)
                sp.dma_start(rw_p[layer, i], fin).then_inc(sig("stored"), 16)
                done(sp, "stn", i)
                sp.dma_start(rw_s[layer, i], stn).then_inc(sig("stored"), 16)
            sp.wait_ge(sig("stored"), KT * 32 + 32)

        SA = B[7], B[3]

        def unit(h, t):
            return 2 * h + t

        def tile(t):
            return slice(128 * t, 128 * t + 128)

        @block.tensor
        def _(pe):
            grant(pe, sig("var_ps"))
            with pe.Fori(0, KT) as i:
                done(pe, "y", i, 0)
                pe.wait_ge(sig("wr"), (i + 1) * 16)
                done(pe, "th", 0)
                nc.tensor.matmul(B[0][:, 0:T], wr[0:64, 0:128], th[0:64, :], start=True, stop=True)
                nc.tensor.matmul(B[1][:, 0:T], wr[64:128, 0:128], th[64:128, :], start=True, stop=True)
                nc.tensor.matmul(B[2][:, 0:T], wr[:, 128:256], sg, start=True, stop=True).then_inc(sig("up"), 1)
                done(pe, "kk2", i)
                nc.tensor.matmul(B[3][:, 0:T], headones, kk2, start=True, stop=True).then_inc(sig("kk_ps"), 1)
                pe.wait_ge(sig("state"), (i + 1) * 16)
                settle(pe)
                for h in range(2):
                    for b in range(NB):
                        mm = nc.tensor.matmul(heads_of(B[4], h)[:, 64 * b:64 * b + 64], heads_of(st, h)[:, b, :],
                                              heads_of(eye64, h), start=True, stop=True)
                mm.then_inc(sig("s0_ps"), 1)
                done(pe, "ab", i)
                for h in range(2):
                    for t in range(2):
                        nc.tensor.matmul(B[5 + h][:, tile(t)], heads_of(bt, h)[:, tile(t)],
                                         heads_of(at, h)[:, tile(t)], start=True, stop=True)
                        nc.tensor.matmul(B[5 + h][:, NP + 128 * t:NP + 128 * t + 128], heads_of(at, h)[:, tile(t)],
                                         heads_of(bt, h)[:, tile(t)], start=True, stop=True)
                for h in range(2):
                    nc.tensor.matmul(SA[h][0:NS, 0:32], heads_of(bt, h)[:, SAMPLE], heads_of(at, h)[:, SAMPLE],
                                     start=True, stop=True)
                    mm = nc.tensor.matmul(SA[h][0:NS, 32:64], heads_of(at, h)[:, SAMPLE],
                                          heads_of(bt, h)[:, SAMPLE], start=True, stop=True)
                mm.then_inc(sig("A_ps"), 1)
                done(pe, "rkt", i)
                done(pe, "s0T", i)
                for h in range(2):
                    for n, (lhs, rhs) in enumerate(((kt, at), (bt, rt), (kt, rt))):
                        for t in range(2):
                            out = B[h][:, 256 * n:] if n < 2 else B[2 + 2 * h][:, :]
                            nc.tensor.matmul(out[:, tile(t)], heads_of(lhs, h)[:, tile(t)],
                                             heads_of(rhs, h)[:, tile(t)], start=True, stop=True)
                for h in range(2):
                    for n, (lhs, rhs) in enumerate(((kt, at), (bt, rt), (kt, rt))):
                        mm = nc.tensor.matmul(B[2 + 2 * h][0:NS, NP + 32 * n:NP + 32 * n + 32],
                                              heads_of(lhs, h)[:, SAMPLE], heads_of(rhs, h)[:, SAMPLE],
                                              start=True, stop=True)
                mm.then_inc(sig("P_ps"), 1)
                done(pe, "X0", i)
                settle(pe)
                for h in range(2):
                    mm = nc.tensor.matmul(B[7][0:NS, 32 * h:32 * h + 32], ATs[0:NS, h, :], Xs[0:NS, h, :],
                                          start=True, stop=True)
                mm.then_inc(sig("W1s_ps"), 1)
                done(pe, "W1s", i)
                settle(pe)
                for h in range(2):
                    nc.tensor.matmul(B[7][0:NS, 64 + 32 * h:96 + 32 * h], XTs[0:NS, h, :], W1s[0:NS, h, :],
                                     start=True, stop=True)
                    mm = nc.tensor.matmul(B[7][0:NS, 128 + 32 * h:160 + 32 * h], W1s[0:NS, h, :], XTs[0:NS, h, :],
                                          start=True, stop=True)
                mm.then_inc(sig("Xs_ps"), 1)
                nlev = len(LEVELS) - 1
                for n in range(nlev):
                    if n:
                        done(pe, "X", i, n, nlev)
                    for j in range(4):
                        mm = nc.tensor.matmul(B[3][:, 128 * j:128 * j + 128], AT[:, j, :], X[:, j, :],
                                              start=True, stop=True)
                    mm.then_inc(sig("W1_ps"), 1)
                    done(pe, "W1", i, n + 1, nlev)
                    for j in range(4):
                        if n < nlev - 1:
                            nc.tensor.matmul(B[5][:, 128 * j:128 * j + 128], XT[:, j, :], W1[:, j, :],
                                             start=True, stop=True)
                        mm = nc.tensor.matmul(B[6][:, 128 * j:128 * j + 128], W1[:, j, :], XT[:, j, :],
                                              start=True, stop=True)
                    mm.then_inc(sig("X_ps"), 1)
                done(pe, "P", i)
                done(pe, "hat", i)
                done(pe, "v", i)
                for n, src in enumerate((v, bh, kh)):
                    for t in range(2):
                        nc.tensor.transpose(B[t][:, 128 * n:128 * n + 128], src[:, tile(t)], ident)
                    mm = nc.tensor.transpose(B[2][0:NS, 128 * n:128 * n + 128], src[:, SAMPLE], ident)
                mm.then_inc(sig("tok_ps"), 1)
                done(pe, "tok", i)
                done(pe, "X", i, nlev, nlev)
                for h in range(2):
                    mm = nc.tensor.matmul(B[3 + 2 * h][:, 0:64], Pk[:, unit(h, 0), :],
                                          tok[:, 0, 0, 64 * h:64 * h + 64], start=True, stop=True)
                mm.then_inc(sig("R_ps"), 1)
                done(pe, "R", i, 1, 2)
                for h in range(2):
                    mm = nc.tensor.matmul(B[4][:, 64 * h:64 * h + 64], XT[:, unit(h, 0), :], R[:, h, :],
                                          start=True, stop=True)
                mm.then_inc(sig("U_ps"), 1)
                done(pe, "aseq", i)
                done(pe, "s0m", i)
                settle(pe)
                for h in range(2):
                    f = slice(64 * h, 64 * h + 64)
                    nc.tensor.matmul(B[h][0:NS, 0:64], Pks[0:NS, h, :], tokS[0:NS, 0, f], start=True, stop=False)
                    for b in range(NB):
                        mm = nc.tensor.matmul(B[h][0:NS, 0:64], heads_of(aseq, h)[:, b, :], heads_of(s0m, h)[:, b, :],
                                              start=False, stop=(b == NB - 1))
                mm.then_inc(sig("Rs_ps"), 1)
                done(pe, "U", i, 1, 2)
                for h in range(2):
                    f = slice(64 * h, 64 * h + 64)
                    o_h = heads_of(B[6], h)
                    nc.tensor.matmul(o_h[:, 0:128], U[:, h, :], Pb[:, unit(h, 0), :], start=True, stop=False)
                    nc.tensor.matmul(o_h[:, 0:128], tok[:, 0, 0, f], Pr[:, unit(h, 0), :], start=False, stop=True)
                    nc.tensor.matmul(heads_of(B[7], h)[:, 0:64], tok[:, 0, 1, f], U[:, h, :], start=True, stop=False)
                    mm = nc.tensor.matmul(heads_of(B[7], h)[:, 0:64], tok[:, 0, 2, f], tok[:, 0, 0, f],
                                          start=False, stop=True)
                mm.then_inc(sig("mid_ps"), 1)
                done(pe, "Rs", i)
                settle(pe)
                for h in range(2):
                    mm = nc.tensor.matmul(B[2][0:NS, 64 * h:64 * h + 64], XTs[0:NS, h, :], Rs[0:NS, h, :],
                                          start=True, stop=True)
                mm.then_inc(sig("Us_ps"), 1)
                done(pe, "mid", i)
                for h in range(2):
                    f = slice(64 * h, 64 * h + 64)
                    nc.tensor.matmul(B[3 + 2 * h][:, 0:64], Pk[:, unit(h, 1), :], tok[:, 1, 0, f], start=True,
                                     stop=False)
                    mm = nc.tensor.matmul(B[3 + 2 * h][:, 0:64], heads_of(at, h)[:, tile(1)], heads_of(midm, h),
                                          start=False, stop=True)
                mm.then_inc(sig("R_ps"), 1)
                done(pe, "R", i, 2, 2)
                for h in range(2):
                    mm = nc.tensor.matmul(B[4][:, 64 * h:64 * h + 64], XT[:, unit(h, 1), :], R[:, h, :],
                                          start=True, stop=True)
                mm.then_inc(sig("U_ps"), 1)
                done(pe, "U", i, 2, 2)
                done(pe, "Us", i)
                for h in range(2):
                    f = slice(64 * h, 64 * h + 64)
                    o_h = heads_of(B[6], h)
                    nc.tensor.matmul(o_h[:, tile(1)], U[:, h, :], Pb[:, unit(h, 1), :], start=True, stop=False)
                    nc.tensor.matmul(o_h[:, tile(1)], tok[:, 1, 0, f], Pr[:, unit(h, 1), :], start=False, stop=False)
                    nc.tensor.matmul(o_h[:, tile(1)], heads_of(midm, h), heads_of(rt, h)[:, tile(1)],
                                     start=False, stop=True)
                    nc.tensor.matmul(o_h[:, SAMPLE], Us[0:NS, h, :], Pbs[0:NS, h, :], start=True, stop=False)
                    nc.tensor.matmul(o_h[:, SAMPLE], tokS[0:NS, 0, f], Prs[0:NS, h, :], start=False, stop=False)
                    for b in range(NB):
                        c = slice(NP + NT * b, NP + NT * b + NT)
                        mm = nc.tensor.matmul(o_h[:, c], heads_of(s0m, h)[:, b, :], heads_of(rt, h)[:, c],
                                              start=False, stop=(b == NB - 1))
                mm.then_inc(sig("o_ps"), 1)
                done(pe, "dg", i)
                for h in range(2):
                    f = slice(64 * h, 64 * h + 64)
                    s_h = heads_of(B[7], h)[:, 0:64]
                    nc.tensor.matmul(s_h, U[:, h, :], tok[:, 1, 1, f], start=True, stop=False)
                    nc.tensor.matmul(s_h, tok[:, 1, 0, f], tok[:, 1, 2, f], start=False, stop=False)
                    mm = nc.tensor.matmul(s_h, heads_of(mid, h), heads_of(dg, h)[:, 0, :], start=False, stop=True)
                mm.then_inc(sig("fin_ps"), 1)
                done(pe, "seq", i)
                for h in range(2):
                    f = slice(64 * h, 64 * h + 64)
                    s_h = heads_of(B[5], h)
                    nc.tensor.matmul(s_h, Us[0:NS, h, :], bseq[0:NS, :, f], start=True, stop=False)
                    nc.tensor.matmul(s_h, tokS[0:NS, 0, f], kseq[0:NS, :, f], start=False, stop=False)
                    for b in range(NB):
                        mm = nc.tensor.matmul(s_h[:, 64 * b:64 * b + 64], heads_of(s0T, h)[:, b, :],
                                              heads_of(dg, h)[:, 1 + b, :], start=False, stop=(b == NB - 1))
                mm.then_inc(sig("stn_ps"), 1)
                done(pe, "o", i)
                nc.tensor.matmul(B[0][:, 0:T], headones, o, start=True, stop=True).then_inc(sig("mean_ps"), 1)
                done(pe, "osq", i)
                nc.tensor.matmul(B[1][:, 0:T], headones, osq, start=True, stop=True)
                nc.tensor.matmul(B[2][:, 0:T], headones, rk, start=True, stop=True).then_inc(sig("var_ps"), 1)

        @block.scalar
        def _(act):
            nc.scalar.activation(th[0:64], lora[0:64, 0, :], ACT.Tanh)
            nc.scalar.activation(th[64:128], lora[64:128, 0, :], ACT.Copy)
            nc.scalar.activation(sg, lora[:, 1, :], ACT.Sigmoid).then_inc(sig("th"), 1)
            grant(act, sig("g"), sig("s0T"))
            with act.Fori(0, KT) as i:
                done(act, "y", i, 0)
                nc.scalar.activation(v, proj[:, i + 16, :], ACT.Copy).then_inc(sig("v"), 1)
                done(act, "up", i)
                nc.scalar.activation(sw, B[0][:, 0:T], ACT.Sigmoid, bias=vec[:, bass.ds(i + V_W0, 1)])
                nc.scalar.activation(a, B[1][:, 0:T], ACT.Sigmoid, bias=vec[:, bass.ds(i + V_A0, 1)])\
                    .then_inc(sig("sw"), 1)
                nc.scalar.activation(g, B[2][:, 0:T], ACT.Copy).then_inc(sig("g"), 1)
                done(act, "kk_ps", i)
                nc.scalar.activation(lnk, B[3][:, 0:T], ACT.Ln, bias=tiny).then_inc(sig("lnk"), 1)
                done(act, "lnk", i)
                nc.scalar.activation(rsk, lnk, ACT.Exp, scale=-0.5).then_inc(sig("rsk"), 1)
                done(act, "dif", i)
                nc.scalar.activation(e_in, dif, ACT.Exp, scale=-KAPPA)
                nc.scalar.activation(e_out, dif, ACT.Exp, scale=KAPPA)
                nc.scalar.activation(e_ex, dex, ACT.Exp, scale=-KAPPA).then_inc(sig("e"), 1)
                nc.scalar.activation(emid[:, 0:2], cum[:, 63:256:128], ACT.Exp, scale=-KAPPA)
                nc.scalar.activation(emid[:, 2:], cum[:, NP + 1:T:NT], ACT.Exp, scale=-KAPPA)
                nc.scalar.activation(edec[:, 0:2], cum[:, 127:256:128], ACT.Exp, scale=-KAPPA)
                nc.scalar.activation(edec[:, 2:], cum[:, NP + NT - 1:T:NT], ACT.Exp, scale=-KAPPA)
                nc.scalar.activation(eend, dend, ACT.Exp, scale=-KAPPA).then_inc(sig("ec"), 1)
                done(act, "s0_ps", i)
                nc.scalar.activation(s0T, B[4][:, :].rearrange("p (b v) -> p b v", b=NB), ACT.Copy)\
                    .then_inc(sig("s0T"), 1)
                done(act, "A_ps", i)
                for h in range(2):
                    nc.scalar.activation(AT[:, 2 * h:2 * h + 2, :], B[5 + h][:, 0:NP].rearrange("p (t s) -> p t s", t=2),
                                         ACT.Copy)
                    ins = nc.scalar.activation(ATs[0:NS, h, :], SA[h][0:NS, 0:32], ACT.Copy)
                ins.then_inc(sig("AT"), 1)
                done(act, "W1s_ps", i)
                nc.scalar.activation(W1s[0:NS], B[7][0:NS, 0:64].rearrange("p (u s) -> p u s", u=2), ACT.Copy)\
                    .then_inc(sig("W1s"), 1)
                nlev = len(LEVELS) - 1
                for n in range(nlev):
                    done(act, "W1_ps", i, n + 1, nlev)
                    nc.scalar.activation(W1, B[3][:, :].rearrange("p (u s) -> p u s", u=4), ACT.Copy)\
                        .then_inc(sig("W1"), 1)
                done(act, "tok_ps", i)
                for t in range(2):
                    nc.scalar.activation(tok[:, t], B[t][:, 0:384].rearrange("p (n d) -> p n d", n=3), ACT.Copy)
                nc.scalar.activation(tokS[0:NS], B[2][0:NS, 0:384].rearrange("p (n d) -> p n d", n=3), ACT.Copy)\
                    .then_inc(sig("tok"), 1)
                for t in range(2):
                    done(act, "R_ps", i, t + 1, 2)
                    nc.scalar.activation(R[:, 0, :], B[3][:, 0:64], ACT.Copy)
                    nc.scalar.activation(R[:, 1, :], B[5][:, 0:64], ACT.Copy).then_inc(sig("R"), 1)
                    done(act, "U_ps", i, t + 1, 2)
                    nc.scalar.activation(U, B[4][:, 0:128].rearrange("p (h v) -> p h v", h=2), ACT.Copy)\
                        .then_inc(sig("U"), 1)
                    if t == 0:
                        done(act, "Rs_ps", i)
                        nc.scalar.activation(Rs[0:NS, 0, :], B[0][0:NS, 0:64], ACT.Copy)
                        nc.scalar.activation(Rs[0:NS, 1, :], B[1][0:NS, 0:64], ACT.Copy).then_inc(sig("Rs"), 1)
                        done(act, "Us_ps", i)
                        nc.scalar.activation(Us[0:NS], B[2][0:NS, 0:128].rearrange("p (h v) -> p h v", h=2),
                                             ACT.Copy).then_inc(sig("Us"), 1)
                done(act, "o_ps", i)
                nc.scalar.activation(o, B[6][:, 0:T], ACT.Copy).then_inc(sig("o"), 1)
                done(act, "oc", i)
                nc.scalar.activation(osq, oc, ACT.Square).then_inc(sig("osq"), 1)
                done(act, "var_ps", i)
                nc.scalar.activation(lnv, B[1][:, 0:T], ACT.Ln, scale=1.0 / RW_HD, bias=gn_eps).then_inc(sig("lnv"), 1)
                done(act, "lnv", i)
                nc.scalar.activation(rs, lnv, ACT.Exp, scale=-0.5).then_inc(sig("rs"), 1)

        @block.vector
        def _(dve):
            tt, stt = nc.vector.tensor_tensor, nc.vector.scalar_tensor_tensor
            nc.vector.tensor_scalar(oneka, vec[:, V_KA:V_KA + KT], -1.0, 1.0, ALU.mult, ALU.add)\
                .then_inc(sig("oneka"), 1)
            dve.wait_ge(sig("oneka"), 1)
            grant(dve, sig("y"))
            with dve.Fori(0, KT) as i:
                def then(ins, name):
                    ins.then_inc(sig(name), 1)
                    done(dve, name, i)

                k_i, r_i = proj[:, i + 8, :], proj[:, i, :]
                done(dve, "var_ps", i, 0)
                then(nc.vector.tensor_scalar(kk, k_i, vec[:, bass.ds(i + V_KKS, 1)], None, ALU.mult), "kk")
                tt(kk2, kk, kk, ALU.mult).then_inc(sig("kk2"), 1)
                done(dve, "sw", i)
                tt_scan = nc.vector.tensor_tensor_scan(cum, cst("keep"), sw, 0.0, ALU.mult, ALU.add)
                then(tt_scan, "cum")
                then(nc.vector.tensor_scalar(u1, a, vec[:, bass.ds(i + V_KA, 1)], oneka[:, bass.ds(i, 1)],
                                             ALU.mult, ALU.add), "u1")
                tt(knew, k_i, u1, ALU.mult)
                for o0, n, m, c0, c1 in ((0, 128, 2, 63, 0), (NP, NT, NB, 1, 2)):
                    cc = cum[:, o0:o0 + n * m].rearrange("p (m n) -> p m n", n=n)
                    tt(dif[:, o0:o0 + n * m].rearrange("p (m n) -> p m n", n=n), cc, wide(cc[:, :, c0:c0 + 1], n),
                       ALU.subtract)
                    ins = tt(dend[:, c1:c1 + m].unsqueeze(2), cc[:, :, n - 1:n], cc[:, :, c0:c0 + 1], ALU.subtract)
                then(ins, "dif0")
                tt(dex, dif, sw, ALU.subtract).then_inc(sig("dif"), 1)
                then(stt(out=rk, in0=knew, scalar=vec[:, bass.ds(i + V_RK, 1)], in1=r_i, op0=ALU.mult,
                         op1=ALU.mult), "rk")
                done(dve, "rsk", i)
                then(tt(kk, kk, rsk, ALU.mult), "kkn")
                then(tt(kka, kk, a, ALU.mult), "kka")
                done(dve, "e", i)
                stt(out=at, in0=kk, scalar=-1.0, in1=e_ex, op0=ALU.mult, op1=ALU.mult)
                then(tt(bt, kka, e_out, ALU.mult), "ab")
                tt(kt, knew, e_out, ALU.mult)
                then(tt(rt, r_i, e_in, ALU.mult), "rkt")
                done(dve, "ec", i)
                for src, dst in ((bt, bh), (kt, kh)):
                    for o0, n, m, c1 in ((0, 128, 2, 0), (NP, NT, NB, 2)):
                        ins = tt(dst[:, o0:o0 + n * m].rearrange("p (m n) -> p m n", n=n),
                                 src[:, o0:o0 + n * m].rearrange("p (m n) -> p m n", n=n),
                                 wide(eend[:, c1:c1 + m].unsqueeze(2), n), ALU.mult)
                ins.then_inc(sig("hat"), 1)
                done(dve, "A_ps", i)
                nc.vector.tensor_copy(X, rep(ident, 1, 4))
                nc.vector.tensor_copy(XT, rep(ident, 1, 4))
                nc.vector.tensor_copy(Xs[0:NS], rep(ident[0:NS, 0:NS], 1, 2))
                then(nc.vector.tensor_copy(XTs[0:NS], rep(ident[0:NS, 0:NS], 1, 2)), "eye")
                done(dve, "AT", i)
                settle(dve)
                u4 = lambda bk: bk[:, :].rearrange("p (u s) -> p u s", u=4)
                u2 = lambda ap: ap.rearrange("p (t s) -> p t s", t=2)
                for h in range(2):
                    hh = slice(2 * h, 2 * h + 2)
                    nc.vector.copy_predicated(X[:, hh, :], rep(level_mask(1, True), 1, 2), u2(B[5 + h][:, NP:512]))
                    nc.vector.copy_predicated(XT[:, hh, :], rep(level_mask(1), 1, 2), u2(B[5 + h][:, 0:NP]))
                    nc.vector.copy_predicated(Xs[0:NS, h, :], level_mask(1, True)[0:NS, 0:NS], SA[h][0:NS, 32:64])
                    ins = nc.vector.copy_predicated(XTs[0:NS, h, :], level_mask(1)[0:NS, 0:NS], SA[h][0:NS, 0:32])
                then(ins, "X0")
                done(dve, "P_ps", i)
                for h in range(2):
                    hh = slice(2 * h, 2 * h + 2)
                    small = B[2 + 2 * h]
                    for n, (dst, dstS, m) in enumerate(((Pk, Pks, "strict"), (Pb, Pbs, "causal"), (Pr, Prs, "causal"))):
                        src = B[h][:, 256 * n:256 * n + 256] if n < 2 else small[:, 0:256]
                        tt(dst[:, hh, :], u2(src), rep(cst(m), 1, 2), ALU.mult)
                        ins = tt(dstS[0:NS, h, :], small[0:NS, NP + 32 * n:NP + 32 * n + 32], cst(m + "S")[0:NS],
                                 ALU.mult)
                ins.then_inc(sig("P"), 1)
                done(dve, "Xs_ps", i)
                settle(dve)
                nc.vector.copy_predicated(XTs[0:NS], rep(level_mask(2)[0:NS, 0:NS], 1, 2), u2(B[7][0:NS, 128:192]))\
                    .then_inc(sig("XTs"), 1)
                done(dve, "s0T", i)
                tt(s0m, s0T, wide(emid[:, 2:].unsqueeze(2), 64), ALU.mult).then_inc(sig("s0m"), 1)
                tt(aseq, rep(at[:, SAMPLE], 1, NB), cst("seqcols").rearrange("p (b t) -> p b t", b=NB), ALU.mult)\
                    .then_inc(sig("aseq"), 1)
                tt(dg[:, 0, :], eye64, wide(edec[:, 1:2], 64), ALU.mult)
                tt(dg[:, 1:, :], rep(eye64, 1, NB), wide(edec[:, 2:].unsqueeze(2), 64), ALU.mult)\
                    .then_inc(sig("dg"), 1)
                nlev = len(LEVELS) - 1
                for n in range(nlev):
                    done(dve, "X_ps", i, n + 1, nlev)
                    s = LEVELS[n + 1]
                    settle(dve)
                    if n < nlev - 1:
                        nc.vector.copy_predicated(X, rep(level_mask(s, True), 1, 4), u4(B[5]))
                    nc.vector.copy_predicated(XT, rep(level_mask(s), 1, 4), u4(B[6])).then_inc(sig("X"), 1)
                done(dve, "tok", i)
                for n, dst in ((1, bseq), (2, kseq)):
                    ins = tt(dst[0:NS], rep(tokS[0:NS, n, :], 1, NB), wide(cst("inseq")[0:NS].unsqueeze(2), 128),
                             ALU.mult)
                ins.then_inc(sig("seq"), 1)
                done(dve, "mid_ps", i)
                tt(midm, B[7][:, 0:64], wide(emid[:, 1:2], 64), ALU.mult)
                nc.vector.tensor_copy(mid, B[7][:, 0:64]).then_inc(sig("mid"), 1)
                done(dve, "fin_ps", i)
                dve.wait_ge(sig("stored"), i * 32 + 32)
                nc.vector.tensor_copy(fin, B[7][:, 0:64]).then_inc(sig("fin"), 1)
                done(dve, "stn_ps", i)
                nc.vector.tensor_copy(stn, B[5][:, :].rearrange("p (b k) -> p b k", b=NB)).then_inc(sig("stn"), 1)
                done(dve, "mean_ps", i)
                done(dve, "o", i)
                then(stt(out=oc, in0=B[0][:, 0:T], scalar=-1.0 / RW_HD, in1=o, op0=ALU.mult, op1=ALU.add), "oc")
                done(dve, "rs", i)
                then(tt(mean, B[2][:, 0:T], v, ALU.mult), "bonus")
                then(stt(out=oc, in0=oc, scalar=vec[:, bass.ds(i + V_LNW, 1)], in1=rs, op0=ALU.mult,
                         op1=ALU.mult), "yn")
                then(stt(out=oc, in0=oc, scalar=vec[:, bass.ds(i + V_LNB, 1)], in1=mean, op0=ALU.add,
                         op1=ALU.add), "yb")
                tt(y[:, i, :], oc, g, ALU.mult).then_inc(sig("y"), 1)

    with nc.Fori(0, DEPTH) as layer:
        with nc.cleanup_on_exit():
            slab_in = [nc.alloc_semaphore(name=f"slab_in{s}") for s in range(RING)]
            slab_done = nc.alloc_semaphore(name="slab_done")

            def load_group(sp, group):
                for s in range(RING):
                    if not isinstance(group, int) or group > 0:
                        sp.wait_ge(slab_done, (group - 1) * RING + s + 1)
                    sp.dma_start(ring[:, s], w_mix[layer, group * RING + s]).then_inc(slab_in[s], 16)

            def load_ff_slab(sp, e, j, s, before, n=KT):
                sp.wait_ge(slab_done, before)
                sp.dma_start(ring[:, s, 0:n], w_ff[e, j, :, 0:n]).then_inc(slab_in[s], 16)

            def slab_products(pe, s, out, rhs, n=KT, k0=0, last=KT):
                for k in range(n):
                    mm = nc.tensor.matmul(out, ring[:, s, k, :], rhs[:, k0 + k, :],
                                          start=(k0 + k == 0), stop=(k0 + k == last - 1))
                mm.then_inc(slab_done, 1)

            with phase(nc, "norm") as (block, sig):
                @block.sync
                def _(sp):
                    sp.dma_start(vec[:, :], vec_in[layer]).then_inc(sig("vec"), 16)
                    sp.dma_start(lora_w[:, :, :], w_lora[layer]).then_inc(sig("small"), 16)
                    sp.dma_start(gkup[:, :], w_gkup[layer]).then_inc(sig("small"), 16)
                    load_group(sp, 0)
                    sp.wait_ge(sig("small"), 32)

                rms(block, sig, vec[:, V_MIX:V_MIX + KT], hT, bank[7], Work())

            def project(name, first):
                with phase(nc, name) as (block, sig):
                    @block.sync
                    def _(sp):
                        with sp.Fori(1, 3) as g:
                            load_group(sp, g + first)
                        load_group(sp, first + 3)

                    @block.tensor
                    def _(pe):
                        with pe.Fori(0, 3) as g:
                            for s in range(RING):
                                pe.wait_ge(slab_in[s], (g + first + 1) * 16)
                                pe.wait_ge(sig("bank_free"), g * RING + s + 1)
                                slab_products(pe, s, bank[s % 4][:, 0:T], hT)

                    @block.scalar
                    def _(act):
                        act.sem_inc(sig("bank_free"), 4)
                        with act.Fori(0, 2) as g:
                            for s in range(RING):
                                act.wait_ge(slab_done, (g + first) * RING + s + 1)
                                nc.scalar.activation(proj[:, g * RING + s, :], bank[s % 4][:, 0:T],
                                                     ACT.Copy).then_inc(sig("bank_free"), 1)
                        for s in range(RING):
                            act.wait_ge(slab_done, (first + 2) * RING + s + 1)
                            nc.scalar.activation(proj[:, 2 * RING + s, :], bank[s % 4][:, 0:T],
                                                 ACT.Silu).then_inc(sig("bank_free"), 1)

            def merge(name, first, fresh):
                with phase(nc, name) as (block, sig):
                    w = Work()
                    gate, part = w(2, T), w(2, T)

                    @block.sync
                    def _(sp):
                        with sp.Fori(1, 2) as g:
                            load_group(sp, g + first)
                        load_group(sp, first + 2)

                    @block.tensor
                    def _(pe):
                        with pe.Fori(0, 2) as g:
                            for s in range(RING):
                                pe.wait_ge(slab_in[s], (g + first + 1) * 16)
                                pe.wait_ge(sig("gate_free" if s % 2 == 0 else "branch_free"),
                                           g * 4 + s // 2 + 1)
                                slab_products(pe, s, bank[s % 4][:, 0:T], y if s % 2 else hT)

                    @block.scalar
                    def _(act):
                        act.sem_inc(sig("gate_free"), 2)
                        with act.Fori(0, 2) as g:
                            for s in range(0, RING, 2):
                                act.wait_ge(slab_done, (g + first) * RING + s + 1)
                                act.wait_ge(sig("gate_used"), g * 4 + s // 2 + 1)
                                nc.scalar.activation(gate[:, s // 2 % 2, :], bank[s % 4][:, 0:T],
                                                     ACT.Sigmoid).then_inc(sig("gate_free"), 1)

                    @block.vector
                    def _(dve):
                        dve.sem_inc(sig("branch_free"), 2)
                        dve.sem_inc(sig("gate_used"), 2)
                        with dve.Fori(0, 2) as g:
                            for s in range(1, RING, 2):
                                m, b = g * 4 + s // 2, s // 2 % 2
                                dve.wait_ge(slab_done, (g + first) * RING + s + 1)
                                dve.wait_ge(sig("gate_free"), m + 3)
                                out = merged[:, m, :] if fresh else part[:, b, :]
                                nc.vector.tensor_tensor(out, bank[s % 4][:, 0:T], gate[:, b, :],
                                                        ALU.mult).then_inc(sig("branch_free"), 1)
                                dve.wait_ge(sig("branch_free"), m + 3)
                                if fresh:
                                    dve.sem_inc(sig("gate_used"), 1)
                                else:
                                    nc.vector.tensor_tensor(merged[:, m, :], merged[:, m, :], part[:, b, :],
                                                            ALU.add).then_inc(sig("gate_used"), 1)

            project("ret_in", G_RET)
            with phase(nc, "ret") as (block, sig):
                retention(nc, block, sig, layer)
            merge("ret_out", G_RET_OUT, True)
            project("gla_in", G_GLA)
            with phase(nc, "gla") as (block, sig):
                gated_linear(nc, block, sig, layer)
            merge("gla_out", G_GLA_OUT, False)
            with phase(nc, "rw_in") as (block, sig):
                rwkv_project(nc, block, sig, layer)
            with phase(nc, "rw") as (block, sig):
                rwkv(nc, block, sig, layer)
            merge("rw_out", G_RW_OUT, False)

            with phase(nc, "out") as (block, sig):
                @block.tensor
                def _(pe):
                    for s in range(RING):
                        pe.wait_ge(slab_in[s], (G_OUT + 1) * 16)
                        if s >= 4:
                            pe.wait_ge(sig("added"), s - 3)
                        slab_products(pe, s, bank[s % 4][:, 0:T], merged)

                @block.vector
                def _(dve):
                    for s in range(RING):
                        dve.wait_ge(slab_done, G_OUT * RING + s + 1)
                        nc.vector.tensor_tensor(xT[:, s, :], xT[:, s, :], bank[s % 4][:, 0:T],
                                                ALU.add).then_inc(sig("added"), 1)

            with phase(nc, "norm2") as (block, sig):
                @block.sync
                def _(sp):
                    sp.dma_start(vec[:, :], vec_in[layer]).then_inc(sig("vec"), 16)
                    sp.wait_ge(sig("vec"), 16)

                rms(block, sig, vec[:, V_FFN:V_FFN + KT], hT, bank[7], Work())

            TILES = ((0, 128), (128, 128), (256, 32))
            with phase(nc, "route") as (block, sig):
                w = Work()
                htok, slot, gate2 = w(3, D), w(2, 3), w(2, 3)
                lg, best = w(3, NE), w(3, NE)
                pick = w(3, NE).bitcast(U32)
                idx, hot, member, pos = w(3, NE), w(2, 3, NE), w(3, NE), w(3, NE)
                ex, den = w(3, 1), w(3, 1)
                count, npass, more, end, first = w(NE), w(NE), w(NE), w(NE), w(NE)
                before, ctlf = w(MAXP, NE), w(MAXP + 1)
                flag = cst("flag")
                is_moe, is_dense = flag[:, bass.ds(layer, 1)], flag[:, bass.ds(layer + 2, 1)]

                @block.tensor
                def _(pe):
                    for i, (a, n) in enumerate(TILES):
                        for k in range(KT):
                            mm = nc.tensor.matmul(bank[0][0:n, NE * i:NE * i + NE], hT[:, k, a:a + n],
                                                  router[:, k, :], start=(k == 0), stop=(k == KT - 1))
                    mm.then_inc(sig("logits"), 1)
                    for i, (a, n) in enumerate(TILES):
                        for k in range(KT):
                            mm = nc.tensor.transpose(bank[2 + 2 * i + k // 4][0:n, 128 * (k % 4):128 * (k % 4) + 128],
                                                     hT[:, k, a:a + n], ident)
                        mm.then_inc(sig("htok_ps"), 1)
                    pe.wait_ge(sig("member"), 1)
                    for i in range(3):
                        for j in range(i + 1):
                            nc.tensor.matmul(bank[1][:, NE * i:NE * i + NE], ones if j < i else cst("strict"),
                                             member[:, j, :], start=(j == 0), stop=(j == i))
                    for j in range(3):
                        mm = nc.tensor.matmul(bank[1][:, 3 * NE:4 * NE], ones, member[:, j, :],
                                              start=(j == 0), stop=(j == 2))
                    mm.then_inc(sig("rank"), 1)

                @block.scalar
                def _(act):
                    for i, (a, n) in enumerate(TILES):
                        act.wait_ge(sig("htok_ps"), i + 1)
                        for b in range(2):
                            ins = nc.scalar.activation(htok[0:n, i, 512 * b:512 * b + 512],
                                                       bank[2 + 2 * i + b][0:n, :], ACT.Copy)
                    ins.then_inc(sig("htok"), 1)
                    act.wait_ge(sig("dif"), 1)
                    nc.scalar.activation(ex, ex, ACT.Exp).then_inc(sig("exp"), 1)
                    act.wait_ge(sig("htok"), 1)

                @block.vector
                def _(dve):
                    tt, ts, stt = nc.vector.tensor_tensor, nc.vector.tensor_scalar, nc.vector.scalar_tensor_tensor

                    def then(ins, name):
                        ins.then_inc(sig(name), 1)
                        dve.wait_ge(sig(name), 1)

                    nc.vector.memset(htok[32:64, 2, :], 0.0)
                    nc.vector.memset(htok[64:128, 2, :], 0.0)
                    then(nc.vector.memset(lg, 0.0), "lg0")
                    dve.wait_ge(sig("logits"), 1)
                    for i, (a, n) in enumerate(TILES):
                        ins = nc.vector.tensor_copy(lg[0:n, i, :], bank[0][0:n, NE * i:NE * i + NE])
                    then(ins, "lg")
                    for i in range(3):
                        ins = nc.vector.max(best[:, i, :], lg[:, i, :])
                    then(ins, "best")
                    for i in range(3):
                        ins = nc.vector.max_index(pick[:, i, :], best[:, i, :], lg[:, i, :])
                    tt(ex, best[:, :, 1:2], best[:, :, 0:1], ALU.subtract).then_inc(sig("dif"), 1)
                    dve.wait_ge(sig("dif"), 1)
                    then(nc.vector.tensor_copy(idx, pick), "idx")
                    for i in range(3):
                        for c in range(2):
                            ins = ts(hot[:, c, i, :], cst("iota8"), idx[:, i, c:c + 1], cst("valid")[:, i:i + 1],
                                     ALU.is_equal, ALU.mult)
                    then(ins, "hot")
                    tt(member, hot[:, 0], hot[:, 1], ALU.add).then_inc(sig("member"), 1)
                    dve.wait_ge(sig("exp"), 1)
                    then(ts(den, ex, 1.0, None, ALU.add), "den")
                    then(nc.vector.reciprocal(gate2[:, 0, :], den[:, :, 0]), "p1")
                    then(tt(gate2[:, 1, :], gate2[:, 0, :], ex[:, :, 0], ALU.mult), "p2")
                    ts(gate2[:, 0, :], gate2[:, 0, :], is_moe, is_dense, ALU.mult, ALU.add)
                    ts(gate2[:, 1, :], gate2[:, 1, :], is_moe, None, ALU.mult).then_inc(sig("gates"), 1)
                    dve.wait_ge(sig("rank"), 1)
                    nc.vector.tensor_copy(pos, bank[1][:, 0:3 * NE].rearrange("p (i e) -> p i e", i=3))
                    then(nc.vector.tensor_copy(count, bank[1][:, 3 * NE:4 * NE]), "count")
                    then(ts(npass, count, 0.0, None, ALU.is_gt), "n0")
                    for c in range(1, T // CAP):
                        then(ts(more, count, float(CAP * c), None, ALU.is_gt), f"more{c}")
                        then(tt(npass, npass, more, ALU.add), f"n{c}")
                    then(nc.vector.tensor_tensor_scan(end, cst("ones")[:, 0:NE], npass, 0.0, ALU.mult, ALU.add), "end")
                    then(tt(first, end, npass, ALU.subtract), "first")
                    then(stt(out=pos, in0=rep(first, 1, 3), scalar=float(CAP), in1=pos, op0=ALU.mult, op1=ALU.add),
                         "pos")
                    for c in range(2):
                        then(tt(hot[:, c], hot[:, c], pos, ALU.mult), f"hotpos{c}")
                        then(nc.vector.tensor_reduce(slot[:, c, :], hot[:, c], mybir.AxisListType.X, ALU.add),
                             f"slot{c}")
                        then(ts(slot[:, c, :], slot[:, c, :], is_moe, None, ALU.mult), f"slotm{c}")
                        then(stt(out=slot[:, c, :], in0=cst("place")[:, 3 * c:3 * c + 3], scalar=is_dense,
                                 in1=slot[:, c, :], op0=ALU.mult, op1=ALU.add), f"slotd{c}")
                        then(tt(slot[:, c, :], slot[:, c, :], cst("nowhere"), ALU.add), f"slotv{c}")
                    then(tt(before, rep(end, 1, MAXP), wide(cst("passno").unsqueeze(2), NE), ALU.is_le), "before")
                    then(nc.vector.tensor_reduce(ctlf[:, 0:MAXP], before, mybir.AxisListType.X, ALU.add), "experts")
                    then(ts(ctlf[:, 0:MAXP], ctlf[:, 0:MAXP], 1.0, is_moe, ALU.add, ALU.mult), "experts1")
                    then(ts(ctlf[:, 0:MAXP], ctlf[:, 0:MAXP], float(NE), None, ALU.min), "experts2")
                    then(ts(ctlf[:, MAXP:], end[:, NE - 1:], is_moe, None, ALU.mult), "passes")
                    then(stt(out=ctlf[:, MAXP:], in0=cst("dense_passes"), scalar=is_dense, in1=ctlf[:, MAXP:],
                             op0=ALU.mult, op1=ALU.add), "passes1")
                    then(nc.vector.tensor_copy(ctl[:, :], ctlf), "ctl")

            with phase(nc, "ff") as (block, sig):
                w = Work()
                htok, slot, gate2 = w(3, D), w(2, 3), w(2, 3)
                pick = w(2, 2, 3, CAP)
                gather, gated = w(3, CAP), w(3, CAP)
                scatter = w(T)
                hg, hid = w(KT, CAP), w(FT, CAP)
                act1, oT, otok = w(2, CAP), w(2, CAP), w(2, 128)
                UPG = UP_SLABS // RING

                def passes(eng):
                    return eng.value_load(ctl[0:1, MAXP:MAXP + 1], min_val=1, max_val=MAXP)

                @block.sync
                def _(sp):
                    with sp.Fori(0, passes(sp)) as p:
                        e = sp.value_load(ctl[0:1, bass.ds(p, 1)], min_val=0, max_val=NE)
                        base = p * FF_SLABS + MIX_SLABS
                        for s in range(RING):
                            load_ff_slab(sp, e, s, s, base + s + 1 - (4 if s < 4 else 8))
                        with sp.Fori(1, UPG + 1) as g:
                            for s in range(RING):
                                load_ff_slab(sp, e, g * RING + s, s, base + (g - 1) * RING + s + 1)
                        for j in range((UPG + 1) * RING, FF_SLABS):
                            load_ff_slab(sp, e, j, j % RING, base + j - RING + 1,
                                         6 if (j - UP_SLABS) % 3 == 2 else KT)

                @block.tensor
                def _(pe):
                    grant(pe, sig("sc_ps"), by=2)
                    with pe.Fori(0, passes(pe)) as p:
                        pe.wait_ge(sig("picked"), p + 1)
                        pe.wait_ge(sig("added"), p * KT + 1)
                        pe.wait_ge(sig("otok"), p * KT + 1)
                        for k in range(KT):
                            for i in range(3):
                                mm = nc.tensor.matmul(bank[6 + k // 4][:, CAP * (k % 4):CAP * (k % 4) + CAP],
                                                      htok[:, i, 128 * k:128 * k + 128], gather[:, i, :],
                                                      start=(i == 0), stop=(i == 2))
                        mm.then_inc(sig("hg_ps"), 1)
                        pe.wait_ge(sig("oT"), p * KT + 2)
                        for i, (a, n) in enumerate(TILES):
                            mm = nc.tensor.transpose(bank[5][0:CAP, a:a + n], gated[0:n, i, :], ident[0:n, 0:n])
                        mm.then_inc(sig("scatter_ps"), 1)
                        pe.wait_ge(sig("hg"), p + 1)
                        settle(pe)

                        def arrived(s, g):
                            pe.wait_ge(slab_in[s], (p * (9 if s < 4 else 8) + (G_FF + 1) + g) * 16)

                        def up(g, s):
                            arrived(s, g)
                            pe.wait_ge(sig("w1_free" if s % 2 == 0 else "w3_free"), p * FT + g * 4 + s // 2 + 1)
                            slab_products(pe, s, bank[s % 4][:, 0:CAP], hg)

                        with pe.Fori(0, UPG) as g:
                            for s in range(RING):
                                up(g, s)
                        for s in range(UP_SLABS % RING):
                            up(UPG, s)
                        pe.wait_ge(sig("w3_free"), p * FT + FT + 2)
                        for m in range(KT + 2):
                            if m < KT:
                                pe.wait_ge(sig("oT"), p * KT + m + 1)
                                for c in range(3):
                                    j = UP_SLABS + 3 * m + c
                                    arrived(j % RING, j // RING)
                                    slab_products(pe, j % RING, bank[4 + m % 2][:, 0:CAP], hid,
                                                  n=6 if c == 2 else KT, k0=KT * c, last=FT)
                            if 1 <= m <= KT:
                                pe.wait_ge(sig("oT"), p * KT + m + 2)
                                pe.wait_ge(sig("otok"), p * KT + m)
                                nc.tensor.transpose(bank[6][0:CAP, 0:128], oT[:, (m - 1) % 2, :],
                                                    ident).then_inc(sig("otok_ps"), 1)
                            if m >= 2:
                                pe.wait_ge(sig("scatter"), p + 1)
                                pe.wait_ge(sig("otok"), p * KT + m)
                                pe.wait_ge(sig("added"), p * KT + m - 1)
                                nc.tensor.matmul(bank[7][:, 0:T], otok[0:CAP, m % 2, :], scatter[0:CAP, :],
                                                 start=True, stop=True).then_inc(sig("sc_ps"), 1)

                @block.scalar
                def _(act):
                    grant(act, sig("w1_free"), sig("oT"), by=2)
                    grant(act, sig("otok"))
                    with act.Fori(0, passes(act)) as p:
                        act.wait_ge(sig("hg_ps"), p + 1)
                        for b in range(2):
                            ins = nc.scalar.activation(hg[:, 4 * b:4 * b + 4, :],
                                                       bank[6 + b][:, 0:4 * CAP].rearrange("p (k c) -> p k c", k=4),
                                                       ACT.Copy)
                        ins.then_inc(sig("hg"), 1)
                        act.wait_ge(sig("scatter_ps"), p + 1)
                        nc.scalar.activation(scatter[0:CAP, :], bank[5][0:CAP, 0:T], ACT.Copy)\
                            .then_inc(sig("scatter"), 1)

                        def silu(g, s):
                            act.wait_ge(slab_done, p * FF_SLABS + MIX_SLABS + g * RING + s + 1)
                            act.wait_ge(sig("w3_free"), p * FT + g * 4 + s // 2 + 1)
                            nc.scalar.activation(act1[:, s // 2 % 2, :], bank[s % 4][:, 0:CAP],
                                                 ACT.Silu).then_inc(sig("w1_free"), 1)

                        with act.Fori(0, UPG) as g:
                            for s in range(0, RING, 2):
                                silu(g, s)
                        for s in range(0, UP_SLABS % RING, 2):
                            silu(UPG, s)
                        for m in range(KT + 1):
                            if m < KT:
                                act.wait_ge(slab_done, p * FF_SLABS + (MIX_SLABS + UP_SLABS) + 3 * m + 3)
                                nc.scalar.activation(oT[:, m % 2, :], bank[4 + m % 2][:, 0:CAP],
                                                     ACT.Copy).then_inc(sig("oT"), 1)
                            if m >= 1:
                                act.wait_ge(sig("otok_ps"), p * KT + m)
                                act.wait_ge(sig("sc_ps"), p * KT + m)
                                nc.scalar.activation(otok[0:CAP, (m - 1) % 2, :], bank[6][0:CAP, 0:128],
                                                     ACT.Copy).then_inc(sig("otok"), 1)

                @block.vector
                def _(dve):
                    def choose(n):
                        for c in range(2):
                            for i in range(3):
                                nc.vector.tensor_scalar(pick[:, c, 0, i, :], cst("column"), slot[:, c, i:i + 1], None,
                                                        ALU.is_equal)
                                ins = nc.vector.tensor_scalar(pick[:, c, 1, i, :], cst("column"),
                                                              slot[:, c, i:i + 1], gate2[:, c, i:i + 1],
                                                              ALU.is_equal, ALU.mult)
                        ins.then_inc(sig("pick"), 1)
                        dve.wait_ge(sig("pick"), n)
                        nc.vector.tensor_tensor(gather, pick[:, 0, 0], pick[:, 1, 0], ALU.add)
                        nc.vector.tensor_tensor(gated, pick[:, 0, 1], pick[:, 1, 1], ALU.add)
                        nc.vector.tensor_scalar(slot, slot, float(-CAP), None, ALU.add).then_inc(sig("picked"), 1)

                    grant(dve, sig("w3_free"), by=2)
                    grant(dve, sig("added"))
                    choose(1)
                    with dve.Fori(0, passes(dve)) as p:
                        dve.wait_ge(sig("scatter_ps"), p + 1)
                        dve.wait_ge(sig("picked"), p + 1)
                        choose(p + 2)

                        def product(g, s):
                            f = g * 4 + s // 2
                            dve.wait_ge(slab_done, p * FF_SLABS + MIX_SLABS + g * RING + s + 1)
                            dve.wait_ge(sig("w1_free"), p * FT + f + 3)
                            nc.vector.tensor_tensor(hid[:, f, :], bank[s % 4][:, 0:CAP], act1[:, s // 2 % 2, :],
                                                    ALU.mult).then_inc(sig("w3_free"), 1)

                        dve.wait_ge(slab_done, p * FF_SLABS + MIX_SLABS)
                        settle(dve)
                        with dve.Fori(0, UPG) as g:
                            for s in range(1, RING, 2):
                                product(g, s)
                        for s in range(1, UP_SLABS % RING, 2):
                            product(UPG, s)
                        for m in range(KT):
                            dve.wait_ge(sig("sc_ps"), p * KT + m + 3)
                            nc.vector.tensor_tensor(xT[:, m, :], xT[:, m, :], bank[7][:, 0:T],
                                                    ALU.add).then_inc(sig("added"), 1)

    with phase(nc, "final") as (block, sig):
        @block.gpsimd
        def _(pool):
            nc.gpsimd.sem_inc(sig("vec"), 16)

        rms(block, sig, vecf, hT, bank[7], Work())

        @block.sync
        def _(sp):
            sp.wait_ge(sig("normed"), 1)
            sp.dma_start(yT_out, hT[:, :, :]).then_inc(sig("stored"), 16)
            sp.wait_ge(sig("stored"), 16)


def kernel(**inputs):
    import concourse.bacc as bacc
    from concourse.bass_utils import run_bass_kernel_spmd

    a = {k: np.asarray(v) for k, v in inputs.items()}

    def feat(v):
        return np.swapaxes(v.reshape(v.shape[:-1] + (-1, 128)), -1, -2)

    def slabs(w):
        k, n = w.shape
        return w.reshape(k // 128, 128, n // 128, 128).transpose(2, 1, 0, 3)

    o1, o2 = 3072, 3072 + 3088
    o3 = o2 + RW_COLS
    rwp = np.concatenate([np.arange(0, 1024), np.arange(1088, 2112), np.arange(2112, 3136), np.arange(1024, 1088),
                          np.arange(3136, 3200), np.arange(3200, 3328)])
    w_mix = np.empty((DEPTH, MIX_SLABS, 128, KT, 128), np.float32)
    w_lora = np.empty((DEPTH, 128, KT, 272), np.float32)
    w_rank = np.empty((DEPTH, KT, 128, 256), np.float32)
    for l in range(DEPTH):
        w = a["w_in"][l]
        parts = [w[:, 0:o1], w[:, o1:o1 + 3072], w[:, o2:o3][:, rwp]]
        at = 0
        for br in range(3):
            w_mix[l, at:at + 24] = slabs(parts[br][:, 0:3072])
            at += 24
            w_mix[l, at:at + 16:2] = slabs(w[:, o3 + 1024 * br:o3 + 1024 * (br + 1)])
            w_mix[l, at + 1:at + 16:2] = slabs(a["w_branch"][l, br])
            at += 16
        w_mix[l, at:at + 8] = slabs(a["w_out"][l])
        low = np.concatenate([parts[2][:, 3072:], w[:, o1 + 3072:o2]], 1)
        w_lora[l] = low.reshape(KT, 128, 272).transpose(1, 0, 2)
        w_rank[l, :, 0:64, 0:128] = a["rwkv_w_up"][l].reshape(64, KT, 128).transpose(1, 0, 2)
        w_rank[l, :, 64:128, 0:128] = a["rwkv_a_up"][l].reshape(64, KT, 128).transpose(1, 0, 2)
        w_rank[l, :, :, 128:256] = a["rwkv_g_up"][l].reshape(128, KT, 128).transpose(1, 0, 2)
    w_ff = np.zeros((NFF, FF_SLABS, 128, KT, 128), np.float32)
    w1 = np.concatenate([a["ffn_w1"], a["moe_w1"][0]])
    w3 = np.concatenate([a["ffn_w3"], a["moe_w3"][0]])
    w2 = np.concatenate([a["ffn_w2"], a["moe_w2"][0]])
    for e in range(NFF):
        w_ff[e, 0:UP_SLABS:2] = slabs(w1[e])
        w_ff[e, 1:UP_SLABS:2] = slabs(w3[e])
        s2 = slabs(w2[e])
        for c in range(3):
            n = 6 if c == 2 else 8
            w_ff[e, UP_SLABS + c::3, :, 0:n] = s2[:, :, 8 * c:8 * c + n]
    vec = np.concatenate([feat(a[k]) for k in ("norm_mix", "norm_ffn", "gla_gk_bias", "gla_norm_w")]
                         + [feat(a["rwkv_mu"][:, rwp])]
                         + [feat(a[k].reshape(DEPTH, -1)) for k in ("rwkv_w0", "rwkv_a0", "rwkv_kk_scale", "rwkv_ka",
                                                                    "rwkv_rk", "rwkv_ln_w", "rwkv_ln_b")], -1)
    toks = np.concatenate([a["x_prompt"][0], a["x_sample"].reshape(NS, D)])
    arrays = {
        "xT": toks.T.reshape(KT, 128, T).transpose(1, 0, 2),
        "w_mix": w_mix, "w_lora": w_lora, "w_rank": w_rank, "w_gkup": a["gla_gk_up"], "vec": vec,
        "vecf": feat(a["norm_final"]), "router": a["moe_router"][0].reshape(KT, 128, NE).transpose(1, 0, 2),
        "w_ff": w_ff,
        "s_ret": a["state_ret"].reshape(DEPTH, NB, 4, 128, RET_DV).transpose(0, 2, 3, 1, 4),
        "s_gla": a["state_gla"].transpose(0, 2, 3, 1, 4),
        "s_rw": a["state_rwkv"].reshape(DEPTH, NB, KT, 128, RW_HD).transpose(0, 2, 3, 1, 4),
        "s_shift": feat(a["state_shift"][:, :, rwp]).transpose(0, 2, 3, 1),
        "table": TABLE, "masks": MASKS,
    }
    nc = bacc.Bacc("TRN2", target_bir_lowering=False, num_devices=1)
    args = []
    arrays = {k + "_dram": np.ascontiguousarray(v) for k, v in arrays.items()}
    for k, v in arrays.items():
        args.append(nc.dram_tensor(k, v.shape, mybir.dt.from_np(v.dtype), kind="ExternalInput").ap())
    outs = {"yT": (128, KT, T), "ret_p": (DEPTH, 4, 128, RET_DV), "ret_s": (DEPTH, 4, 128, NB, RET_DV),
            "gla_p": (DEPTH, GLA_H, 128, GLA_DV), "gla_s": (DEPTH, GLA_H, 128, NB, GLA_DV),
            "rw_p": (DEPTH, KT, 128, RW_HD), "rw_s": (DEPTH, KT, 128, NB, RW_HD),
            "shift": (DEPTH, 128, RW_SLABS, 1 + NB)}
    for k, shape in outs.items():
        args.append(nc.dram_tensor(k + "_out", shape, F32, kind="ExternalOutput").ap())
    build(nc, *args)
    r = run_bass_kernel_spmd(nc, [arrays], core_ids=[0]).results[0]
    r = {k: np.asarray(r[k + "_out"]) for k in outs}
    yt = r["yT"].transpose(1, 0, 2).reshape(D, T).T
    shift = np.empty((DEPTH, 1 + NB, RW_COLS), np.float32)
    shift[:, :, rwp] = r["shift"].transpose(0, 3, 2, 1).reshape(DEPTH, 1 + NB, RW_COLS)
    return (yt[:NP].reshape(1, NP, D), yt[NP:].reshape(NB, NT, D),
            r["ret_p"].reshape(DEPTH, 1, RET_H, RET_DK, RET_DV),
            r["gla_p"].reshape(DEPTH, 1, GLA_H, GLA_DK, GLA_DV),
            r["rw_p"].reshape(DEPTH, 1, RW_H, RW_HD, RW_HD), shift[:, 0:1],
            r["ret_s"].transpose(0, 3, 1, 2, 4).reshape(DEPTH, NB, RET_H, RET_DK, RET_DV),
            r["gla_s"].transpose(0, 3, 1, 2, 4),
            r["rw_s"].transpose(0, 3, 1, 2, 4).reshape(DEPTH, NB, RW_H, RW_HD, RW_HD), shift[:, 1:])
```

```python
from contextlib import ExitStack, contextmanager

import numpy as np

import concourse.bass as bass
from concourse import mybir

F32 = mybir.dt.float32
U32 = mybir.dt.uint32
U8 = mybir.dt.uint8
ALU = mybir.AluOpType
ACT = mybir.ActivationFunctionType

D = 1024
DEPTH = 2
NP = 256
NB, NT = 8, 4
NS = NB * NT
T = NP + NS
TILE = 128
PAST = 2048
KT = D // 128
RET_H, RET_DK, RET_DV = 8, 64, 128
GLA_H, GLA_DK, GLA_DV, GLA_RANK = 4, 128, 256, 16
RW_H, RW_HD = 16, 64
RW_COLS = 3328
NLORA = 2
RW_SLABS = RW_COLS // 128
FF = 2816
FT = FF // 128
NE = 8
CAP = 96
MAXP = NE + 2 * T // CAP
NFF = NE + 1
EPS = 1e-6
GN_EPS = 64e-5
KAPPA = float(np.exp(-0.5))

RING = 8
S_RET, S_GLA, S_RW, S_SIDE, S_RW_OUT, S_OUT = range(6)
STREAM = ((3, 8), (GLA_H, 6), (GLA_H, 6), (KT, 4), (2, 8), (1, 8))
BASE = tuple(sum(g * n for g, n in STREAM[:p]) for p in range(len(STREAM) + 1))
MIX_SLABS = BASE[-1]


def slabs_of_head(i):
    return i, i + 4, i * 2 + 8, i * 2 + 9, i * 2 + 16, i * 2 + 17


def fills(p, place):
    return sum(g for g, n in STREAM[:p] if place < n)


UP_SLABS = 2 * FT
DOWN_SLABS = 24
FF_SLABS = UP_SLABS + DOWN_SLABS

V_MIX, V_FFN, V_GKB, V_GNW, V_MU, V_W0, V_A0, V_KKS, V_KA, V_RK, V_LNW, V_LNB, NV = (
    0, 8, 16, 20, 22, 48, 56, 64, 72, 80, 88, 96, 104)

LEVELS = (1, 2, 4, 8, 16, 32, 64)


def constants():
    c = {}
    p = np.arange(128)
    eye = np.eye(128)
    c["ident"] = eye
    c["ones"] = np.ones((128, 128))
    c["headones"] = (p[:, None] // 64 == p[None, :] // 64) * 1.0
    c["swap"] = (p[:, None] == (p[None, :] ^ 32)) * 1.0
    c["eye64"] = (p[:, None] % 64 == np.arange(64)[None, :]) * 1.0
    pos = np.concatenate([np.arange(NP), np.tile(PAST + np.arange(NT), NB)]).astype(np.float32)
    inv = (np.float32(10000.0) ** (-np.arange(32, dtype=np.float32) / np.float32(32))).astype(np.float32)
    ang = (pos[:, None] * inv[None, :]).astype(np.float32)
    cos, sin = np.cos(ang.astype(np.float64)).T, np.sin(ang.astype(np.float64)).T
    cosp = cos[p % 32]
    sinp = sin[p % 32] * np.where(p % 64 < 32, -1.0, 1.0)[:, None]
    c["qcos"], c["qsin"] = cosp, sinp
    c["kcos"], c["ksin"] = cosp * RET_DK ** -0.5, sinp * RET_DK ** -0.5
    lg = np.log1p(-np.exp2(-5.0 - np.arange(RET_H)))
    i = np.arange(128)
    dif = i[None, :] - i[:, None]
    dm = np.where(dif >= 0, np.exp(lg[:, None, None] * np.maximum(dif, 0)), 0.0)
    c["dmP"] = dm.transpose(1, 0, 2).reshape(128, -1)
    same = (i[:32, None] // NT == i[None, :32] // NT)
    dms = np.zeros((128, RET_H, 32))
    dms[:32] = (dm[:, :32, :32] * same).transpose(1, 0, 2)
    c["dmS"] = dms.reshape(128, -1)
    n = np.concatenate([np.arange(128), np.tile(np.arange(NT), NB)])
    hp = 2 * np.arange(4)[None, :] + (p // 64)[:, None]
    c["qdec"] = np.exp(lg[hp][:, :, None] * (n + 1.0)).reshape(128, -1)
    c["kdecP"] = np.exp(lg[None, :] * (127.0 - i)[:, None])
    c["kdecS"] = np.exp(lg[None, :] * (NT - 1.0 - i % NT)[:, None])
    c["cdec"] = np.stack([np.exp(lg[hp] * 128), np.exp(lg[hp] * NT)], -1).reshape(128, -1)
    c["strict"] = (i[:, None] < i[None, :]) * 1.0
    c["causal"] = (i[:, None] <= i[None, :]) * 1.0
    c["strictS"] = np.zeros((128, 32)); c["strictS"][:32] = c["strict"][:32, :32] * same
    c["causalS"] = np.zeros((128, 32)); c["causalS"][:32] = c["causal"][:32, :32] * same
    keep = np.ones(T); keep[[0, 128]] = 0; keep[NP::NT] = 0
    c["keep"] = np.tile(keep, (128, 1))
    c["inseq"] = np.zeros((128, NB)); c["inseq"][:32] = (i[:32, None] // NT == np.arange(NB)[None, :])
    c["seqcols"] = np.tile((np.arange(NB)[:, None] == np.arange(32)[None, :] // NT).reshape(-1), (128, 1))
    c["valid"] = np.stack([np.ones(128), np.ones(128), p < NS], 1)
    c["nowhere"] = (c["valid"] - 1) * 1e6
    c["column"] = np.tile(np.arange(float(CAP)), (128, 1))
    c["passno"] = np.tile(np.arange(float(MAXP)), (128, 1))
    c["iota8"] = np.tile(np.arange(8.0), (128, 1))
    c["eps"] = np.tile(np.array([EPS, 1e-12, GN_EPS, 0.0]), (128, 1))
    off, at = 0, {}
    for k, v in c.items():
        at[k] = (off, v.shape[1])
        off += v.shape[1]
    table = np.concatenate([v.astype(np.float32) for v in c.values()], 1)
    m = []
    for s in LEVELS:
        blk = i // (2 * s)
        lo, hi = i % (2 * s) < s, i % (2 * s) >= s
        m.append((blk[:, None] == blk[None, :]) & lo[:, None] & hi[None, :])
    m += [x.T for x in m]
    m.append(eye > 0)
    return table, at, np.concatenate(m, 1).astype(np.uint32)


TABLE, TABLE_AT, MASKS = constants()


class Signals:

    def __init__(self, nc, phase):
        self.nc, self.phase, self.sems = nc, phase, {}

    def __call__(self, name):
        if name not in self.sems:
            self.sems[name] = self.nc.alloc_semaphore(name=f"{self.phase}_{name}")
        return self.sems[name]


@contextmanager
def phase(nc, name):
    with nc.cleanup_on_exit():
        sig = Signals(nc, name)
        with nc.Block() as block:
            yield block, sig


def rep(ap, axis, n):
    shape = list(ap.shape)
    return ap.unsqueeze(axis).to_broadcast(shape[:axis] + [n] + shape[axis:])


def wide(ap, n):
    return ap.to_broadcast(list(ap.shape[:-1]) + [n])


def build(nc, xT_in, w_mix, w_lora, w_rank, w_gkup, vec_in, vecf_in, router_in, w_ff, s_ret, s_gla, s_rw,
          s_shift, table_in, masks_in, yT_out, ret_p, ret_s, gla_p, gla_s, rw_p, rw_s, shift_out):
    def sb(name, shape, dt=F32):
        return nc.alloc_sbuf_tensor(name, shape, dt)

    xT = sb("xT", [128, KT, T])
    hT = sb("hT", [128, KT, T])
    merged = sb("merged", [128, KT, T])
    proj = sb("proj", [128, 24, T])
    y_ret = sb("y_ret", [128, KT, T])
    y_gla = sb("y_gla", [128, KT, T])
    y_rw = proj[:, 0:KT, :]
    ring = sb("ring", [128, RING, KT, 128])
    lora_w = sb("lora_w", [128, KT, 272])
    gkup = sb("gkup", [16, 512])
    vec = sb("vec", [128, NV])
    vecf = sb("vecf", [128, KT])
    router = sb("router", [128, KT, NE])
    ctl = sb("ctl", [128, MAXP + 1], U32)
    table = sb("table", [128, TABLE.shape[1]])
    masks = sb("masks", [128, MASKS.shape[1]], U8)
    lora = sb("lora", [128, NLORA, T])
    work = sb("work", [128, 17440])
    bank = [nc.alloc_psum_tensor(f"bank{i}", [128, 512], F32) for i in range(8)]

    def cst(name):
        o, n = TABLE_AT[name]
        return table[:, o:o + n]

    ident, ones, headones, eye64 = cst("ident"), cst("ones"), cst("headones"), cst("eye64")
    eps, tiny, gn_eps = (cst("eps")[:, i:i + 1] for i in range(3))

    def level_mask(s, later_rows=False):
        i = LEVELS.index(s) + (len(LEVELS) if later_rows else 0)
        return masks[:, 128 * i:128 * i + 128]

    diag_mask = masks[:, 128 * 2 * len(LEVELS):128 * (2 * len(LEVELS) + 1)]

    def settle(eng):
        eng.sem_inc(settled, 1)

    def grant(eng, *sems, by=1):
        for sem in sems:
            eng.sem_inc(sem, by)

    class Work:

        def __init__(self):
            self.at = 0

        def __call__(self, *dims):
            n = int(np.prod(dims))
            assert self.at + n <= work.shape[1], (self.at, n)
            ap = work[:, self.at:self.at + n]
            self.at += n
            if len(dims) == 1:
                return ap
            names = [f"d{i}" for i in range(len(dims))]
            return ap.rearrange(f"p ({' '.join(names)}) -> p {' '.join(names)}", **dict(zip(names, dims)))

    class Between:

        def __init__(self, slabs):
            self.products = self.emit(slabs)

        def emit(self, slabs):
            for wait, s, out, rhs in slabs:
                wait()
                for k in range(KT):
                    mm = nc.tensor.matmul(out, ring[:, s, k, :], rhs[:, k, :], start=(k == 0), stop=(k == KT - 1))
                    if k == KT - 1:
                        mm.then_inc(slab_done, 1)
                    yield

        def __call__(self, n):
            for _ in range(n):
                next(self.products, None)

    settled = nc.alloc_semaphore(name="settled")

    with phase(nc, "start") as (block, sig):
        masks32 = work[:, 0:MASKS.shape[1]].bitcast(U32)

        @block.sync
        def _(sp):
            sp.dma_start(table[:, :], table_in).then_inc(sig("loaded"), 16)
            sp.dma_start(masks32, masks_in).then_inc(sig("masks"), 16)
            sp.dma_start(xT[:, :, :], xT_in).then_inc(sig("loaded"), 16)
            sp.dma_start(vecf[:, :], vecf_in).then_inc(sig("loaded"), 16)
            sp.dma_start(router[:, :, :], router_in).then_inc(sig("loaded"), 16)
            sp.wait_ge(sig("loaded"), 4 * 16)

        @block.vector
        def _(dve):
            dve.wait_ge(sig("masks"), 16)
            nc.vector.tensor_copy(masks[:, :], masks32).then_inc(sig("narrowed"), 1)
            dve.wait_ge(sig("narrowed"), 1)

    def rms(block, sig, gain, out, psum, w):
        sq = w(KT, T)
        root, rs = w(T), w(T)

        @block.scalar
        def _(act):
            nc.scalar.activation(sq, xT[:, :, :], ACT.Square).then_inc(sig("squares"), 1)
            act.wait_ge(sig("sum"), 1)
            nc.scalar.activation(root, psum[:, 0:T], ACT.Sqrt, scale=1.0 / D, bias=eps).then_inc(sig("root"), 1)

        @block.tensor
        def _(pe):
            pe.wait_ge(sig("squares"), 1)
            for k in range(KT):
                mm = nc.tensor.matmul(psum[:, 0:T], ones, sq[:, k, :], start=(k == 0), stop=(k == KT - 1))
            mm.then_inc(sig("sum"), 1)

        @block.vector
        def _(dve):
            dve.wait_ge(sig("root"), 1)
            nc.vector.reciprocal(rs, root).then_inc(sig("rs"), 1)
            dve.wait_ge(sig("rs"), 1)
            dve.wait_ge(sig("vec"), 16)
            for k in range(KT):
                last = nc.vector.scalar_tensor_tensor(out=out[:, k, :], in0=xT[:, k, :], scalar=gain[:, k:k + 1],
                                                      in1=rs, op0=ALU.mult, op1=ALU.mult)
            last.then_inc(sig("normed"), 1)

    SAMPLE = slice(NP, T)

    def heads_of(ap, hh):
        return ap[64 * hh:64 * hh + 64]

    def retention(nc, block, sig, layer):
        w = Work()
        c1, c2, qr, kr = w(2, T), w(2, T), w(T), w(T)
        qd = w(128 + NS)
        vst = w(2, T)
        vtok, vtokS = w(2, 2, 128), w(2, 128)
        ktok, ktokS = w(2, 2, 64), w(2, 64)
        kseq = w(NB, 128)
        att, attS = w(2, 2, 128), w(2, 32)
        mid, fin = w(RET_DV), w(RET_DV)
        st = w(NB, RET_DV)
        o, osq, lnv, rs = w(2, T), w(2, T), w(2, T), w(2, T)
        dmP = cst("dmP").rearrange("p (h i) -> p h i", h=RET_H)
        dmS = cst("dmS").rearrange("p (h i) -> p h i", h=RET_H)
        qdec = cst("qdec").rearrange("p (h i) -> p h i", h=4)
        cdec = cst("cdec").rearrange("p (h i) -> p h i", h=4)
        gate = w(2, T)
        B = bank
        PAIRS = RET_H // 2

        @block.sync
        def _(sp):
            def pair(i, load_next):
                sp.wait_ge(sig("stored"), i * 32 + 32)
                sp.dma_start(st, s_ret[layer, i]).then_inc(sig("state"), 16)
                sp.wait_ge(sig("fin"), i + 1)
                sp.dma_start(ret_p[layer, i], fin).then_inc(sig("stored"), 16)
                sp.wait_ge(sig("stS"), i * 2 + 2)
                sp.dma_start(ret_s[layer, i], st).then_inc(sig("stored"), 16)
                load_next()

            grant(sp, sig("stored"), by=32)
            with sp.Fori(0, PAIRS - 1) as i:
                pair(i, lambda: load_group(sp, S_GLA, i + 1))
            pair(PAIRS - 1, lambda: load_first_group(sp, S_RW))
            sp.wait_ge(sig("stored"), PAIRS * 32 + 32)

        @block.tensor
        def _(pe):
            with pe.Fori(0, PAIRS) as i:
                gla = Between([(lambda j=j: (pe.wait_ge(sig("evac"), i * 6 + j + 1), slab_arrived(pe, S_GLA, i, j)),
                                j, B[6 + j % 2][:, 0:T], hT) for j in range(6)])
                pe.wait_ge(sig("y"), i + 1)
                nc.tensor.matmul(B[0][:, 0:T], cst("swap"), proj[:, i, :], start=True, stop=True)
                nc.tensor.matmul(B[1][:, 0:T], cst("swap"), proj[:, i + 4, :], start=True,
                                 stop=True).then_inc(sig("swapped"), 1)
                gla(KT)
                pe.wait_ge(sig("vst"), i + 1)
                for t in range(2):
                    for h in range(2):
                        nc.tensor.transpose(B[2][:, 256 * t + 128 * h:][:, 0:128], vst[:, h, 128 * t:128 * t + 128], ident)
                for h in range(2):
                    mm = nc.tensor.transpose(B[3][0:NS, 128 * h:128 * h + 128], vst[:, h, SAMPLE], ident)
                mm.then_inc(sig("vT"), 1)
                gla(KT)
                pe.wait_ge(sig("rot"), i + 1)
                for t in range(2):
                    nc.tensor.transpose(B[4][:, 128 * t:128 * t + 128], kr[:, 128 * t:128 * t + 128], ident)
                nc.tensor.transpose(B[4][0:NS, 256:384], kr[:, SAMPLE], ident).then_inc(sig("kT"), 1)
                for h in range(2):
                    for t in range(2):
                        c = slice(128 * t, 128 * t + 128)
                        nc.tensor.matmul(B[h][:, c], heads_of(kr, h)[:, c],
                                         heads_of(qr, h)[:, c], start=True, stop=True)
                for h in range(2):
                    mm = nc.tensor.matmul(B[h][0:NS, SAMPLE], heads_of(kr, h)[:, SAMPLE],
                                          heads_of(qr, h)[:, SAMPLE], start=True, stop=True)
                mm.then_inc(sig("scores"), 1)
                gla(KT)
                pe.wait_ge(sig("ktok"), i + 1)
                pe.wait_ge(sig("vtok"), i + 1)
                for h in range(2):
                    mm = nc.tensor.matmul(heads_of(B[5], h)[:, 0:128], ktok[:, 0, h, :], vtok[:, 0, h, :],
                                          start=True, stop=True)
                mm.then_inc(sig("mid_ps"), 1)
                pe.wait_ge(sig("att"), i + 1)
                pe.wait_ge(sig("qd"), i + 1)
                pe.wait_ge(sig("state"), (i + 1) * 16)
                pe.wait_ge(sig("mid"), i + 1)
                for h in range(2):
                    ob = B[h]
                    nc.tensor.matmul(ob[:, 0:128], vtok[:, 0, h, :], att[:, h, 0, :], start=True, stop=True)
                    nc.tensor.matmul(ob[:, SAMPLE], vtokS[0:NS, h, :], attS[0:NS, h, :], start=True, stop=False)
                    for b in range(NB):
                        nc.tensor.matmul(ob[:, NP + NT * b:NP + NT * b + NT], heads_of(st, h)[:, b, :],
                                         heads_of(qd, h)[:, 128 + NT * b:128 + NT * b + NT], start=False,
                                         stop=(b == NB - 1))
                        gla(b % 2)
                    nc.tensor.matmul(ob[:, 128:256], vtok[:, 1, h, :], att[:, h, 1, :], start=True, stop=False)
                    mm = nc.tensor.matmul(ob[:, 128:256], heads_of(mid, h), heads_of(qd, h)[:, 0:128],
                                          start=False, stop=True)
                mm.then_inc(sig("o_ps"), 1)
                for h in range(2):
                    mm = nc.tensor.matmul(heads_of(B[5], h)[:, 0:128], ktok[:, 1, h, :], vtok[:, 1, h, :],
                                          start=True, stop=True)
                mm.then_inc(sig("fin_ps"), 1)
                pe.wait_ge(sig("kseq"), i + 1)
                for b in range(NB):
                    for h in range(2):
                        mm = nc.tensor.matmul(heads_of(B[3 + b // 4], h)[:, 128 * (b % 4):128 * (b % 4) + 128],
                                              kseq[0:NS, b, 64 * h:64 * h + 64], vtokS[0:NS, h, :],
                                              start=True, stop=True)
                mm.then_inc(sig("stS_ps"), 1)
                gla(KT)
                pe.wait_ge(sig("osq"), i + 1)
                pe.wait_ge(sig("fin"), i + 1)
                for h in range(2):
                    mm = nc.tensor.matmul(B[2 + 3 * h][:, 0:T], ones, osq[:, h, :], start=True, stop=True)
                mm.then_inc(sig("ss"), 1)
                gla(KT)

        @block.scalar
        def _(act):
            grant(act, sig("evac"), by=2)
            with act.Fori(0, PAIRS) as i:
                def evacuate(j):
                    act.wait_ge(slab_done, i * 6 + (BASE[S_GLA] + j + 1))
                    settle(act)
                    nc.scalar.activation(proj[:, slabs_of_head(i)[j], :], B[6 + j % 2][:, 0:T],
                                         ACT.Copy).then_inc(sig("evac"), 1)

                act.wait_ge(sig("y"), i + 1)
                nc.scalar.activation(vst, proj[:, bass.ds(i * 2 + 8, 2), :], ACT.Copy).then_inc(sig("vst"), 1)
                nc.scalar.activation(gate, proj[:, bass.ds(i * 2 + 16, 2), :], ACT.Copy).then_inc(sig("gate"), 1)
                act.wait_ge(sig("cs"), i + 1)
                evacuate(0)
                act.wait_ge(sig("vT"), i + 1)
                nc.scalar.activation(vtok, B[2][:, :].rearrange("p (t h d) -> p t h d", t=2, h=2), ACT.Copy)
                nc.scalar.activation(vtokS[0:NS], B[3][0:NS, 0:256].rearrange("p (h d) -> p h d", h=2),
                                     ACT.Copy).then_inc(sig("vtok"), 1)
                evacuate(1)
                act.wait_ge(sig("mid_ps"), i + 1)
                nc.scalar.activation(mid, B[5][:, 0:128], ACT.Copy).then_inc(sig("mid"), 1)
                evacuate(2)
                act.wait_ge(sig("o_ps"), i + 1)
                for h in range(2):
                    nc.scalar.activation(o[:, h, :], B[h][:, 0:T], ACT.Copy)
                    ins = nc.scalar.activation(osq[:, h, :], B[h][:, 0:T], ACT.Square)
                ins.then_inc(sig("osq"), 1)
                evacuate(3)
                act.wait_ge(sig("ss"), i + 1)
                for h in range(2):
                    ins = nc.scalar.activation(lnv[:, h, :], B[2 + 3 * h][:, 0:T], ACT.Ln, scale=1.0 / RET_DV, bias=eps)
                ins.then_inc(sig("ln"), 1)
                act.wait_ge(sig("ln"), i + 1)
                nc.scalar.activation(rs, lnv, ACT.Exp, scale=-0.5).then_inc(sig("rs"), 1)
                evacuate(4)
                evacuate(5)

        @block.vector
        def _(dve):
            grant(dve, sig("y"))
            with dve.Fori(0, PAIRS) as i:
                dve.wait_ge(sig("swapped"), i + 1)
                nc.vector.tensor_tensor(c1[:, 0, :], proj[:, i, :], cst("qcos"), ALU.mult)
                nc.vector.tensor_tensor(c1[:, 1, :], proj[:, i + 4, :], cst("kcos"), ALU.mult)
                nc.vector.tensor_tensor(c2[:, 0, :], B[0][:, 0:T], cst("qsin"), ALU.mult)
                nc.vector.tensor_tensor(c2[:, 1, :], B[1][:, 0:T], cst("ksin"), ALU.mult).then_inc(sig("cs"), 1)
                dve.wait_ge(sig("cs"), i + 1)
                nc.vector.tensor_tensor(qr, c1[:, 0, :], c2[:, 0, :], ALU.add)
                nc.vector.tensor_tensor(kr, c1[:, 1, :], c2[:, 1, :], ALU.add).then_inc(sig("rot"), 1)
                dve.wait_ge(sig("rot"), i + 1)
                nc.vector.tensor_tensor(qd, qr[:, 128:T], qdec[:, i, :], ALU.mult).then_inc(sig("qd"), 1)
                dve.wait_ge(sig("kT"), i + 1)
                nc.vector.tensor_tensor(ktok, B[4][:, 0:256].rearrange("p (t h d) -> p t h d", t=2, h=2),
                                        rep(wide(cst("kdecP")[:, bass.ds(i * 2, 2)].unsqueeze(2), 64), 1, 2), ALU.mult)
                nc.vector.tensor_tensor(ktokS[0:NS], B[4][0:NS, 256:384].rearrange("p (h d) -> p h d", h=2),
                                        wide(cst("kdecS")[0:NS, bass.ds(i * 2, 2)].unsqueeze(2), 64),
                                        ALU.mult).then_inc(sig("ktok"), 1)
                dve.wait_ge(sig("scores"), i + 1)
                for h in range(2):
                    nc.vector.tensor_tensor(att[:, h], B[h][:, 0:NP].rearrange("p (t q) -> p t q", t=2),
                                            rep(dmP[:, i * 2 + h, :], 1, 2), ALU.mult)
                    ins = nc.vector.tensor_tensor(attS[0:NS, h, :], B[h][0:NS, SAMPLE], dmS[0:NS, i * 2 + h, :],
                                                  ALU.mult)
                ins.then_inc(sig("att"), 1)
                dve.wait_ge(sig("ktok"), i + 1)
                nc.vector.tensor_tensor(kseq[0:NS], rep(ktokS[0:NS].rearrange("p h d -> p (h d)"), 1, NB),
                                        wide(cst("inseq")[0:NS].unsqueeze(2), 128), ALU.mult).then_inc(sig("kseq"), 1)
                dve.wait_ge(sig("mid"), i + 1)
                dve.wait_ge(sig("fin_ps"), i + 1)
                dve.wait_ge(sig("stored"), i * 32 + 32)
                nc.vector.scalar_tensor_tensor(out=fin, in0=mid, scalar=cdec[:, i, 0:1], in1=B[5][:, 0:128],
                                               op0=ALU.mult, op1=ALU.add).then_inc(sig("fin"), 1)
                dve.wait_ge(sig("stS_ps"), i + 1)
                for n in range(2):
                    nc.vector.scalar_tensor_tensor(out=st[:, 4 * n:4 * n + 4, :], in0=st[:, 4 * n:4 * n + 4, :],
                                                   scalar=cdec[:, i, 1:2],
                                                   in1=B[3 + n][:, :].rearrange("p (b d) -> p b d", b=4),
                                                   op0=ALU.mult, op1=ALU.add).then_inc(sig("stS"), 1)
                dve.wait_ge(sig("rs"), i + 1)
                nc.vector.tensor_tensor(c1, o, rs, ALU.mult).then_inc(sig("on"), 1)
                dve.wait_ge(sig("on"), i + 1)
                dve.wait_ge(sig("gate"), i + 1)
                nc.vector.tensor_tensor(y_ret[:, bass.ds(i * 2, 2), :], c1, gate,
                                        ALU.mult).then_inc(sig("y"), 1)

    def gated_linear(nc, block, sig, layer):
        w = Work()
        cum = w(4, T)
        z = w(4, T)
        tmp1, tmp2 = w(4, T), w(4, T)
        la = w(4, T)
        w.at -= 4 * 4 * T
        q, k, v = w(T), w(T), w(2, T)
        dif, fac, ql, kl = w(2, T), w(2, T), w(2, T), w(2, T)
        dend, fend, kend, eb, qb = w(T), w(T), w(T), w(T), w(T)
        eend = w(2 + NB)
        w.at = max(w.at, 5 * 4 * T)
        vtok, vtokS = w(2, 256), w(256)
        ktok, ktokS, kseq = w(2, 128), w(128), w(NB, 128)
        att, attS = w(2, 128), w(32)
        mid, fin, st = w(256), w(256), w(NB, 256)
        o, osq, lnv, rs = w(2, T), w(2, T), w(T), w(T)
        gate = w(2, T)
        ROW = 1 + NP + (NT + 1) * NB
        row, step = w(2, ROW), w(2, ROW)
        shin, shout = w(RW_SLABS, NB), w(RW_SLABS, 1 + NB)
        B = bank

        @block.sync
        def _(sp):
            def head(i, load_next):
                sp.wait_ge(sig("stored"), i * 32 + 32)
                sp.dma_start(st, s_gla[layer, i]).then_inc(sig("state"), 16)
                sp.wait_ge(sig("fin"), i + 1)
                sp.dma_start(gla_p[layer, i], fin).then_inc(sig("stored"), 16)
                sp.wait_ge(sig("stS"), i * NB + NB)
                sp.dma_start(gla_s[layer, i], st).then_inc(sig("stored"), 16)
                load_next()

            sp.dma_start(shin, s_shift[layer]).then_inc(sig("shift"), 16)
            grant(sp, sig("stored"), by=32)
            with sp.Fori(0, GLA_H - 1) as i:
                head(i, lambda: load_group(sp, S_RW, i + 1))
            head(GLA_H - 1, lambda: load_first_group(sp, S_SIDE))
            sp.wait_ge(sig("row"), RW_SLABS)
            sp.dma_start(shift_out[layer], shout).then_inc(sig("stored"), 16)
            sp.wait_ge(sig("stored"), GLA_H * 32 + 32 + 16)

        @block.tensor
        def _(pe):
            for kt in range(KT):
                mm = nc.tensor.matmul(B[4][0:GLA_RANK, 0:T], lora_w[:, kt, 256:272], hT[:, kt, :],
                                      start=(kt == 0), stop=(kt == KT - 1))
            mm.then_inc(sig("gk_ps"), 1)
            for s in range(NLORA):
                for kt in range(KT):
                    mm = nc.tensor.matmul(B[6 + s][:, 0:T], lora_w[:, kt, 128 * s:128 * s + 128], hT[:, kt, :],
                                          start=(kt == 0), stop=(kt == KT - 1))
                mm.then_inc(sig("lora_ps"), 1)
            pe.wait_ge(sig("gk"), 1)
            for h in range(GLA_H):
                mm = nc.tensor.matmul(B[h][:, 0:T], gkup[:, 128 * h:128 * h + 128], tmp2[0:GLA_RANK, 0, :],
                                      start=True, stop=True)
            mm.then_inc(sig("z_ps"), 1)
            grant(pe, sig("kT"), sig("o_ps"))
            pe.wait_ge(sig("z"), 1)
            with pe.Fori(0, GLA_H) as i:
                rw = Between([(lambda j=j: (pe.wait_ge(sig("row"), i * 6 + j + 1), slab_arrived(pe, S_RW, i, j)),
                               j, B[6 + j % 2][:, 0:T], hT) for j in range(6)])
                pe.wait_ge(sig("staged"), i + 1)
                for t in range(2):
                    for h in range(2):
                        nc.tensor.transpose(B[2][:, 256 * t + 128 * h:][:, 0:128], v[:, h, 128 * t:128 * t + 128], ident)
                for h in range(2):
                    mm = nc.tensor.transpose(B[3][0:NS, 128 * h:128 * h + 128], v[:, h, SAMPLE], ident)
                mm.then_inc(sig("vT"), 1)
                rw(KT)
                for n, s in enumerate((0,) + LEVELS):
                    if n == 0:
                        kk, qq = k, q
                    else:
                        pe.wait_ge(sig("lev"), i * len(LEVELS) + n)
                        kk, qq = kl[:, n % 2, :], ql[:, n % 2, :]
                    if n >= 2:
                        pe.wait_ge(sig("att"), i * 8 + n - 1)
                    for t in range(2):
                        c = slice(128 * t, 128 * t + 128)
                        mm = nc.tensor.matmul(B[n % 2][:, c], kk[:, c], qq[:, c], start=True, stop=True)
                    if s <= 2:
                        mm = nc.tensor.matmul(B[n % 2][0:NS, 256:288], kk[:, SAMPLE], qq[:, SAMPLE],
                                              start=True, stop=True)
                    mm.then_inc(sig("scores"), 1)
                    rw(3 * KT // (len(LEVELS) + 1))
                pe.wait_ge(sig("kend"), i + 1)
                for t in range(2):
                    nc.tensor.transpose(B[4][:, 128 * t:128 * t + 128], kend[:, 128 * t:128 * t + 128], ident)
                nc.tensor.transpose(B[4][0:NS, 256:384], kend[:, SAMPLE], ident).then_inc(sig("kT"), 1)
                pe.wait_ge(sig("ktok"), i + 1)
                nc.tensor.matmul(B[5][:, 0:256], ktok[:, 0, :], vtok[:, 0, :], start=True,
                                 stop=True).then_inc(sig("mid_ps"), 1)
                nc.tensor.matmul(B[3][:, 0:256], ktok[:, 1, :], vtok[:, 1, :], start=True,
                                 stop=True).then_inc(sig("fin_ps"), 1)
                pe.wait_ge(sig("qb"), i + 1)
                pe.wait_ge(sig("att"), i * 8 + 8)
                pe.wait_ge(sig("mid"), i + 1)
                pe.wait_ge(sig("state"), (i + 1) * 16)
                for h in range(2):
                    ob, f = B[h], slice(128 * h, 128 * h + 128)
                    nc.tensor.matmul(ob[:, 0:128], vtok[:, 0, f], att[:, 0, :], start=True, stop=True)
                    nc.tensor.matmul(ob[:, SAMPLE], vtokS[0:NS, f], attS[0:NS, :], start=True, stop=False)
                    for b in range(NB):
                        c = slice(NP + NT * b, NP + NT * b + NT)
                        nc.tensor.matmul(ob[:, c], st[:, b, f], qb[:, c], start=False, stop=(b == NB - 1))
                        rw(b % 2)
                    nc.tensor.matmul(ob[:, 128:256], vtok[:, 1, f], att[:, 1, :], start=True, stop=False)
                    mm = nc.tensor.matmul(ob[:, 128:256], mid[:, f], qb[:, 128:256], start=False, stop=True)
                mm.then_inc(sig("o_ps"), 1)
                pe.wait_ge(sig("kseq"), i + 1)
                pe.wait_ge(sig("fin"), i + 1)
                for b in range(NB):
                    mm = nc.tensor.matmul(B[2 + b // 2][:, 256 * (b % 2):256 * (b % 2) + 256], kseq[0:NS, b, :],
                                          vtokS[0:NS, :], start=True, stop=True)
                mm.then_inc(sig("stS_ps"), 1)
                pe.wait_ge(sig("osq"), i + 1)
                for h in range(2):
                    mm = nc.tensor.matmul(B[0][:, 0:T], ones, osq[:, h, :], start=(h == 0), stop=(h == 1))
                mm.then_inc(sig("ss"), 1)
                rw(KT)

        @block.scalar
        def _(act):
            def fill(slab, r, ps):
                tail = row[:, r, 1 + NP:ROW].rearrange("p (b t) -> p b t", t=NT + 1)
                nc.scalar.activation(row[:, r, 1:1 + NP], ps[:, 0:NP], ACT.Copy)
                nc.scalar.activation(tail[:, :, 1:], ps[:, SAMPLE].rearrange("p (b t) -> p b t", t=NT), ACT.Copy)
                nc.scalar.activation(tail[:, :, 0:1], shin[:, slab, :].unsqueeze(2), ACT.Copy)
                nc.scalar.activation(shout[:, slab, 0:1], ps[:, NP - 1:NP], ACT.Copy)
                nc.scalar.activation(shout[:, slab, 1:1 + NB], ps[:, NP + NT - 1:T:NT], ACT.Copy)\
                    .then_inc(sig("row"), 1)

            nc.scalar.activation(proj[:, 16:24, :], proj[:, 16:24, :], ACT.Silu).then_inc(sig("silu"), 1)
            act.wait_ge(sig("gk_ps"), 1)
            nc.scalar.activation(tmp2[0:GLA_RANK, 0, :], B[4][0:GLA_RANK, 0:T], ACT.Copy).then_inc(sig("gk"), 1)
            act.wait_ge(sig("z_ps"), 1)
            for h in range(GLA_H):
                ins = nc.scalar.activation(z[:, h, :], B[h][:, 0:T], ACT.Identity, bias=vec[:, V_GKB + h:V_GKB + h + 1])
            ins.then_inc(sig("z"), 1)
            act.wait_ge(sig("shift"), 16)
            act.wait_ge(sig("zero_col"), 1)
            for s in range(NLORA):
                act.wait_ge(sig("lora_ps"), s + 1)
                fill(24 + s, s, B[6 + s])
            act.wait_ge(sig("z"), 1)
            nc.scalar.activation(tmp1, z, ACT.Abs).then_inc(sig("absz"), 1)
            act.wait_ge(sig("absz"), 1)
            nc.scalar.activation(tmp2, tmp1, ACT.Exp, scale=-1.0).then_inc(sig("ez"), 1)
            act.wait_ge(sig("ez"), 1)
            nc.scalar.activation(tmp1, tmp2, ACT.Ln, bias=1.0).then_inc(sig("lnz"), 1)
            act.wait_ge(sig("cum"), 1)
            act.wait_ge(sig("silu"), 1)
            with act.Fori(0, GLA_H) as i:
                def rw_row(j):
                    act.wait_ge(slab_done, i * 6 + (BASE[S_RW] + j + 1))
                    act.wait_ge(sig("mixed"), i * 6 + j + 1)
                    fill(slabs_of_head(i)[j], j % 2, B[6 + j % 2])

                act.wait_ge(sig("y"), i + 1)
                nc.scalar.activation(q, proj[:, i, :], ACT.Copy, scale=GLA_DK ** -0.5)
                nc.scalar.activation(k, proj[:, i + 4, :], ACT.Copy)
                nc.scalar.activation(v, proj[:, bass.ds(i * 2 + 8, 2), :], ACT.Copy)
                nc.scalar.activation(gate, proj[:, bass.ds(i * 2 + 16, 2), :], ACT.Copy).then_inc(sig("staged"), 1)
                act.wait_ge(sig("dend"), i + 1)
                nc.scalar.activation(eb, cum[:, i, :], ACT.Exp)
                nc.scalar.activation(fend, dend, ACT.Exp)
                nc.scalar.activation(eend[:, 0:2], cum[:, i, 127:256:128], ACT.Exp)
                nc.scalar.activation(eend[:, 2:2 + NB], cum[:, i, NP + NT - 1:T:NT], ACT.Exp).then_inc(sig("eb"), 1)
                act.wait_ge(sig("vT"), i + 1)
                nc.scalar.activation(vtok, B[2][:, :].rearrange("p (t d) -> p t d", t=2), ACT.Copy)
                nc.scalar.activation(vtokS[0:NS], B[3][0:NS, 0:256], ACT.Copy).then_inc(sig("vtok"), 1)
                for n, s in enumerate(LEVELS):
                    cols = T if s <= 2 else NP
                    act.wait_ge(sig("dif"), i * len(LEVELS) + n + 1)
                    d = dif[:, (n + 1) % 2, 0:cols].rearrange("p (n c s) -> p n c s", c=2, s=s)
                    f = fac[:, (n + 1) % 2, 0:cols].rearrange("p (n c s) -> p n c s", c=2, s=s)
                    nc.scalar.activation(f[:, :, 0, :], d[:, :, 0, :], ACT.Exp, scale=-1.0)
                    nc.scalar.activation(f[:, :, 1, :], d[:, :, 1, :], ACT.Exp).then_inc(sig("fac"), 1)
                    if n in (0, 2, 5, 6):
                        rw_row((0, 2, 5, 6).index(n))
                act.wait_ge(sig("kT"), i + 2)
                nc.scalar.activation(ktok, B[4][:, 0:256].rearrange("p (t d) -> p t d", t=2), ACT.Copy)
                nc.scalar.activation(ktokS[0:NS], B[4][0:NS, 256:384], ACT.Copy).then_inc(sig("ktok"), 1)
                act.wait_ge(sig("mid_ps"), i + 1)
                nc.scalar.activation(mid, B[5][:, 0:256], ACT.Copy).then_inc(sig("mid"), 1)
                rw_row(4)
                act.wait_ge(sig("o_ps"), i + 2)
                for h in range(2):
                    nc.scalar.activation(o[:, h, :], B[h][:, 0:T], ACT.Copy)
                    ins = nc.scalar.activation(osq[:, h, :], B[h][:, 0:T], ACT.Square)
                ins.then_inc(sig("osq"), 1)
                act.wait_ge(sig("ss"), i + 1)
                nc.scalar.activation(lnv, B[0][:, 0:T], ACT.Ln, scale=1.0 / GLA_DV, bias=eps).then_inc(sig("ln"), 1)
                act.wait_ge(sig("ln"), i + 1)
                nc.scalar.activation(rs, lnv, ACT.Exp, scale=-0.5).then_inc(sig("rs"), 1)
                rw_row(5)

        @block.vector
        def _(dve):
            def mix(n, r, mu, out):
                dve.wait_ge(sig("row"), n + 1)
                nc.vector.tensor_tensor(step[:, r, 0:ROW - 1], row[:, r, 0:ROW - 1], row[:, r, 1:ROW],
                                        ALU.subtract).then_inc(sig("step"), 1)
                dve.wait_ge(sig("step"), n + 1)
                nc.vector.scalar_tensor_tensor(out=out[:, 0:NP], in0=step[:, r, 0:NP], scalar=mu,
                                               in1=row[:, r, 1:1 + NP], op0=ALU.mult, op1=ALU.add)
                tail = slice(1 + NP, ROW)
                nc.vector.scalar_tensor_tensor(
                    out=out[:, SAMPLE].rearrange("p (b t) -> p b t", t=NT),
                    in0=step[:, r, tail].rearrange("p (b t) -> p b t", t=NT + 1)[:, :, 0:NT], scalar=mu,
                    in1=row[:, r, tail].rearrange("p (b t) -> p b t", t=NT + 1)[:, :, 1:],
                    op0=ALU.mult, op1=ALU.add).then_inc(sig("mixed"), 1)

            nc.vector.memset(row[:, :, 0:1], 0.0).then_inc(sig("zero_col"), 1)
            for s in range(NLORA):
                mix(s, s, vec[:, V_MU + 24 + s:V_MU + 25 + s], lora[:, s, :])
            dve.wait_ge(sig("z"), 1)
            nc.vector.tensor_scalar(la, z, 0.0, None, ALU.min).then_inc(sig("minz"), 1)
            dve.wait_ge(sig("minz"), 1)
            dve.wait_ge(sig("lnz"), 1)
            nc.vector.tensor_tensor(la, la, tmp1, ALU.subtract).then_inc(sig("ls"), 1)
            dve.wait_ge(sig("ls"), 1)
            nc.vector.tensor_scalar(la, la, 1.0 / 16.0, None, ALU.mult).then_inc(sig("la"), 1)
            dve.wait_ge(sig("la"), 1)
            for h in range(GLA_H):
                ins = nc.vector.tensor_tensor_scan(cum[:, h, :], cst("keep"), la[:, h, :], 0.0, ALU.mult, ALU.add)
            ins.then_inc(sig("cum"), 1)
            dve.wait_ge(sig("cum"), 1)
            grant(dve, sig("y"))
            with dve.Fori(0, GLA_H) as i:
                def rw_mix(j):
                    slab = slabs_of_head(i)[j]
                    mix(i * 6 + j + 2, j % 2, vec[:, bass.ds(slab + V_MU, 1)], proj[:, slab, :])

                dve.wait_ge(sig("kT"), i + 1)
                c = cum[:, i, :]
                for a, n, m in ((0, 128, 2), (NP, NT, NB)):
                    cc = c[:, a:a + n * m].rearrange("p (m n) -> p m n", n=n)
                    ins = nc.vector.tensor_tensor(dend[:, a:a + n * m].rearrange("p (m n) -> p m n", n=n),
                                                  wide(cc[:, :, n - 1:n], n), cc, ALU.subtract)
                ins.then_inc(sig("dend"), 1)

                def distance(n, s):
                    cols = T if s <= 2 else NP
                    cc = c[:, 0:cols].rearrange("p (n c) -> p n c", c=2 * s)
                    nc.vector.tensor_tensor(dif[:, (n + 1) % 2, 0:cols].rearrange("p (n c) -> p n c", c=2 * s), cc,
                                            wide(cc[:, :, s - 1:s], 2 * s), ALU.subtract).then_inc(sig("dif"), 1)

                distance(0, LEVELS[0])
                dve.wait_ge(sig("o_ps"), i + 1)
                nc.vector.memset(att, 0.0)
                nc.vector.memset(attS[0:NS], 0.0).then_inc(sig("zero"), 1)
                dve.wait_ge(sig("staged"), i + 1)
                dve.wait_ge(sig("eb"), i + 1)
                nc.vector.tensor_tensor(kend, k, fend, ALU.mult).then_inc(sig("kend"), 1)
                nc.vector.tensor_tensor(qb, q, eb, ALU.mult).then_inc(sig("qb"), 1)

                def take(n, s):
                    dve.wait_ge(sig("scores"), i * 8 + n + 1)
                    dve.wait_ge(sig("att" if n else "zero"), i * 8 + n if n else i + 1)
                    mask = level_mask(s) if n else diag_mask
                    settle(dve)
                    if s <= 2:
                        nc.vector.copy_predicated(attS[0:NS], mask[0:NS, 0:NS], B[n % 2][0:NS, 256:288])
                    nc.vector.copy_predicated(att, rep(mask, 1, 2),
                                              B[n % 2][:, 0:256].rearrange("p (t q) -> p t q", t=2)).then_inc(sig("att"), 1)

                for n, s in enumerate(LEVELS):
                    if n + 1 < len(LEVELS):
                        if n >= 1:
                            dve.wait_ge(sig("fac"), i * len(LEVELS) + n)
                        distance(n + 1, LEVELS[n + 1])
                    dve.wait_ge(sig("fac"), i * len(LEVELS) + n + 1)
                    cols = T if s <= 2 else NP
                    b = (n + 1) % 2
                    if n >= 1:
                        take(n - 1, LEVELS[n - 2] if n >= 2 else 0)
                    nc.vector.tensor_tensor(ql[:, b, 0:cols], q[:, 0:cols], fac[:, b, 0:cols], ALU.mult)
                    nc.vector.tensor_tensor(kl[:, b, 0:cols], k[:, 0:cols], fac[:, b, 0:cols],
                                            ALU.mult).then_inc(sig("lev"), 1)
                    if n in (2, 4, 6):
                        rw_mix((2, 4, 6).index(n))
                take(6, LEVELS[5])
                take(7, LEVELS[6])
                rw_mix(3)
                dve.wait_ge(sig("ktok"), i + 1)
                nc.vector.tensor_tensor(kseq[0:NS], rep(ktokS[0:NS], 1, NB),
                                        wide(cst("inseq")[0:NS].unsqueeze(2), 128), ALU.mult).then_inc(sig("kseq"), 1)
                dve.wait_ge(sig("mid"), i + 1)
                dve.wait_ge(sig("fin_ps"), i + 1)
                dve.wait_ge(sig("stored"), i * 32 + 32)
                nc.vector.scalar_tensor_tensor(out=fin, in0=mid, scalar=eend[:, 1:2], in1=B[3][:, 0:256],
                                               op0=ALU.mult, op1=ALU.add).then_inc(sig("fin"), 1)
                rw_mix(4)
                dve.wait_ge(sig("stS_ps"), i + 1)
                for b in range(NB):
                    nc.vector.scalar_tensor_tensor(out=st[:, b, :], in0=st[:, b, :], scalar=eend[:, 2 + b:3 + b],
                                                   in1=B[2 + b // 2][:, 256 * (b % 2):256 * (b % 2) + 256],
                                                   op0=ALU.mult, op1=ALU.add).then_inc(sig("stS"), 1)
                dve.wait_ge(sig("rs"), i + 1)
                for h in range(2):
                    ins = nc.vector.scalar_tensor_tensor(out=o[:, h, :], in0=o[:, h, :],
                                                         scalar=vec[:, V_GNW + h:V_GNW + h + 1], in1=rs,
                                                         op0=ALU.mult, op1=ALU.mult)
                ins.then_inc(sig("on"), 1)
                dve.wait_ge(sig("on"), i + 1)
                nc.vector.tensor_tensor(y_gla[:, bass.ds(i * 2, 2), :], o, gate, ALU.mult).then_inc(sig("y"), 1)
                rw_mix(5)

    def rwkv(nc, block, sig, layer):
        w = Work()
        th, sg = w(T), w(T)
        wr = w(256)
        v = w(T)
        sw, a, g = w(T), w(T), w(T)
        early1, early2 = w(4 * T), w(4 * T)
        kk2, lnk, rsk, u1 = (early1[:, T * n:T * n + T] for n in range(4))
        dif, dex, e_in, e_out = (early2[:, T * n:T * n + T] for n in range(4))
        bseq, kseq = (x[:, 0:NB * 128].rearrange("p (b k) -> p b k", b=NB) for x in (early1, early2))
        kk, cum, e_ex = w(T), w(T), w(T)
        emid, eend, edec = w(2 + NB), w(2 + NB), w(2 + NB)
        dend = w(2 + NB)
        knew, kka = w(T), w(T)
        rt, at, bt, kt = w(T), w(T), w(T), w(T)
        bh, kh = w(T), w(T)
        rk = w(T)
        oneka = w(KT)
        tok, tokS = w(2, 3, 128), w(3, 128)
        AT, X, XT, W1 = w(4, 128), w(4, 128), w(4, 128), w(4, 128)
        ATs, Xs, XTs, W1s = w(2, 32), w(2, 32), w(2, 32), w(2, 32)
        Pk, Pb, Pr = w(4, 128), w(4, 128), w(4, 128)
        Pks, Pbs, Prs = w(2, 32), w(2, 32), w(2, 32)
        R, U = w(2, 64), w(2, 64)
        Rs, Us = w(2, 64), w(2, 64)
        mid, midm = w(64), w(64)
        st, s0T, s0m, stn = w(NB, 64), w(NB, 64), w(NB, 64), w(NB, 64)
        dg = w(1 + NB, 64)
        aseq = w(NB, NS)
        fin = w(64)
        gate, part = w(2, T), w(T)
        o, mean, oc, osq, lnv, rs = bh, kh, at, bt, kt, knew
        B = bank

        GRANTED = {"y": 1, "g": 1, "s0T": 1, "var_ps": 1}

        def done(eng, name, i, n=1, of=1):
            eng.wait_ge(sig(name), i * of + n + GRANTED.get(name, 0))

        @block.sync
        def _(sp):
            grant(sp, sig("stored"), by=32)
            with sp.Fori(0, KT) as i:
                done(sp, "g", i, 0)
                sp.dma_start(wr, w_rank[layer, i]).then_inc(sig("wr"), 16)
                done(sp, "s0T", i, 0)
                sp.dma_start(st, s_rw[layer, i]).then_inc(sig("state"), 16)
                load_group(sp, S_SIDE, i + 1)
                done(sp, "fin", i)
                sp.dma_start(rw_p[layer, i], fin).then_inc(sig("stored"), 16)
                done(sp, "stn", i)
                sp.dma_start(rw_s[layer, i], stn).then_inc(sig("stored"), 16)
            load_first_group(sp, S_RW_OUT, STREAM[S_SIDE][1])
            sp.wait_ge(sig("stored"), KT * 32 + 32)

        SA = B[2], B[3]
        small = B[4], B[5]
        nlev = len(LEVELS) - 1

        def unit(h, t):
            return 2 * h + t

        def tile(t):
            return slice(128 * t, 128 * t + 128)

        @block.tensor
        def _(pe):
            grant(pe, sig("var_ps"))
            with pe.Fori(0, KT) as i:
                def used(n):
                    if n < 2:
                        pe.wait_ge(sig("side_used"), i * 2 + n + 1)
                    else:
                        done(pe, "gates", i)

                side = Between([(lambda j=j: (used(j), slab_arrived(pe, S_SIDE, i, j)), j, B[6 + j % 2][:, 0:T],
                                 (hT, hT, y_ret, y_gla)[j]) for j in range(4)])
                side(2 * KT)
                done(pe, "y", i, 0)
                pe.wait_ge(sig("wr"), (i + 1) * 16)
                done(pe, "th", 0)
                nc.tensor.matmul(B[0][:, 0:T], wr[0:64, 0:128], th[0:64, :], start=True, stop=True)
                nc.tensor.matmul(B[1][:, 0:T], wr[64:128, 0:128], th[64:128, :], start=True, stop=True)
                nc.tensor.matmul(B[2][:, 0:T], wr[:, 128:256], sg, start=True, stop=True).then_inc(sig("up"), 1)
                done(pe, "kk2", i)
                nc.tensor.matmul(B[3][:, 0:T], headones, kk2, start=True, stop=True).then_inc(sig("kk_ps"), 1)
                pe.wait_ge(sig("state"), (i + 1) * 16)
                settle(pe)
                for h in range(2):
                    for b in range(NB):
                        mm = nc.tensor.matmul(heads_of(B[4], h)[:, 64 * b:64 * b + 64], heads_of(st, h)[:, b, :],
                                              heads_of(eye64, h), start=True, stop=True)
                mm.then_inc(sig("s0_ps"), 1)
                side(KT)
                done(pe, "ab", i)
                for h in range(2):
                    for t in range(2):
                        nc.tensor.matmul(B[h][:, tile(t)], heads_of(bt, h)[:, tile(t)],
                                         heads_of(at, h)[:, tile(t)], start=True, stop=True)
                        nc.tensor.matmul(B[h][:, NP + 128 * t:NP + 128 * t + 128], heads_of(at, h)[:, tile(t)],
                                         heads_of(bt, h)[:, tile(t)], start=True, stop=True)
                for h in range(2):
                    nc.tensor.matmul(SA[h][0:NS, 0:32], heads_of(bt, h)[:, SAMPLE], heads_of(at, h)[:, SAMPLE],
                                     start=True, stop=True)
                    mm = nc.tensor.matmul(SA[h][0:NS, 32:64], heads_of(at, h)[:, SAMPLE],
                                          heads_of(bt, h)[:, SAMPLE], start=True, stop=True)
                mm.then_inc(sig("A_ps"), 1)
                done(pe, "rkt", i)
                done(pe, "s0T", i)
                for h in range(2):
                    for t in range(2):
                        nc.tensor.matmul(small[h][:, tile(t)], heads_of(kt, h)[:, tile(t)],
                                         heads_of(rt, h)[:, tile(t)], start=True, stop=True)
                for h in range(2):
                    for n, (lhs, rhs) in enumerate(((kt, at), (bt, rt), (kt, rt))):
                        mm = nc.tensor.matmul(small[h][0:NS, NP + 32 * n:NP + 32 * n + 32],
                                              heads_of(lhs, h)[:, SAMPLE], heads_of(rhs, h)[:, SAMPLE],
                                              start=True, stop=True)
                mm.then_inc(sig("Pr_ps"), 1)
                done(pe, "AT", i)
                done(pe, "X0", i)
                settle(pe)
                for n in range(nlev):
                    if n:
                        done(pe, "X", i, n, nlev)
                    for j in range(4):
                        mm = nc.tensor.matmul(B[2][:, 128 * j:128 * j + 128], AT[:, j, :], X[:, j, :],
                                              start=True, stop=True)
                    mm.then_inc(sig("W1_ps"), 1)
                    if n == 0:
                        for h in range(2):
                            for m, (lhs, rhs) in enumerate(((kt, at), (bt, rt))):
                                for t in range(2):
                                    mm = nc.tensor.matmul(B[h][:, 256 * m + 128 * t:][:, 0:128],
                                                          heads_of(lhs, h)[:, tile(t)], heads_of(rhs, h)[:, tile(t)],
                                                          start=True, stop=True)
                        mm.then_inc(sig("P_ps"), 1)
                        done(pe, "Pr", i)
                    elif n == 3:
                        done(pe, "P", i)
                        done(pe, "hat", i)
                        done(pe, "v", i)
                        done(pe, "XTs", i)
                        for m, src in enumerate((v, bh, kh)):
                            for t in range(2):
                                nc.tensor.transpose(B[t][:, 128 * m:128 * m + 128], src[:, tile(t)], ident)
                            mm = nc.tensor.transpose(B[5][0:NS, 128 * m:128 * m + 128], src[:, SAMPLE], ident)
                        mm.then_inc(sig("tok_ps"), 1)
                    else:
                        side(1)
                    done(pe, "W1", i, n + 1, nlev)
                    for j in range(4):
                        if n < nlev - 1:
                            nc.tensor.matmul(B[3][:, 128 * j:128 * j + 128], XT[:, j, :], W1[:, j, :],
                                             start=True, stop=True)
                        mm = nc.tensor.matmul(B[4][:, 128 * j:128 * j + 128], W1[:, j, :], XT[:, j, :],
                                              start=True, stop=True)
                    mm.then_inc(sig("X_ps"), 1)
                    if n == 0:
                        settle(pe)
                        for h in range(2):
                            mm = nc.tensor.matmul(B[5][0:NS, 384 + 32 * h:416 + 32 * h], ATs[0:NS, h, :],
                                                  Xs[0:NS, h, :], start=True, stop=True)
                        mm.then_inc(sig("W1s_ps"), 1)
                    elif n == 1:
                        done(pe, "W1s", i)
                        settle(pe)
                        for h in range(2):
                            mm = nc.tensor.matmul(B[5][0:NS, 448 + 32 * h:480 + 32 * h], W1s[0:NS, h, :],
                                                  XTs[0:NS, h, :], start=True, stop=True)
                        mm.then_inc(sig("Xs_ps"), 1)
                    side(1)
                side(KT)
                done(pe, "tok", i)
                done(pe, "X", i, nlev, nlev)
                for h in range(2):
                    mm = nc.tensor.matmul(B[2 + h][:, 0:64], Pk[:, unit(h, 0), :],
                                          tok[:, 0, 0, 64 * h:64 * h + 64], start=True, stop=True)
                mm.then_inc(sig("R_ps"), 1)
                done(pe, "R", i, 1, 2)
                for h in range(2):
                    mm = nc.tensor.matmul(B[4][:, 64 * h:64 * h + 64], XT[:, unit(h, 0), :], R[:, h, :],
                                          start=True, stop=True)
                mm.then_inc(sig("U_ps"), 1)
                done(pe, "aseq", i)
                done(pe, "s0m", i)
                settle(pe)
                for h in range(2):
                    f = slice(64 * h, 64 * h + 64)
                    nc.tensor.matmul(B[h][0:NS, 0:64], Pks[0:NS, h, :], tokS[0:NS, 0, f], start=True, stop=False)
                    for b in range(NB):
                        mm = nc.tensor.matmul(B[h][0:NS, 0:64], heads_of(aseq, h)[:, b, :], heads_of(s0m, h)[:, b, :],
                                              start=False, stop=(b == NB - 1))
                mm.then_inc(sig("Rs_ps"), 1)
                done(pe, "U", i, 1, 2)
                for h in range(2):
                    f = slice(64 * h, 64 * h + 64)
                    o_h = heads_of(B[5], h)
                    nc.tensor.matmul(o_h[:, 0:128], U[:, h, :], Pb[:, unit(h, 0), :], start=True, stop=False)
                    nc.tensor.matmul(o_h[:, 0:128], tok[:, 0, 0, f], Pr[:, unit(h, 0), :], start=False, stop=True)
                    nc.tensor.matmul(heads_of(B[2], h)[:, 0:64], tok[:, 0, 1, f], U[:, h, :], start=True, stop=False)
                    mm = nc.tensor.matmul(heads_of(B[2], h)[:, 0:64], tok[:, 0, 2, f], tok[:, 0, 0, f],
                                          start=False, stop=True)
                mm.then_inc(sig("mid_ps"), 1)
                done(pe, "Rs", i)
                settle(pe)
                for h in range(2):
                    mm = nc.tensor.matmul(B[1][0:NS, 64 * h:64 * h + 64], XTs[0:NS, h, :], Rs[0:NS, h, :],
                                          start=True, stop=True)
                mm.then_inc(sig("Us_ps"), 1)
                done(pe, "mid", i)
                for h in range(2):
                    f = slice(64 * h, 64 * h + 64)
                    nc.tensor.matmul(B[2 + h][:, 0:64], Pk[:, unit(h, 1), :], tok[:, 1, 0, f], start=True,
                                     stop=False)
                    mm = nc.tensor.matmul(B[2 + h][:, 0:64], heads_of(at, h)[:, tile(1)], heads_of(midm, h),
                                          start=False, stop=True)
                mm.then_inc(sig("R_ps"), 1)
                done(pe, "R", i, 2, 2)
                for h in range(2):
                    mm = nc.tensor.matmul(B[4][:, 64 * h:64 * h + 64], XT[:, unit(h, 1), :], R[:, h, :],
                                          start=True, stop=True)
                mm.then_inc(sig("U_ps"), 1)
                done(pe, "U", i, 2, 2)
                done(pe, "Us", i)
                for h in range(2):
                    f = slice(64 * h, 64 * h + 64)
                    o_h = heads_of(B[5], h)
                    nc.tensor.matmul(o_h[:, tile(1)], U[:, h, :], Pb[:, unit(h, 1), :], start=True, stop=False)
                    nc.tensor.matmul(o_h[:, tile(1)], tok[:, 1, 0, f], Pr[:, unit(h, 1), :], start=False, stop=False)
                    nc.tensor.matmul(o_h[:, tile(1)], heads_of(midm, h), heads_of(rt, h)[:, tile(1)],
                                     start=False, stop=True)
                    nc.tensor.matmul(o_h[:, SAMPLE], Us[0:NS, h, :], Pbs[0:NS, h, :], start=True, stop=False)
                    nc.tensor.matmul(o_h[:, SAMPLE], tokS[0:NS, 0, f], Prs[0:NS, h, :], start=False, stop=False)
                    for b in range(NB):
                        c = slice(NP + NT * b, NP + NT * b + NT)
                        mm = nc.tensor.matmul(o_h[:, c], heads_of(s0m, h)[:, b, :], heads_of(rt, h)[:, c],
                                              start=False, stop=(b == NB - 1))
                mm.then_inc(sig("o_ps"), 1)
                done(pe, "dg", i)
                for h in range(2):
                    f = slice(64 * h, 64 * h + 64)
                    s_h = heads_of(B[0], h)[:, 0:64]
                    nc.tensor.matmul(s_h, U[:, h, :], tok[:, 1, 1, f], start=True, stop=False)
                    nc.tensor.matmul(s_h, tok[:, 1, 0, f], tok[:, 1, 2, f], start=False, stop=False)
                    mm = nc.tensor.matmul(s_h, heads_of(mid, h), heads_of(dg, h)[:, 0, :], start=False, stop=True)
                mm.then_inc(sig("fin_ps"), 1)
                done(pe, "seq", i)
                for h in range(2):
                    f = slice(64 * h, 64 * h + 64)
                    s_h = heads_of(B[3], h)
                    nc.tensor.matmul(s_h, Us[0:NS, h, :], bseq[0:NS, :, f], start=True, stop=False)
                    nc.tensor.matmul(s_h, tokS[0:NS, 0, f], kseq[0:NS, :, f], start=False, stop=False)
                    for b in range(NB):
                        mm = nc.tensor.matmul(s_h[:, 64 * b:64 * b + 64], heads_of(s0T, h)[:, b, :],
                                              heads_of(dg, h)[:, 1 + b, :], start=False, stop=(b == NB - 1))
                mm.then_inc(sig("stn_ps"), 1)
                done(pe, "o", i)
                nc.tensor.matmul(B[1][:, 0:T], headones, o, start=True, stop=True).then_inc(sig("mean_ps"), 1)
                done(pe, "osq", i)
                nc.tensor.matmul(B[2][:, 0:T], headones, osq, start=True, stop=True)
                nc.tensor.matmul(B[4][:, 0:T], headones, rk, start=True, stop=True).then_inc(sig("var_ps"), 1)

        @block.scalar
        def _(act):
            nc.scalar.activation(th[0:64], lora[0:64, 0, :], ACT.Tanh)
            nc.scalar.activation(th[64:128], lora[64:128, 0, :], ACT.Copy)
            nc.scalar.activation(sg, lora[:, 1, :], ACT.Sigmoid).then_inc(sig("th"), 1)
            grant(act, sig("g"), sig("s0T"))
            with act.Fori(0, KT) as i:
                done(act, "y", i, 0)
                nc.scalar.activation(v, proj[:, i + 16, :], ACT.Copy).then_inc(sig("v"), 1)
                done(act, "up", i)
                nc.scalar.activation(sw, B[0][:, 0:T], ACT.Sigmoid, bias=vec[:, bass.ds(i + V_W0, 1)])
                nc.scalar.activation(a, B[1][:, 0:T], ACT.Sigmoid, bias=vec[:, bass.ds(i + V_A0, 1)])\
                    .then_inc(sig("sw"), 1)
                nc.scalar.activation(g, B[2][:, 0:T], ACT.Copy).then_inc(sig("g"), 1)
                act.wait_ge(slab_done, i * 4 + (BASE[S_SIDE] + 2))
                for n in range(2):
                    ins = nc.scalar.activation(gate[:, n, :], B[6 + n][:, 0:T], ACT.Sigmoid)
                ins.then_inc(sig("gates"), 1)
                done(act, "kk_ps", i)
                nc.scalar.activation(lnk, B[3][:, 0:T], ACT.Ln, bias=tiny).then_inc(sig("lnk"), 1)
                done(act, "lnk", i)
                nc.scalar.activation(rsk, lnk, ACT.Exp, scale=-0.5).then_inc(sig("rsk"), 1)
                done(act, "dif", i)
                nc.scalar.activation(e_in, dif, ACT.Exp, scale=-KAPPA)
                nc.scalar.activation(e_out, dif, ACT.Exp, scale=KAPPA)
                nc.scalar.activation(e_ex, dex, ACT.Exp, scale=-KAPPA).then_inc(sig("e"), 1)
                nc.scalar.activation(emid[:, 0:2], cum[:, 63:256:128], ACT.Exp, scale=-KAPPA)
                nc.scalar.activation(emid[:, 2:], cum[:, NP + 1:T:NT], ACT.Exp, scale=-KAPPA)
                nc.scalar.activation(edec[:, 0:2], cum[:, 127:256:128], ACT.Exp, scale=-KAPPA)
                nc.scalar.activation(edec[:, 2:], cum[:, NP + NT - 1:T:NT], ACT.Exp, scale=-KAPPA)
                nc.scalar.activation(eend, dend, ACT.Exp, scale=-KAPPA).then_inc(sig("ec"), 1)
                done(act, "s0_ps", i)
                nc.scalar.activation(s0T, B[4][:, :].rearrange("p (b v) -> p b v", b=NB), ACT.Copy)\
                    .then_inc(sig("s0T"), 1)
                done(act, "A_ps", i)
                for h in range(2):
                    nc.scalar.activation(AT[:, 2 * h:2 * h + 2, :], B[h][:, 0:NP].rearrange("p (t s) -> p t s", t=2),
                                         ACT.Copy)
                    ins = nc.scalar.activation(ATs[0:NS, h, :], SA[h][0:NS, 0:32], ACT.Copy)
                ins.then_inc(sig("AT"), 1)
                for n in range(nlev):
                    done(act, "W1_ps", i, n + 1, nlev)
                    nc.scalar.activation(W1, B[2][:, :].rearrange("p (u s) -> p u s", u=4), ACT.Copy)\
                        .then_inc(sig("W1"), 1)
                    if n == 0:
                        done(act, "W1s_ps", i)
                        nc.scalar.activation(W1s[0:NS], B[5][0:NS, 384:448].rearrange("p (u s) -> p u s", u=2),
                                             ACT.Copy).then_inc(sig("W1s"), 1)
                    elif n == 3:
                        done(act, "tok_ps", i)
                        for t in range(2):
                            nc.scalar.activation(tok[:, t], B[t][:, 0:384].rearrange("p (n d) -> p n d", n=3), ACT.Copy)
                        nc.scalar.activation(tokS[0:NS], B[5][0:NS, 0:384].rearrange("p (n d) -> p n d", n=3),
                                             ACT.Copy).then_inc(sig("tok"), 1)
                for t in range(2):
                    done(act, "R_ps", i, t + 1, 2)
                    nc.scalar.activation(R[:, 0, :], B[2][:, 0:64], ACT.Copy)
                    nc.scalar.activation(R[:, 1, :], B[3][:, 0:64], ACT.Copy).then_inc(sig("R"), 1)
                    done(act, "U_ps", i, t + 1, 2)
                    nc.scalar.activation(U, B[4][:, 0:128].rearrange("p (h v) -> p h v", h=2), ACT.Copy)\
                        .then_inc(sig("U"), 1)
                    if t == 0:
                        done(act, "Rs_ps", i)
                        nc.scalar.activation(Rs[0:NS, 0, :], B[0][0:NS, 0:64], ACT.Copy)
                        nc.scalar.activation(Rs[0:NS, 1, :], B[1][0:NS, 0:64], ACT.Copy).then_inc(sig("Rs"), 1)
                        done(act, "Us_ps", i)
                        nc.scalar.activation(Us[0:NS], B[1][0:NS, 0:128].rearrange("p (h v) -> p h v", h=2),
                                             ACT.Copy).then_inc(sig("Us"), 1)
                done(act, "o_ps", i)
                nc.scalar.activation(o, B[5][:, 0:T], ACT.Copy).then_inc(sig("o"), 1)
                done(act, "oc", i)
                nc.scalar.activation(osq, oc, ACT.Square).then_inc(sig("osq"), 1)
                done(act, "var_ps", i)
                nc.scalar.activation(lnv, B[2][:, 0:T], ACT.Ln, scale=1.0 / RW_HD, bias=gn_eps).then_inc(sig("lnv"), 1)
                done(act, "lnv", i)
                nc.scalar.activation(rs, lnv, ACT.Exp, scale=-0.5).then_inc(sig("rs"), 1)

        @block.vector
        def _(dve):
            tt, stt = nc.vector.tensor_tensor, nc.vector.scalar_tensor_tensor
            nc.vector.tensor_scalar(oneka, vec[:, V_KA:V_KA + KT], -1.0, 1.0, ALU.mult, ALU.add)\
                .then_inc(sig("oneka"), 1)
            dve.wait_ge(sig("oneka"), 1)
            grant(dve, sig("side_used"), by=2)
            grant(dve, sig("y"))
            with dve.Fori(0, KT) as i:
                def then(ins, name):
                    ins.then_inc(sig(name), 1)
                    done(dve, name, i)

                k_i, r_i = proj[:, i + 8, :], proj[:, i, :]
                done(dve, "var_ps", i, 0)
                then(nc.vector.tensor_scalar(kk, k_i, vec[:, bass.ds(i + V_KKS, 1)], None, ALU.mult), "kk")
                tt(kk2, kk, kk, ALU.mult).then_inc(sig("kk2"), 1)
                done(dve, "sw", i)
                tt_scan = nc.vector.tensor_tensor_scan(cum, cst("keep"), sw, 0.0, ALU.mult, ALU.add)
                then(tt_scan, "cum")
                then(nc.vector.tensor_scalar(u1, a, vec[:, bass.ds(i + V_KA, 1)], oneka[:, bass.ds(i, 1)],
                                             ALU.mult, ALU.add), "u1")
                tt(knew, k_i, u1, ALU.mult)
                for o0, n, m, c0, c1 in ((0, 128, 2, 63, 0), (NP, NT, NB, 1, 2)):
                    cc = cum[:, o0:o0 + n * m].rearrange("p (m n) -> p m n", n=n)
                    tt(dif[:, o0:o0 + n * m].rearrange("p (m n) -> p m n", n=n), cc, wide(cc[:, :, c0:c0 + 1], n),
                       ALU.subtract)
                    ins = tt(dend[:, c1:c1 + m].unsqueeze(2), cc[:, :, n - 1:n], cc[:, :, c0:c0 + 1], ALU.subtract)
                then(ins, "dif0")
                tt(dex, dif, sw, ALU.subtract).then_inc(sig("dif"), 1)
                then(stt(out=rk, in0=knew, scalar=vec[:, bass.ds(i + V_RK, 1)], in1=r_i, op0=ALU.mult,
                         op1=ALU.mult), "rk")
                done(dve, "rsk", i)
                then(tt(kk, kk, rsk, ALU.mult), "kkn")
                then(tt(kka, kk, a, ALU.mult), "kka")
                done(dve, "e", i)
                stt(out=at, in0=kk, scalar=-1.0, in1=e_ex, op0=ALU.mult, op1=ALU.mult)
                then(tt(bt, kka, e_out, ALU.mult), "ab")
                tt(kt, knew, e_out, ALU.mult)
                then(tt(rt, r_i, e_in, ALU.mult), "rkt")
                done(dve, "ec", i)
                for src, dst in ((bt, bh), (kt, kh)):
                    for o0, n, m, c1 in ((0, 128, 2, 0), (NP, NT, NB, 2)):
                        ins = tt(dst[:, o0:o0 + n * m].rearrange("p (m n) -> p m n", n=n),
                                 src[:, o0:o0 + n * m].rearrange("p (m n) -> p m n", n=n),
                                 wide(eend[:, c1:c1 + m].unsqueeze(2), n), ALU.mult)
                ins.then_inc(sig("hat"), 1)
                dve.wait_ge(slab_done, i * 4 + (BASE[S_SIDE] + 3))
                done(dve, "gates", i)
                tt(merged[:, i, :], B[6][:, 0:T], gate[:, 0, :], ALU.mult).then_inc(sig("side_used"), 1)
                done(dve, "A_ps", i)
                nc.vector.tensor_copy(X, rep(ident, 1, 4))
                nc.vector.tensor_copy(XT, rep(ident, 1, 4))
                nc.vector.tensor_copy(Xs[0:NS], rep(ident[0:NS, 0:NS], 1, 2))
                then(nc.vector.tensor_copy(XTs[0:NS], rep(ident[0:NS, 0:NS], 1, 2)), "eye")
                done(dve, "AT", i)
                settle(dve)
                u4 = lambda bk: bk[:, :].rearrange("p (u s) -> p u s", u=4)
                u2 = lambda ap: ap.rearrange("p (t s) -> p t s", t=2)
                for h in range(2):
                    hh = slice(2 * h, 2 * h + 2)
                    nc.vector.copy_predicated(X[:, hh, :], rep(level_mask(1, True), 1, 2), u2(B[h][:, NP:512]))
                    nc.vector.copy_predicated(XT[:, hh, :], rep(level_mask(1), 1, 2), u2(B[h][:, 0:NP]))
                    nc.vector.copy_predicated(Xs[0:NS, h, :], level_mask(1, True)[0:NS, 0:NS], SA[h][0:NS, 32:64])
                    ins = nc.vector.copy_predicated(XTs[0:NS, h, :], level_mask(1)[0:NS, 0:NS], SA[h][0:NS, 0:32])
                then(ins, "X0")
                done(dve, "Pr_ps", i)
                for h in range(2):
                    tt(Pr[:, 2 * h:2 * h + 2, :], u2(small[h][:, 0:256]), rep(cst("causal"), 1, 2), ALU.mult)
                    for n, (dst, m) in enumerate(((Pks, "strictS"), (Pbs, "causalS"), (Prs, "causalS"))):
                        ins = tt(dst[0:NS, h, :], small[h][0:NS, NP + 32 * n:NP + 32 * n + 32], cst(m)[0:NS], ALU.mult)
                ins.then_inc(sig("Pr"), 1)

                def level(n):
                    done(dve, "X_ps", i, n + 1, nlev)
                    settle(dve)
                    if n < nlev - 1:
                        nc.vector.copy_predicated(X, rep(level_mask(LEVELS[n + 1], True), 1, 4), u4(B[3]))
                    nc.vector.copy_predicated(XT, rep(level_mask(LEVELS[n + 1]), 1, 4), u4(B[4]))\
                        .then_inc(sig("X"), 1)

                level(0)
                done(dve, "P_ps", i)
                for h in range(2):
                    hh = slice(2 * h, 2 * h + 2)
                    tt(Pk[:, hh, :], u2(B[h][:, 0:256]), rep(cst("strict"), 1, 2), ALU.mult)
                    ins = tt(Pb[:, hh, :], u2(B[h][:, 256:512]), rep(cst("causal"), 1, 2), ALU.mult)
                ins.then_inc(sig("P"), 1)
                level(1)
                done(dve, "Xs_ps", i)
                settle(dve)
                nc.vector.copy_predicated(XTs[0:NS], rep(level_mask(2)[0:NS, 0:NS], 1, 2), u2(B[5][0:NS, 448:512]))\
                    .then_inc(sig("XTs"), 1)
                level(2)
                done(dve, "s0T", i)
                tt(s0m, s0T, wide(emid[:, 2:].unsqueeze(2), 64), ALU.mult).then_inc(sig("s0m"), 1)
                tt(aseq, rep(at[:, SAMPLE], 1, NB), cst("seqcols").rearrange("p (b t) -> p b t", b=NB), ALU.mult)\
                    .then_inc(sig("aseq"), 1)
                tt(dg[:, 0, :], eye64, wide(edec[:, 1:2], 64), ALU.mult)
                tt(dg[:, 1:, :], rep(eye64, 1, NB), wide(edec[:, 2:].unsqueeze(2), 64), ALU.mult)\
                    .then_inc(sig("dg"), 1)
                for n in range(3, nlev):
                    level(n)
                done(dve, "tok", i)
                for n, dst in ((1, bseq), (2, kseq)):
                    ins = tt(dst[0:NS], rep(tokS[0:NS, n, :], 1, NB), wide(cst("inseq")[0:NS].unsqueeze(2), 128),
                             ALU.mult)
                ins.then_inc(sig("seq"), 1)
                dve.wait_ge(slab_done, i * 4 + (BASE[S_SIDE] + 4))
                tt(part, B[7][:, 0:T], gate[:, 1, :], ALU.mult).then_inc(sig("side_used"), 1)
                dve.wait_ge(sig("side_used"), i * 2 + 4)
                tt(merged[:, i, :], merged[:, i, :], part, ALU.add)
                done(dve, "mid_ps", i)
                tt(midm, B[2][:, 0:64], wide(emid[:, 1:2], 64), ALU.mult)
                nc.vector.tensor_copy(mid, B[2][:, 0:64]).then_inc(sig("mid"), 1)
                done(dve, "fin_ps", i)
                dve.wait_ge(sig("stored"), i * 32 + 32)
                nc.vector.tensor_copy(fin, B[0][:, 0:64]).then_inc(sig("fin"), 1)
                done(dve, "stn_ps", i)
                nc.vector.tensor_copy(stn, B[3][:, :].rearrange("p (b k) -> p b k", b=NB)).then_inc(sig("stn"), 1)
                done(dve, "mean_ps", i)
                done(dve, "o", i)
                then(stt(out=oc, in0=B[1][:, 0:T], scalar=-1.0 / RW_HD, in1=o, op0=ALU.mult, op1=ALU.add), "oc")
                done(dve, "rs", i)
                then(tt(mean, B[4][:, 0:T], v, ALU.mult), "bonus")
                then(stt(out=oc, in0=oc, scalar=vec[:, bass.ds(i + V_LNW, 1)], in1=rs, op0=ALU.mult,
                         op1=ALU.mult), "yn")
                then(stt(out=oc, in0=oc, scalar=vec[:, bass.ds(i + V_LNB, 1)], in1=mean, op0=ALU.add,
                         op1=ALU.add), "yb")
                tt(y_rw[:, i, :], oc, g, ALU.mult).then_inc(sig("y"), 1)

    with nc.Fori(0, DEPTH) as layer:
        with nc.cleanup_on_exit():
            slab_in = [nc.alloc_semaphore(name=f"slab_in{s}") for s in range(RING)]
            slab_done = nc.alloc_semaphore(name="slab_done")

            def load_group(sp, p, g):
                n = STREAM[p][1]
                for s in range(n):
                    sp.wait_ge(slab_done, g * n + (BASE[p] - n + s + 1))
                    sp.dma_start(ring[:, s], w_mix[layer, g * n + (BASE[p] + s)]).then_inc(slab_in[s], 16)

            def load_first_group(sp, p, start=0):
                before = STREAM[p - 1][1] if p else 0
                for s in range(start, STREAM[p][1]):
                    if p:
                        sp.wait_ge(slab_done, BASE[p] - before + min(s + 1, before))
                    sp.dma_start(ring[:, s], w_mix[layer, BASE[p] + s]).then_inc(slab_in[s], 16)

            def slab_arrived(pe, p, g, s):
                pe.wait_ge(slab_in[s], (g + (fills(p, s) + 1)) * 16)

            def load_ff_slab(sp, e, j, s, before, n=KT):
                sp.wait_ge(slab_done, before)
                sp.dma_start(ring[:, s, 0:n], w_ff[e, j, :, 0:n]).then_inc(slab_in[s], 16)

            def slab_products(pe, s, out, rhs, n=KT, k0=0, last=KT):
                for k in range(n):
                    mm = nc.tensor.matmul(out, ring[:, s, k, :], rhs[:, k0 + k, :],
                                          start=(k0 + k == 0), stop=(k0 + k == last - 1))
                mm.then_inc(slab_done, 1)

            with phase(nc, "norm") as (block, sig):
                @block.sync
                def _(sp):
                    sp.dma_start(vec[:, :], vec_in[layer]).then_inc(sig("vec"), 16)
                    sp.dma_start(lora_w[:, :, :], w_lora[layer]).then_inc(sig("small"), 16)
                    sp.dma_start(gkup[:, :], w_gkup[layer]).then_inc(sig("small"), 16)
                    load_first_group(sp, S_RET)
                    sp.wait_ge(sig("small"), 32)

                rms(block, sig, vec[:, V_MIX:V_MIX + KT], hT, bank[7], Work())

            def project(name, p):
                with phase(nc, name) as (block, sig):
                    @block.sync
                    def _(sp):
                        with sp.Fori(1, 3) as g:
                            load_group(sp, p, g)
                        load_first_group(sp, p + 1)

                    @block.tensor
                    def _(pe):
                        with pe.Fori(0, 3) as g:
                            for s in range(RING):
                                slab_arrived(pe, p, g, s)
                                pe.wait_ge(sig("bank_free"), g * RING + s + 1)
                                slab_products(pe, s, bank[s % 4][:, 0:T], hT)

                    @block.scalar
                    def _(act):
                        act.sem_inc(sig("bank_free"), 4)
                        with act.Fori(0, 2) as g:
                            for s in range(RING):
                                act.wait_ge(slab_done, g * RING + (BASE[p] + s + 1))
                                nc.scalar.activation(proj[:, g * RING + s, :], bank[s % 4][:, 0:T],
                                                     ACT.Copy).then_inc(sig("bank_free"), 1)
                        for s in range(RING):
                            act.wait_ge(slab_done, BASE[p] + 2 * RING + s + 1)
                            nc.scalar.activation(proj[:, 2 * RING + s, :], bank[s % 4][:, 0:T],
                                                 ACT.Silu).then_inc(sig("bank_free"), 1)

            def merge(name, p, y):
                with phase(nc, name) as (block, sig):
                    w = Work()
                    gate, part = w(2, T), w(2, T)

                    @block.sync
                    def _(sp):
                        with sp.Fori(1, 2) as g:
                            load_group(sp, p, g)
                        load_first_group(sp, p + 1)

                    @block.tensor
                    def _(pe):
                        with pe.Fori(0, 2) as g:
                            for s in range(RING):
                                slab_arrived(pe, p, g, s)
                                pe.wait_ge(sig("gate_free" if s % 2 == 0 else "branch_free"),
                                           g * 4 + s // 2 + 1)
                                slab_products(pe, s, bank[s % 4][:, 0:T], y if s % 2 else hT)

                    @block.scalar
                    def _(act):
                        act.sem_inc(sig("gate_free"), 2)
                        with act.Fori(0, 2) as g:
                            for s in range(0, RING, 2):
                                act.wait_ge(slab_done, g * RING + (BASE[p] + s + 1))
                                act.wait_ge(sig("gate_used"), g * 4 + s // 2 + 1)
                                nc.scalar.activation(gate[:, s // 2 % 2, :], bank[s % 4][:, 0:T],
                                                     ACT.Sigmoid).then_inc(sig("gate_free"), 1)

                    @block.vector
                    def _(dve):
                        dve.sem_inc(sig("branch_free"), 2)
                        dve.sem_inc(sig("gate_used"), 2)
                        with dve.Fori(0, 2) as g:
                            for s in range(1, RING, 2):
                                m, b = g * 4 + s // 2, s // 2 % 2
                                dve.wait_ge(slab_done, g * RING + (BASE[p] + s + 1))
                                dve.wait_ge(sig("gate_free"), m + 3)
                                nc.vector.tensor_tensor(part[:, b, :], bank[s % 4][:, 0:T], gate[:, b, :],
                                                        ALU.mult).then_inc(sig("branch_free"), 1)
                                dve.wait_ge(sig("branch_free"), m + 3)
                                nc.vector.tensor_tensor(merged[:, m, :], merged[:, m, :], part[:, b, :],
                                                        ALU.add).then_inc(sig("gate_used"), 1)

            project("ret_in", S_RET)
            with phase(nc, "ret") as (block, sig):
                retention(nc, block, sig, layer)
            with phase(nc, "gla") as (block, sig):
                gated_linear(nc, block, sig, layer)
            with phase(nc, "rw") as (block, sig):
                rwkv(nc, block, sig, layer)
            merge("rw_out", S_RW_OUT, y_rw)

            with phase(nc, "out") as (block, sig):
                @block.tensor
                def _(pe):
                    for s in range(RING):
                        slab_arrived(pe, S_OUT, 0, s)
                        if s >= 4:
                            pe.wait_ge(sig("added"), s - 3)
                        slab_products(pe, s, bank[s % 4][:, 0:T], merged)

                @block.vector
                def _(dve):
                    for s in range(RING):
                        dve.wait_ge(slab_done, BASE[S_OUT] + s + 1)
                        nc.vector.tensor_tensor(xT[:, s, :], xT[:, s, :], bank[s % 4][:, 0:T],
                                                ALU.add).then_inc(sig("added"), 1)

            with phase(nc, "norm2") as (block, sig):
                @block.sync
                def _(sp):
                    sp.dma_start(vec[:, :], vec_in[layer]).then_inc(sig("vec"), 16)
                    sp.wait_ge(sig("vec"), 16)

                rms(block, sig, vec[:, V_FFN:V_FFN + KT], hT, bank[7], Work())

            UPG = UP_SLABS // RING

            def arrived(pe, p, s, g):
                pe.wait_ge(slab_in[s], (p * (9 if s < 4 else 8) + (fills(len(STREAM), s) + 1) + g) * 16)

            def ff_up(pe, sig, p, x):
                def up(g, s):
                    arrived(pe, p, s, g)
                    pe.wait_ge(sig("w1_free" if s % 2 == 0 else "w3_free"), p * FT + g * 4 + s // 2 + 1)
                    slab_products(pe, s, bank[s % 4][:, 0:x.shape[-1]], x)

                with pe.Fori(0, UPG) as g:
                    for s in range(RING):
                        up(g, s)
                for s in range(UP_SLABS % RING):
                    up(UPG, s)
                pe.wait_ge(sig("w3_free"), p * FT + FT + 2)

            def ff_silu(act, sig, p, act1):
                def silu(g, s):
                    act.wait_ge(slab_done, p * FF_SLABS + MIX_SLABS + g * RING + s + 1)
                    act.wait_ge(sig("w3_free"), p * FT + g * 4 + s // 2 + 1)
                    nc.scalar.activation(act1[:, s // 2 % 2, :], bank[s % 4][:, 0:act1.shape[-1]],
                                         ACT.Silu).then_inc(sig("w1_free"), 1)

                with act.Fori(0, UPG) as g:
                    for s in range(0, RING, 2):
                        silu(g, s)
                for s in range(0, UP_SLABS % RING, 2):
                    silu(UPG, s)

            def ff_product(dve, sig, p, act1, hid):
                def product(g, s):
                    f = g * 4 + s // 2
                    dve.wait_ge(slab_done, p * FF_SLABS + MIX_SLABS + g * RING + s + 1)
                    dve.wait_ge(sig("w1_free"), p * FT + f + 3)
                    nc.vector.tensor_tensor(hid[:, f, :], bank[s % 4][:, 0:act1.shape[-1]],
                                            act1[:, s // 2 % 2, :], ALU.mult).then_inc(sig("w3_free"), 1)

                with dve.Fori(0, UPG) as g:
                    for s in range(1, RING, 2):
                        product(g, s)
                for s in range(1, UP_SLABS % RING, 2):
                    product(UPG, s)

            def ff_down(pe, p, m, out, hid):
                for c in range(3):
                    j = UP_SLABS + 3 * m + c
                    arrived(pe, p, j % RING, j // RING)
                    slab_products(pe, j % RING, out, hid, n=6 if c == 2 else KT, k0=KT * c, last=FT)

            def ff_load(sp, e, base):
                for s in range(RING):
                    load_ff_slab(sp, e, s, s, base + s + 1 - (4 if s < 4 else 8))
                with sp.Fori(1, UPG + 1) as g:
                    for s in range(RING):
                        load_ff_slab(sp, e, g * RING + s, s, base + (g - 1) * RING + s + 1)
                for j in range((UPG + 1) * RING, FF_SLABS):
                    load_ff_slab(sp, e, j, j % RING, base + j - RING + 1, 6 if (j - UP_SLABS) % 3 == 2 else KT)

            with phase(nc, "dense") as (block, sig):
                w = Work()
                act1, hid = w(2, T), w(FT, T)

                @block.sync
                def _(sp):
                    with sp.If(layer < 1):
                        ff_load(sp, 0, MIX_SLABS)

                @block.tensor
                def _(pe):
                    with pe.If(layer < 1):
                        ff_up(pe, sig, 0, hT)
                        for m in range(KT):
                            if m >= 2:
                                pe.wait_ge(sig("added"), m - 1)
                            ff_down(pe, 0, m, bank[4 + m % 2][:, 0:T], hid)

                @block.scalar
                def _(act):
                    with act.If(layer < 1):
                        act.sem_inc(sig("w1_free"), 2)
                        ff_silu(act, sig, 0, act1)

                @block.vector
                def _(dve):
                    with dve.If(layer < 1):
                        dve.sem_inc(sig("w3_free"), 2)
                        ff_product(dve, sig, 0, act1, hid)
                        for m in range(KT):
                            dve.wait_ge(slab_done, MIX_SLABS + UP_SLABS + 3 * m + 3)
                            nc.vector.tensor_tensor(xT[:, m, :], xT[:, m, :], bank[4 + m % 2][:, 0:T],
                                                    ALU.add).then_inc(sig("added"), 1)

            TILES = ((0, 128), (128, 128), (256, 32))
            with phase(nc, "route") as (block, sig):
                w = Work()
                htok, slot, gate2 = w(3, D), w(2, 3), w(2, 3)
                lg, best = w(3, NE), w(3, NE)
                pick = w(3, NE).bitcast(U32)
                idx, hot, member, pos = w(3, NE), w(2, 3, NE), w(3, NE), w(3, NE)
                ex, den = w(3, 1), w(3, 1)
                count, npass, more, end, first = w(NE), w(NE), w(NE), w(NE), w(NE)
                before, ctlf = w(MAXP, NE), w(MAXP + 1)

                @block.tensor
                def _(pe):
                    with pe.If(layer > 0):
                        for i, (a, n) in enumerate(TILES):
                            for k in range(KT):
                                mm = nc.tensor.matmul(bank[0][0:n, NE * i:NE * i + NE], hT[:, k, a:a + n],
                                                      router[:, k, :], start=(k == 0), stop=(k == KT - 1))
                        mm.then_inc(sig("logits"), 1)
                        for i, (a, n) in enumerate(TILES):
                            for k in range(KT):
                                mm = nc.tensor.transpose(bank[2 + 2 * i + k // 4][0:n, 128 * (k % 4):128 * (k % 4) + 128],
                                                         hT[:, k, a:a + n], ident)
                            mm.then_inc(sig("htok_ps"), 1)
                        pe.wait_ge(sig("member"), 1)
                        for i in range(3):
                            for j in range(i + 1):
                                nc.tensor.matmul(bank[1][:, NE * i:NE * i + NE], ones if j < i else cst("strict"),
                                                 member[:, j, :], start=(j == 0), stop=(j == i))
                        for j in range(3):
                            mm = nc.tensor.matmul(bank[1][:, 3 * NE:4 * NE], ones, member[:, j, :],
                                                  start=(j == 0), stop=(j == 2))
                        mm.then_inc(sig("rank"), 1)

                @block.scalar
                def _(act):
                    with act.If(layer > 0):
                        for i, (a, n) in enumerate(TILES):
                            act.wait_ge(sig("htok_ps"), i + 1)
                            for b in range(2):
                                ins = nc.scalar.activation(htok[0:n, i, 512 * b:512 * b + 512],
                                                           bank[2 + 2 * i + b][0:n, :], ACT.Copy)
                        ins.then_inc(sig("htok"), 1)
                        act.wait_ge(sig("dif"), 1)
                        nc.scalar.activation(ex, ex, ACT.Exp).then_inc(sig("exp"), 1)
                        act.wait_ge(sig("htok"), 1)

                @block.vector
                def _(dve):
                    with dve.If(layer > 0):
                        tt, ts, stt = nc.vector.tensor_tensor, nc.vector.tensor_scalar, nc.vector.scalar_tensor_tensor

                        def then(ins, name):
                            ins.then_inc(sig(name), 1)
                            dve.wait_ge(sig(name), 1)

                        nc.vector.memset(htok[32:64, 2, :], 0.0)
                        nc.vector.memset(htok[64:128, 2, :], 0.0)
                        then(nc.vector.memset(lg, 0.0), "lg0")
                        dve.wait_ge(sig("logits"), 1)
                        for i, (a, n) in enumerate(TILES):
                            ins = nc.vector.tensor_copy(lg[0:n, i, :], bank[0][0:n, NE * i:NE * i + NE])
                        then(ins, "lg")
                        for i in range(3):
                            ins = nc.vector.max(best[:, i, :], lg[:, i, :])
                        then(ins, "best")
                        for i in range(3):
                            ins = nc.vector.max_index(pick[:, i, :], best[:, i, :], lg[:, i, :])
                        tt(ex, best[:, :, 1:2], best[:, :, 0:1], ALU.subtract).then_inc(sig("dif"), 1)
                        dve.wait_ge(sig("dif"), 1)
                        then(nc.vector.tensor_copy(idx, pick), "idx")
                        for i in range(3):
                            for c in range(2):
                                ins = ts(hot[:, c, i, :], cst("iota8"), idx[:, i, c:c + 1], cst("valid")[:, i:i + 1],
                                         ALU.is_equal, ALU.mult)
                        then(ins, "hot")
                        tt(member, hot[:, 0], hot[:, 1], ALU.add).then_inc(sig("member"), 1)
                        dve.wait_ge(sig("exp"), 1)
                        then(ts(den, ex, 1.0, None, ALU.add), "den")
                        then(nc.vector.reciprocal(gate2[:, 0, :], den[:, :, 0]), "p1")
                        tt(gate2[:, 1, :], gate2[:, 0, :], ex[:, :, 0], ALU.mult).then_inc(sig("gates"), 1)
                        dve.wait_ge(sig("rank"), 1)
                        nc.vector.tensor_copy(pos, bank[1][:, 0:3 * NE].rearrange("p (i e) -> p i e", i=3))
                        then(nc.vector.tensor_copy(count, bank[1][:, 3 * NE:4 * NE]), "count")
                        then(ts(npass, count, 0.0, None, ALU.is_gt), "n0")
                        for c in range(1, -(-T // CAP)):
                            then(ts(more, count, float(CAP * c), None, ALU.is_gt), f"more{c}")
                            then(tt(npass, npass, more, ALU.add), f"n{c}")
                        then(nc.vector.tensor_tensor_scan(end, cst("ones")[:, 0:NE], npass, 0.0, ALU.mult, ALU.add), "end")
                        then(tt(first, end, npass, ALU.subtract), "first")
                        then(stt(out=pos, in0=rep(first, 1, 3), scalar=float(CAP), in1=pos, op0=ALU.mult, op1=ALU.add),
                             "pos")
                        for c in range(2):
                            then(tt(hot[:, c], hot[:, c], pos, ALU.mult), f"hotpos{c}")
                            then(nc.vector.tensor_reduce(slot[:, c, :], hot[:, c], mybir.AxisListType.X, ALU.add),
                                 f"slot{c}")
                            then(tt(slot[:, c, :], slot[:, c, :], cst("nowhere"), ALU.add), f"slotv{c}")
                        then(tt(before, rep(end, 1, MAXP), wide(cst("passno").unsqueeze(2), NE), ALU.is_le), "before")
                        then(nc.vector.tensor_reduce(ctlf[:, 0:MAXP], before, mybir.AxisListType.X, ALU.add), "experts")
                        then(ts(ctlf[:, 0:MAXP], ctlf[:, 0:MAXP], 1.0, None, ALU.add), "experts1")
                        then(ts(ctlf[:, 0:MAXP], ctlf[:, 0:MAXP], float(NE), None, ALU.min), "experts2")
                        then(nc.vector.tensor_copy(ctlf[:, MAXP:], end[:, NE - 1:]), "passes")
                        then(nc.vector.tensor_copy(ctl[:, :], ctlf), "ctl")

            with phase(nc, "ff") as (block, sig):
                w = Work()
                htok, slot, gate2 = w(3, D), w(2, 3), w(2, 3)
                pick = w(2, 2, 3, CAP)
                gather, gated = w(3, CAP), w(3, CAP)
                scatter = w(T)
                hg, hid = w(KT, CAP), w(FT, CAP)
                act1, oT, otok = w(2, CAP), w(2, CAP), w(2, 128)

                def passes(eng):
                    return eng.value_load(ctl[0:1, MAXP:MAXP + 1], min_val=1, max_val=MAXP)

                @block.sync
                def _(sp):
                    with sp.If(layer > 0):
                        with sp.Fori(0, passes(sp)) as p:
                            e = sp.value_load(ctl[0:1, bass.ds(p, 1)], min_val=0, max_val=NE)
                            ff_load(sp, e, p * FF_SLABS + MIX_SLABS)

                @block.tensor
                def _(pe):
                    with pe.If(layer > 0):
                        def gather_tokens(n):
                            pe.wait_ge(sig("picked"), n)
                            for k in range(KT):
                                for i in range(3):
                                    mm = nc.tensor.matmul(bank[k // 4][:, CAP * (k % 4):CAP * (k % 4) + CAP],
                                                          htok[:, i, 128 * k:128 * k + 128], gather[:, i, :],
                                                          start=(i == 0), stop=(i == 2))
                            mm.then_inc(sig("hg_ps"), 1)

                        grant(pe, sig("sc_ps"), by=2)
                        gather_tokens(1)
                        with pe.Fori(0, passes(pe)) as p:
                            pe.wait_ge(sig("oT"), p * KT + 2)
                            for i, (a, n) in enumerate(TILES):
                                mm = nc.tensor.transpose(bank[5][0:CAP, a:a + n], gated[0:n, i, :], ident[0:n, 0:n])
                            mm.then_inc(sig("scatter_ps"), 1)
                            pe.wait_ge(sig("hg"), p + 1)
                            settle(pe)
                            ff_up(pe, sig, p, hg)
                            for m in range(KT + 2):
                                if m < KT:
                                    pe.wait_ge(sig("oT"), p * KT + m + 1)
                                    ff_down(pe, p, m, bank[4 + m % 2][:, 0:CAP], hid)
                                if m == 2:
                                    gather_tokens(p + 2)
                                if 1 <= m <= KT:
                                    pe.wait_ge(sig("oT"), p * KT + m + 2)
                                    pe.wait_ge(sig("otok"), p * KT + m)
                                    nc.tensor.transpose(bank[6][0:CAP, 0:128], oT[:, (m - 1) % 2, :],
                                                        ident).then_inc(sig("otok_ps"), 1)
                                if m >= 2:
                                    pe.wait_ge(sig("scatter"), p + 1)
                                    pe.wait_ge(sig("otok"), p * KT + m)
                                    pe.wait_ge(sig("added"), p * KT + m - 1)
                                    nc.tensor.matmul(bank[7][:, 0:T], otok[0:CAP, m % 2, :], scatter[0:CAP, :],
                                                     start=True, stop=True).then_inc(sig("sc_ps"), 1)

                @block.scalar
                def _(act):
                    with act.If(layer > 0):
                        def gathered(n):
                            act.wait_ge(sig("hg_ps"), n)
                            for b in range(2):
                                ins = nc.scalar.activation(hg[:, 4 * b:4 * b + 4, :],
                                                           bank[b][:, 0:4 * CAP].rearrange("p (k c) -> p k c", k=4),
                                                           ACT.Copy)
                            ins.then_inc(sig("hg"), 1)

                        grant(act, sig("w1_free"), sig("oT"), by=2)
                        grant(act, sig("otok"))
                        gathered(1)
                        with act.Fori(0, passes(act)) as p:
                            act.wait_ge(sig("scatter_ps"), p + 1)
                            act.wait_ge(sig("sc_ps"), p * KT + 2)
                            nc.scalar.activation(scatter[0:CAP, :], bank[5][0:CAP, 0:T], ACT.Copy)\
                                .then_inc(sig("scatter"), 1)
                            ff_silu(act, sig, p, act1)
                            for m in range(KT + 1):
                                if m < KT:
                                    act.wait_ge(slab_done, p * FF_SLABS + (MIX_SLABS + UP_SLABS) + 3 * m + 3)
                                    nc.scalar.activation(oT[:, m % 2, :], bank[4 + m % 2][:, 0:CAP],
                                                         ACT.Copy).then_inc(sig("oT"), 1)
                                if m >= 1:
                                    act.wait_ge(sig("otok_ps"), p * KT + m)
                                    act.wait_ge(sig("sc_ps"), p * KT + m)
                                    nc.scalar.activation(otok[0:CAP, (m - 1) % 2, :], bank[6][0:CAP, 0:128],
                                                         ACT.Copy).then_inc(sig("otok"), 1)
                                if m == 3:
                                    gathered(p + 2)

                @block.vector
                def _(dve):
                    with dve.If(layer > 0):
                        def choose(n):
                            for c in range(2):
                                for i in range(3):
                                    nc.vector.tensor_scalar(pick[:, c, 0, i, :], cst("column"), slot[:, c, i:i + 1], None,
                                                            ALU.is_equal)
                                    ins = nc.vector.tensor_scalar(pick[:, c, 1, i, :], cst("column"),
                                                                  slot[:, c, i:i + 1], gate2[:, c, i:i + 1],
                                                                  ALU.is_equal, ALU.mult)
                            ins.then_inc(sig("pick"), 1)
                            dve.wait_ge(sig("pick"), n)
                            nc.vector.tensor_tensor(gather, pick[:, 0, 0], pick[:, 1, 0], ALU.add)
                            nc.vector.tensor_tensor(gated, pick[:, 0, 1], pick[:, 1, 1], ALU.add)
                            nc.vector.tensor_scalar(slot, slot, float(-CAP), None, ALU.add).then_inc(sig("picked"), 1)

                        grant(dve, sig("w3_free"), by=2)
                        grant(dve, sig("added"))
                        choose(1)
                        with dve.Fori(0, passes(dve)) as p:
                            dve.wait_ge(sig("scatter_ps"), p + 1)
                            dve.wait_ge(sig("hg_ps"), p + 1)
                            dve.wait_ge(sig("picked"), p + 1)
                            choose(p + 2)

                            dve.wait_ge(slab_done, p * FF_SLABS + MIX_SLABS)
                            settle(dve)
                            ff_product(dve, sig, p, act1, hid)
                            for m in range(KT):
                                dve.wait_ge(sig("sc_ps"), p * KT + m + 3)
                                nc.vector.tensor_tensor(xT[:, m, :], xT[:, m, :], bank[7][:, 0:T],
                                                        ALU.add).then_inc(sig("added"), 1)

    with phase(nc, "final") as (block, sig):
        @block.gpsimd
        def _(pool):
            nc.gpsimd.sem_inc(sig("vec"), 16)

        rms(block, sig, vecf, hT, bank[7], Work())

        @block.sync
        def _(sp):
            sp.wait_ge(sig("normed"), 1)
            sp.dma_start(yT_out, hT[:, :, :]).then_inc(sig("stored"), 16)
            sp.wait_ge(sig("stored"), 16)


def kernel(**inputs):
    import concourse.bacc as bacc
    from concourse.bass_utils import run_bass_kernel_spmd

    a = {k: np.asarray(v) for k, v in inputs.items()}

    def feat(v):
        return np.swapaxes(v.reshape(v.shape[:-1] + (-1, 128)), -1, -2)

    def slabs(w):
        k, n = w.shape
        return w.reshape(k // 128, 128, n // 128, 128).transpose(2, 1, 0, 3)

    o1, o2 = 3072, 3072 + 3088
    o3 = o2 + RW_COLS
    rwp = np.concatenate([np.arange(0, 1024), np.arange(1088, 2112), np.arange(2112, 3136), np.arange(1024, 1088),
                          np.arange(3136, 3200), np.arange(3200, 3328)])
    w_mix = np.empty((DEPTH, MIX_SLABS, 128, KT, 128), np.float32)
    w_lora = np.empty((DEPTH, 128, KT, 272), np.float32)
    w_rank = np.empty((DEPTH, KT, 128, 256), np.float32)
    for l in range(DEPTH):
        w = a["w_in"][l]
        parts = [w[:, 0:o1], w[:, o1:o1 + 3072], w[:, o2:o3][:, rwp]]
        order = [n for i in range(GLA_H) for n in slabs_of_head(i)]
        for br in range(3):
            p = slabs(parts[br][:, 0:3072])
            w_mix[l, BASE[br]:BASE[br] + 24] = p[order] if br else p
        gates = [slabs(w[:, o3 + 1024 * br:o3 + 1024 * (br + 1)]) for br in range(3)]
        branches = [slabs(a["w_branch"][l, br]) for br in range(3)]
        for j, x in enumerate((gates[0], gates[1], branches[0], branches[1])):
            w_mix[l, BASE[S_SIDE] + j:BASE[S_RW_OUT]:4] = x
        w_mix[l, BASE[S_RW_OUT]:BASE[S_OUT]:2] = gates[2]
        w_mix[l, BASE[S_RW_OUT] + 1:BASE[S_OUT]:2] = branches[2]
        w_mix[l, BASE[S_OUT]:] = slabs(a["w_out"][l])
        low = np.concatenate([parts[2][:, 3072:], w[:, o1 + 3072:o2]], 1)
        w_lora[l] = low.reshape(KT, 128, 272).transpose(1, 0, 2)
        w_rank[l, :, 0:64, 0:128] = a["rwkv_w_up"][l].reshape(64, KT, 128).transpose(1, 0, 2)
        w_rank[l, :, 64:128, 0:128] = a["rwkv_a_up"][l].reshape(64, KT, 128).transpose(1, 0, 2)
        w_rank[l, :, :, 128:256] = a["rwkv_g_up"][l].reshape(128, KT, 128).transpose(1, 0, 2)
    w_ff = np.zeros((NFF, FF_SLABS, 128, KT, 128), np.float32)
    w1 = np.concatenate([a["ffn_w1"], a["moe_w1"][0]])
    w3 = np.concatenate([a["ffn_w3"], a["moe_w3"][0]])
    w2 = np.concatenate([a["ffn_w2"], a["moe_w2"][0]])
    for e in range(NFF):
        w_ff[e, 0:UP_SLABS:2] = slabs(w1[e])
        w_ff[e, 1:UP_SLABS:2] = slabs(w3[e])
        s2 = slabs(w2[e])
        for c in range(3):
            n = 6 if c == 2 else 8
            w_ff[e, UP_SLABS + c::3, :, 0:n] = s2[:, :, 8 * c:8 * c + n]
    vec = np.concatenate([feat(a[k]) for k in ("norm_mix", "norm_ffn", "gla_gk_bias", "gla_norm_w")]
                         + [feat(a["rwkv_mu"][:, rwp])]
                         + [feat(a[k].reshape(DEPTH, -1)) for k in ("rwkv_w0", "rwkv_a0", "rwkv_kk_scale", "rwkv_ka",
                                                                    "rwkv_rk", "rwkv_ln_w", "rwkv_ln_b")], -1)
    toks = np.concatenate([a["x_prompt"][0], a["x_sample"].reshape(NS, D)])
    arrays = {
        "xT": toks.T.reshape(KT, 128, T).transpose(1, 0, 2),
        "w_mix": w_mix, "w_lora": w_lora, "w_rank": w_rank, "w_gkup": a["gla_gk_up"], "vec": vec,
        "vecf": feat(a["norm_final"]), "router": a["moe_router"][0].reshape(KT, 128, NE).transpose(1, 0, 2),
        "w_ff": w_ff,
        "s_ret": a["state_ret"].reshape(DEPTH, NB, 4, 128, RET_DV).transpose(0, 2, 3, 1, 4),
        "s_gla": a["state_gla"].transpose(0, 2, 3, 1, 4),
        "s_rw": a["state_rwkv"].reshape(DEPTH, NB, KT, 128, RW_HD).transpose(0, 2, 3, 1, 4),
        "s_shift": feat(a["state_shift"][:, :, rwp]).transpose(0, 2, 3, 1),
        "table": TABLE, "masks": MASKS,
    }
    nc = bacc.Bacc("TRN2", target_bir_lowering=False, num_devices=1)
    args = []
    arrays = {k + "_dram": np.ascontiguousarray(v) for k, v in arrays.items()}
    for k, v in arrays.items():
        args.append(nc.dram_tensor(k, v.shape, mybir.dt.from_np(v.dtype), kind="ExternalInput").ap())
    outs = {"yT": (128, KT, T), "ret_p": (DEPTH, 4, 128, RET_DV), "ret_s": (DEPTH, 4, 128, NB, RET_DV),
            "gla_p": (DEPTH, GLA_H, 128, GLA_DV), "gla_s": (DEPTH, GLA_H, 128, NB, GLA_DV),
            "rw_p": (DEPTH, KT, 128, RW_HD), "rw_s": (DEPTH, KT, 128, NB, RW_HD),
            "shift": (DEPTH, 128, RW_SLABS, 1 + NB)}
    for k, shape in outs.items():
        args.append(nc.dram_tensor(k + "_out", shape, F32, kind="ExternalOutput").ap())
    build(nc, *args)
    r = run_bass_kernel_spmd(nc, [arrays], core_ids=[0]).results[0]
    r = {k: np.asarray(r[k + "_out"]) for k in outs}
    yt = r["yT"].transpose(1, 0, 2).reshape(D, T).T
    shift = np.empty((DEPTH, 1 + NB, RW_COLS), np.float32)
    shift[:, :, rwp] = r["shift"].transpose(0, 3, 2, 1).reshape(DEPTH, 1 + NB, RW_COLS)
    return (yt[:NP].reshape(1, NP, D), yt[NP:].reshape(NB, NT, D),
            r["ret_p"].reshape(DEPTH, 1, RET_H, RET_DK, RET_DV),
            r["gla_p"].reshape(DEPTH, 1, GLA_H, GLA_DK, GLA_DV),
            r["rw_p"].reshape(DEPTH, 1, RW_H, RW_HD, RW_HD), shift[:, 0:1],
            r["ret_s"].transpose(0, 3, 1, 2, 4).reshape(DEPTH, NB, RET_H, RET_DK, RET_DV),
            r["gla_s"].transpose(0, 3, 1, 2, 4),
            r["rw_s"].transpose(0, 3, 1, 2, 4).reshape(DEPTH, NB, RW_H, RW_HD, RW_HD), shift[:, 1:])
```
